# Optimizing a Trainium2 kernel written in Bass

```python
import math
import jax, jax.numpy as jnp
from jax import lax
import numpy as np

D_MODEL = 1024
BATCH = 1
SEQ = 256
DEPTH = 2
DEC_BATCH = 1
DEC_SEQ = 64
PAST_LEN = 128

CHUNK = 64
EPS = 1e-6
HALF = 0.5
D_FF = 2816
PLE_DIM = 256
SSM_HEAD_DIM = 64
D_INNER = D_MODEL
SSM_HEADS = D_INNER // SSM_HEAD_DIM
N_GROUPS = 4
HEADS_PER_GROUP = SSM_HEADS // N_GROUPS
D_STATE = 128
CONV_W = 4
CONV_CH = D_INNER + 2 * N_GROUPS * D_STATE
DSA_HEAD_DIM = 128
DSA_HEADS = D_MODEL // DSA_HEAD_DIM
KV_HEADS = 2
KV_REP = DSA_HEADS // KV_HEADS
IDX_HEADS = 4
IDX_DIM = 64
TOPK_MAX = 256
Q_BLOCK = 128
BAND_HEAD_DIM = 64
BAND_HEADS = D_MODEL // BAND_HEAD_DIM
LEFT_CHUNKS = 8
BAND = LEFT_CHUNKS * CHUNK
REL_CLIP = 256
N_BRANCH = 3
IN_WIDTHS = (D_INNER, CONV_CH, SSM_HEADS,
             DSA_HEADS * DSA_HEAD_DIM, KV_HEADS * DSA_HEAD_DIM, KV_HEADS * DSA_HEAD_DIM,
             IDX_HEADS * IDX_DIM, IDX_DIM, IDX_HEADS,
             BAND_HEADS * BAND_HEAD_DIM, BAND_HEADS * BAND_HEAD_DIM, BAND_HEADS * BAND_HEAD_DIM)
IN_WIDTH = sum(IN_WIDTHS)
IN_SPLITS = tuple(int(s) for s in np.cumsum(IN_WIDTHS)[:-1])

kernel_name = 'hybrid_streaming_encoder_step'

def rmsnorm(x, g):
    xf = x.astype(jnp.float32)
    xf = xf * lax.rsqrt(jnp.mean(xf * xf, axis=-1, keepdims=True) + EPS)
    return (xf * g.astype(jnp.float32)).astype(x.dtype)

def swiglu(u, w13, w2):
    a, b = jnp.split(u @ w13, 2, axis=-1)
    return (jax.nn.silu(a) * b) @ w2

def ssd_scan(xh, dt, a, bm, cm, h0):
    b, t = xh.shape[:2]
    q = min(CHUNK, t)
    nc = t // q
    g, hg = N_GROUPS, HEADS_PER_GROUP
    xdt = (xh.astype(jnp.float32) * dt[..., None]).reshape(b, nc, q, g, hg, SSM_HEAD_DIM)
    cum = jnp.cumsum((dt * a).reshape(b, nc, q, g, hg), axis=2)
    bmc = bm.astype(jnp.float32).reshape(b, nc, q, g, D_STATE)
    cmc = cm.astype(jnp.float32).reshape(b, nc, q, g, D_STATE)
    causal = jnp.tril(jnp.ones((q, q), dtype=bool))[:, :, None, None]
    seg = cum[:, :, :, None] - cum[:, :, None, :]
    decay_ls = jnp.exp(jnp.where(causal, seg, -jnp.inf))
    cb = jnp.einsum('bclgn,bcsgn->bclsg', cmc, bmc)
    y_diag = jnp.einsum('bclsgh,bcsghp->bclghp', cb[..., None] * decay_ls, xdt)
    decay_s = jnp.exp(cum[:, :, -1:] - cum)
    states = jnp.einsum('bcsgn,bcsghp->bcghpn', bmc, xdt * decay_s[..., None])
    chunk_decay = jnp.exp(cum[:, :, -1])

    def step(h, inp):
        st, dec = inp
        return dec[..., None, None] * h + st, h

    h_init = h0.astype(jnp.float32).reshape(b, g, hg, SSM_HEAD_DIM, D_STATE)
    h_fin, h_prev = lax.scan(step, h_init, (jnp.swapaxes(states, 0, 1), jnp.swapaxes(chunk_decay, 0, 1)))
    h_prev = jnp.swapaxes(h_prev, 0, 1)
    y_off = jnp.einsum('bclgn,bcghpn->bclghp', cmc, h_prev) * jnp.exp(cum)[..., None]
    y = (y_diag + y_off).reshape(b, t, SSM_HEADS, SSM_HEAD_DIM)
    return y, h_fin.reshape(b, SSM_HEADS, SSM_HEAD_DIM, D_STATE)

def mamba_branch(z, xbc, dt_raw, conv_buf, h0, conv_w, conv_b, dt_bias, a_log, d_skip, norm_g):
    b, t, _ = xbc.shape
    xp = jnp.concatenate([conv_buf.astype(xbc.dtype), xbc], axis=1)
    acc = conv_b
    for k in range(CONV_W):
        acc = acc + xp[:, k:k + t] * conv_w[k]
    xbc_c = jax.nn.silu(acc)
    xs, bm, cm = jnp.split(xbc_c, [D_INNER, D_INNER + N_GROUPS * D_STATE], axis=-1)
    dt = jax.nn.softplus(dt_raw.astype(jnp.float32) + dt_bias.astype(jnp.float32))
    a = -jnp.exp(a_log.astype(jnp.float32))
    xh = xs.reshape(b, t, SSM_HEADS, SSM_HEAD_DIM)
    y, h = ssd_scan(xh, dt, a, bm.reshape(b, t, N_GROUPS, D_STATE), cm.reshape(b, t, N_GROUPS, D_STATE), h0)
    y = y + d_skip.astype(jnp.float32)[:, None] * xh.astype(jnp.float32)
    gsz = D_INNER // N_GROUPS
    y = y.reshape(b, t, N_GROUPS, gsz) * jax.nn.silu(z.astype(jnp.float32)).reshape(b, t, N_GROUPS, gsz)
    y = y * lax.rsqrt(jnp.mean(y * y, axis=-1, keepdims=True) + EPS)
    y = (y.reshape(b, t, D_INNER) * norm_g.astype(jnp.float32)).astype(z.dtype)
    return y, xp[:, -(CONV_W - 1):], h.astype(h0.dtype)

def dsa_core(q, qi, wi, qpos, k, v, ki, kpos, topk):
    b, t = q.shape[:2]
    logits = jnp.einsum('bthd,bsd->bths', qi, ki) * (IDX_DIM ** -0.5)
    score = jnp.einsum('bths,bth->bts', jax.nn.relu(logits), wi).astype(jnp.float32)
    allowed = (kpos[None, :] // CHUNK) <= (qpos[:, None] // CHUNK)
    score = jnp.where(allowed[None], score, -jnp.inf)
    top_s, top_i = lax.top_k(score, topk)
    valid = jnp.isfinite(top_s)
    kg = jax.vmap(lambda kk, ii: kk[ii])(k, top_i)
    vg = jax.vmap(lambda vv, ii: vv[ii])(v, top_i)
    qg = q.reshape(b, t, KV_HEADS, KV_REP, DSA_HEAD_DIM)
    s = jnp.einsum('btgrd,btkgd->btgrk', qg, kg).astype(jnp.float32) * (DSA_HEAD_DIM ** -0.5)
    s = jnp.where(valid[:, :, None, None, :], s, -jnp.inf)
    pr = jax.nn.softmax(s, axis=-1).astype(v.dtype)
    o = jnp.einsum('btgrk,btkgd->btgrd', pr, vg)
    return o.reshape(b, t, DSA_HEADS * DSA_HEAD_DIM)

def dsa_prompt(q, qi, wi, k, v, ki):
    b, t = q.shape[:2]
    nb = t // Q_BLOCK
    topk = min(TOPK_MAX, t // 4)
    kpos = jnp.arange(t)

    def blk(args):
        j, qj, qij, wij = args
        qpos = j * Q_BLOCK + jnp.arange(Q_BLOCK)
        return dsa_core(qj, qij, wij, qpos, k, v, ki, kpos, topk)

    def to_blocks(a):
        return jnp.swapaxes(a.reshape((b, nb, Q_BLOCK) + a.shape[2:]), 0, 1)

    out = lax.map(blk, (jnp.arange(nb), to_blocks(q), to_blocks(qi), to_blocks(wi)))
    return jnp.swapaxes(out, 0, 1).reshape(b, t, DSA_HEADS * DSA_HEAD_DIM)

def band_core(q, k, v, qpos, kpos, rel_bias):
    rel = jnp.clip(qpos[:, None] - kpos[None, :], -REL_CLIP, REL_CLIP) + REL_CLIP
    bias = jnp.transpose(rel_bias[rel], (2, 0, 1)).astype(jnp.float32)
    dchunk = qpos[:, None] // CHUNK - kpos[None, :] // CHUNK
    allowed = (kpos[None, :] >= 0) & (dchunk >= 0) & (dchunk <= LEFT_CHUNKS)
    s = jnp.einsum('bthd,bshd->bhts', q, k).astype(jnp.float32) * (BAND_HEAD_DIM ** -0.5) + bias[None]
    s = jnp.where(allowed[None, None], s, -jnp.inf)
    pr = jax.nn.softmax(s, axis=-1).astype(v.dtype)
    o = jnp.einsum('bhts,bshd->bthd', pr, v)
    return o.reshape(q.shape[0], q.shape[1], BAND_HEADS * BAND_HEAD_DIM)

def band_prompt(q, k, v, rel_bias):
    b, t = q.shape[:2]
    nc = t // CHUNK
    pad = ((0, 0), (BAND, 0), (0, 0), (0, 0))
    kp, vp = jnp.pad(k, pad), jnp.pad(v, pad)
    band_off = jnp.arange(BAND + CHUNK) - BAND

    def blk(c):
        s0 = c * CHUNK
        qj = lax.dynamic_slice_in_dim(q, s0, CHUNK, axis=1)
        kj = lax.dynamic_slice_in_dim(kp, s0, BAND + CHUNK, axis=1)
        vj = lax.dynamic_slice_in_dim(vp, s0, BAND + CHUNK, axis=1)
        return band_core(qj, kj, vj, s0 + jnp.arange(CHUNK), s0 + band_off, rel_bias)

    out = lax.map(blk, jnp.arange(nc))
    return jnp.swapaxes(out, 0, 1).reshape(b, t, BAND_HEADS * BAND_HEAD_DIM)

def trunk_layer(x, p, lw, cache):
    b, t, _ = x.shape
    g = lw['norm_g']
    x = x + HALF * rmsnorm(swiglu(rmsnorm(x, g[0]), lw['ffn_w13'][0], lw['ffn_w2'][0]), g[1])
    u = rmsnorm(x, g[2])
    z, xbc, dt_raw, qb, kb, vb, qi, ki, wi, qc, kc, vc = jnp.split(u @ lw['w_in'], IN_SPLITS, axis=-1)
    qb = qb.reshape(b, t, DSA_HEADS, DSA_HEAD_DIM)
    kb = kb.reshape(b, t, KV_HEADS, DSA_HEAD_DIM)
    vb = vb.reshape(b, t, KV_HEADS, DSA_HEAD_DIM)
    qi = qi.reshape(b, t, IDX_HEADS, IDX_DIM)
    wi = wi * (IDX_HEADS ** -0.5)
    qc = qc.reshape(b, t, BAND_HEADS, BAND_HEAD_DIM)
    kc = kc.reshape(b, t, BAND_HEADS, BAND_HEAD_DIM)
    vc = vc.reshape(b, t, BAND_HEADS, BAND_HEAD_DIM)

    if cache is None:
        conv_buf = jnp.zeros((b, CONV_W - 1, CONV_CH), x.dtype)
        h0 = jnp.zeros((b, SSM_HEADS, SSM_HEAD_DIM, D_STATE), jnp.float32)
    else:
        conv_buf, h0 = cache['conv'], cache['ssm']
    ya, conv_new, h_new = mamba_branch(z, xbc, dt_raw, conv_buf, h0, lw['conv_w'], lw['conv_b'],
                                       lw['dt_bias'], lw['a_log'], lw['d_skip'], lw['ssm_norm_g'])

    if cache is None:
        yb = dsa_prompt(qb, qi, wi, kb, vb, ki)
        yc = band_prompt(qc, kc, vc, lw['rel_bias'])
        band_rows = min(BAND, t)
        band_k_out, band_v_out = kc[:, t - band_rows:], vc[:, t - band_rows:]
    else:
        past = cache['dsa_k'].shape[1]
        qpos = past + jnp.arange(t)
        k_all = jnp.concatenate([cache['dsa_k'].astype(kb.dtype), kb], axis=1)
        v_all = jnp.concatenate([cache['dsa_v'].astype(vb.dtype), vb], axis=1)
        ki_all = jnp.concatenate([cache['idx_k'].astype(ki.dtype), ki], axis=1)
        topk = min(TOPK_MAX, (past + t) // 4)
        yb = dsa_core(qb, qi, wi, qpos, k_all, v_all, ki_all, jnp.arange(past + t), topk)
        nrows = cache['band_k'].shape[1]
        kc_all = jnp.concatenate([cache['band_k'].astype(kc.dtype), kc], axis=1)
        vc_all = jnp.concatenate([cache['band_v'].astype(vc.dtype), vc], axis=1)
        kpos_c = past - nrows + jnp.arange(nrows + t)
        yc = band_core(qc, kc_all, vc_all, qpos, kpos_c, lw['rel_bias'])
        band_k_out, band_v_out = kc, vc

    gates = jax.nn.sigmoid((u @ lw['w_gate'] + lw['b_gate']).astype(jnp.float32)).astype(x.dtype)
    gates = gates.reshape(b, t, N_BRANCH, D_MODEL)
    branches = jnp.stack([ya, yb, yc], axis=2)
    proj = jnp.einsum('btkc,kcd->btkd', branches, lw['w_branch'])
    mix = jnp.sum(gates * proj, axis=2) @ lw['w_out']
    x = x + rmsnorm(mix, g[3])
    x = x + HALF * rmsnorm(swiglu(rmsnorm(x, g[4]), lw['ffn_w13'][1], lw['ffn_w2'][1]), g[5])
    e = p.astype(x.dtype) @ lw['w_ple']
    pg = jax.nn.sigmoid(rmsnorm(x, g[6]) @ lw['w_ple_gate'])
    x = x + rmsnorm(pg * e, g[7])
    return x, (kb, vb, ki, band_k_out, band_v_out, h_new, conv_new)

def setup_inputs(seed: int = 0) -> dict:
    key = jax.random.key(seed)
    ks = list(jax.random.split(key, 32))

    def nrm(shape, scale):
        return jax.random.normal(ks.pop(), shape, jnp.float32) * scale

    band_rows = min(BAND, PAST_LEN)
    dt0 = jnp.exp(jax.random.uniform(ks.pop(), (DEPTH, SSM_HEADS), jnp.float32,
                                     math.log(1e-3), math.log(1e-1)))
    a_log = jnp.log(jax.random.uniform(ks.pop(), (DEPTH, SSM_HEADS), jnp.float32, 1.0, 16.0))
    return {
        'x_prompt': nrm((BATCH, SEQ, D_MODEL), 1.0),
        'x_sample': nrm((DEC_BATCH, DEC_SEQ, D_MODEL), 1.0),
        'p_prompt': nrm((DEPTH, BATCH, SEQ, PLE_DIM), 1.0),
        'p_sample': nrm((DEPTH, DEC_BATCH, DEC_SEQ, PLE_DIM), 1.0),
        'cache_dsa_k': nrm((DEPTH, DEC_BATCH, PAST_LEN, KV_HEADS, DSA_HEAD_DIM), 1.0),
        'cache_dsa_v': nrm((DEPTH, DEC_BATCH, PAST_LEN, KV_HEADS, DSA_HEAD_DIM), 1.0),
        'cache_idx_k': nrm((DEPTH, DEC_BATCH, PAST_LEN, IDX_DIM), 1.0),
        'cache_band_k': nrm((DEPTH, DEC_BATCH, band_rows, BAND_HEADS, BAND_HEAD_DIM), 1.0),
        'cache_band_v': nrm((DEPTH, DEC_BATCH, band_rows, BAND_HEADS, BAND_HEAD_DIM), 1.0),
        'state_ssm': nrm((DEPTH, DEC_BATCH, SSM_HEADS, SSM_HEAD_DIM, D_STATE), 0.1),
        'state_conv': nrm((DEPTH, DEC_BATCH, CONV_W - 1, CONV_CH), 1.0),
        'norm_g': 1.0 + nrm((DEPTH, 8, D_MODEL), 0.05),
        'ffn_w13': nrm((DEPTH, 2, D_MODEL, 2 * D_FF), D_MODEL ** -0.5),
        'ffn_w2': nrm((DEPTH, 2, D_FF, D_MODEL), D_FF ** -0.5),
        'w_in': nrm((DEPTH, D_MODEL, IN_WIDTH), D_MODEL ** -0.5),
        'conv_w': nrm((DEPTH, CONV_W, CONV_CH), CONV_W ** -0.5),
        'conv_b': nrm((DEPTH, CONV_CH), 0.02),
        'dt_bias': dt0 + jnp.log(-jnp.expm1(-dt0)),
        'a_log': a_log,
        'd_skip': 1.0 + nrm((DEPTH, SSM_HEADS), 0.1),
        'ssm_norm_g': 1.0 + nrm((DEPTH, D_INNER), 0.05),
        'rel_bias': nrm((DEPTH, 2 * REL_CLIP + 1, BAND_HEADS), 0.5),
        'w_gate': nrm((DEPTH, D_MODEL, N_BRANCH * D_MODEL), D_MODEL ** -0.5),
        'b_gate': nrm((DEPTH, N_BRANCH * D_MODEL), 0.01),
        'w_branch': nrm((DEPTH, N_BRANCH, D_MODEL, D_MODEL), D_MODEL ** -0.5),
        'w_out': nrm((DEPTH, D_MODEL, D_MODEL), D_MODEL ** -0.5),
        'w_ple': nrm((DEPTH, PLE_DIM, D_MODEL), PLE_DIM ** -0.5),
        'w_ple_gate': nrm((DEPTH, D_MODEL, D_MODEL), D_MODEL ** -0.5),
    }

def reference(x_prompt, x_sample, p_prompt, p_sample, cache_dsa_k, cache_dsa_v, cache_idx_k,
              cache_band_k, cache_band_v, state_ssm, state_conv, norm_g, ffn_w13, ffn_w2, w_in,
              conv_w, conv_b, dt_bias, a_log, d_skip, ssm_norm_g, rel_bias, w_gate, b_gate,
              w_branch, w_out, w_ple, w_ple_gate):
    yp, ys = x_prompt, x_sample
    st_p, st_s = [], []
    for i in range(DEPTH):
        lw = {'norm_g': norm_g[i], 'ffn_w13': ffn_w13[i], 'ffn_w2': ffn_w2[i], 'w_in': w_in[i],
              'conv_w': conv_w[i], 'conv_b': conv_b[i], 'dt_bias': dt_bias[i], 'a_log': a_log[i],
              'd_skip': d_skip[i], 'ssm_norm_g': ssm_norm_g[i], 'rel_bias': rel_bias[i],
              'w_gate': w_gate[i], 'b_gate': b_gate[i], 'w_branch': w_branch[i], 'w_out': w_out[i],
              'w_ple': w_ple[i], 'w_ple_gate': w_ple_gate[i]}
        yp, sp = trunk_layer(yp, p_prompt[i], lw, None)
        st_p.append(sp)
        cache = {'dsa_k': cache_dsa_k[i], 'dsa_v': cache_dsa_v[i], 'idx_k': cache_idx_k[i],
                 'band_k': cache_band_k[i], 'band_v': cache_band_v[i],
                 'ssm': state_ssm[i], 'conv': state_conv[i]}
        ys, ss = trunk_layer(ys, p_sample[i], lw, cache)
        st_s.append(ss)
    dsa_k_p, dsa_v_p, idx_k_p, band_k_p, band_v_p, ssm_p, conv_p = [jnp.stack(c) for c in zip(*st_p)]
    dsa_k_s, dsa_v_s, idx_k_s, band_k_s, band_v_s, ssm_s, conv_s = [jnp.stack(c) for c in zip(*st_s)]
    return (yp, ys, dsa_k_p, dsa_v_p, idx_k_p, band_k_p, band_v_p, ssm_p, conv_p,
            dsa_k_s, dsa_v_s, idx_k_s, band_k_s, band_v_s, ssm_s, conv_s)


_drawn_inputs = setup_inputs


def setup_inputs(seed=0):
    import zlib

    import numpy as np

    out = dict(_drawn_inputs(seed))
    spreads = {}
    factors = {'b_gate': 8.0}
    for name, (base, spread) in spreads.items():
        noise = np.random.default_rng([zlib.crc32(name.encode()), seed]).standard_normal(out[name].shape)
        drawn = base * np.exp(spread * noise) if base else spread * noise
        out[name] = __import__('jax').numpy.asarray(drawn.astype(out[name].dtype))
    for name, factor in factors.items():
        out[name] = (out[name] * factor).astype(out[name].dtype)
    return out
```

```python
from contextlib import ExitStack

import numpy as np
import concourse.bass as bass
from concourse import mybir

F32 = mybir.dt.float32
F32R = mybir.dt.float32r
I32 = mybir.dt.int32
ALU = mybir.AluOpType
ACT = mybir.ActivationFunctionType

P = 128
DEPTH, SEQ, DEC, PAST, D = 2, 256, 64, 128, 1024
TOK = SEQ + DEC
KT = D // P
D_FF = 2816
FT = D_FF // P
HALF_FT = FT // 2
PLE = 256
CONV_CH = 2048
CT = CONV_CH // P
HEADS = 16
D_STATE = 128
GROUPS = 4
IN_W = 8020
Z0, XBC0, DT0, QB0, KB0, VB0, QI0, KI0, WI0, QC0, KC0, VC0 = (
    0, 1024, 3072, 3088, 4112, 4368, 4624, 4880, 4944, 4948, 5972, 6996)
XP = SEQ + 3 + DEC + 3
CONV_N = XP - 3
RING = 3
SLOT = 2048
EPS = 1e-6
BIG = 1e30
GONE = -3e38
RSQRT_SEED = 1597463007.0
TILES = ((0, 128, 128), (128, 256, 128), (256, 320, 64))
STAT_TILES = (0, 128, 192)


def f32(ap):
    return ap.bitcast(F32)


def plan_chunks():
    chunks, start = [], {}

    def section(name, items):
        start[name] = len(chunks)
        chunks.extend(items)

    def ffn(which):
        section(f"up{which}", [("up", which, j) for j in range(FT)])
        section(f"down{which}", [("down", which, j, half) for j in range(KT) for half in range(2)])

    ffn(0)
    section("z", [("in", Z0 + 256 * c) for c in range(4)])
    section("xbc", [("in", XBC0 + 256 * c) for c in range(8)])
    section("misc", [("misc",)])
    section("merge0", [(kind, 0, c) for c in range(4) for kind in ("gate", "branch")])
    section("qi", [("in", QI0)])
    section("kb", [("in", KB0)])
    section("vb", [("in", VB0)])
    section("qb", [("in", QB0 + 256 * c) for c in range(4)])
    section("merge1", [(kind, 1, c) for c in range(4) for kind in ("gate", "branch")])
    section("kc", [("in", KC0 + 256 * c) for c in range(4)])
    section("vc", [("in", VC0 + 256 * c) for c in range(4)])
    section("qc", [("in", QC0 + 256 * c) for c in range(4)])
    section("merge2", [(kind, 2, c) for c in range(4) for kind in ("gate", "branch")])
    section("out", [("out", c) for c in range(4)])
    ffn(1)
    section("ple", [(kind, c) for c in range(4) for kind in ("ple", "plegate")])
    return chunks, start


CHUNKS, START = plan_chunks()
N_CHUNKS = len(CHUNKS)


def loads_of(n):
    return {"up": 2, "misc": 5}.get(CHUNKS[n][0], 1)


def loaded_count(n):
    return 16 * sum(loads_of(m) for m in range(n % RING, n + 1, RING))


def frees(n):
    return not (CHUNKS[n][0] == "down" and CHUNKS[n][3] == 1)


def freed_before(n):
    return sum(frees(m) for m in range(n % RING, n, RING))


def build(nc, a, outs, bias_line, bias_square):
    (y_p, y_s, dsa_k_p, dsa_v_p, idx_k_p, band_k_p, band_v_p, ssm_p, conv_p,
     dsa_k_s, dsa_v_s, idx_k_s, band_k_s, band_v_s, ssm_s, conv_s) = outs
    with ExitStack() as ctx:
        def sb(name, shape, dt=F32, stack=ctx):
            return stack.enter_context(nc.sbuf_tensor(name, shape, dt))

        bank = [ctx.enter_context(nc.psum_tensor(f"bank{i}", [P, 512], F32)) for i in range(8)]
        stat_bank, row_bank = bank[6], bank[7]

        stage = sb("stage", [P, RING, SLOT])
        w_hi = sb("w_hi", [P, RING, SLOT], F32R)
        w_lo = sb("w_lo", [P, RING, SLOT], F32R)
        x = sb("x", [P, KT, TOK])
        y = sb("y", [P, KT, TOK])
        u_hi = sb("u_hi", [P, KT, TOK], F32R)
        u_lo = sb("u_lo", [P, KT, TOK], F32R)
        p_hi = sb("p_hi", [P, 2, TOK], F32R)
        p_lo = sb("p_lo", [P, 2, TOK], F32R)
        ident = sb("ident", [P, P])
        ones = sb("ones", [P, P])
        tri = sb("tri", [P, P])
        conv_cols = sb("conv_cols", [P, CT, 8])
        gain_cols = sb("gain_cols", [P, KT, 12])
        head_rows = sb("head_rows", [P, TOK])
        head_cols = sb("head_cols", [P, 3, P])
        d_col = sb("d_col", [P, KT])
        dt_bias = sb("dt_bias", [HEADS, 1])
        neg_a = sb("neg_a", [HEADS, 1])
        square = sb("square", [P, 2, TOK])
        split_tmp = sb("split_tmp", [P, RING, TOK])
        th = sb("th", [P, RING, TOK])
        rs = sb("rs", [P, 5, 12])
        diag = sb("diag", [P, 3, P])
        shift = sb("shift", [P, 2, 3])
        denom = sb("denom", [P, 2, 3])
        chunk_decay = sb("chunk_decay", [P, HEADS, 2])

        with ExitStack() as region:
            h_hi = sb("h_hi", [P, FT, TOK], F32R, region)
            h_lo = sb("h_lo", [P, FT, TOK], F32R, region)
        with ExitStack() as region:
            conv_rows = sb("conv_rows", [8, CONV_CH], F32, region)
            gain_rows = sb("gain_rows", [12, D], F32, region)
            p_rows = sb("p_rows", [P, 3, PLE], F32, region)
            bias_rows = sb("bias_rows", [P, 4, HEADS], F32, region)
            bias_rev = sb("bias_rev", [HEADS, 512], F32, region)
        with ExitStack() as region:
            io_rows = sb("io_rows", [P, 3, D], F32, region)
        with ExitStack() as region:
            ki = sb("ki", [P, TOK], F32, region)
            with ExitStack() as over:
                br_hi = sb("br_hi", [P, KT, TOK], F32R, over)
                br_lo = sb("br_lo", [P, KT, TOK], F32R, over)
                band_bias = sb("band_bias", [P, 2, 256], F32, over)
            with ExitStack() as mamba:
                conv_tail = sb("conv_tail", [70, CONV_CH], F32, mamba)
            xdt = sb("xdt", [P, 3, D], F32, region)
            b_rows = sb("b_rows", [P, 3, GROUPS * D_STATE], F32, region)
            xdec = sb("xdec", [P, D], F32, region)
            with ExitStack() as mamba:
                z = sb("z", [P, KT, TOK], F32, mamba)
                xbc = sb("xbc", [P, CT, XP], F32, mamba)
                h_sample = sb("h_sample", [P, D], F32, mamba)
                with ExitStack() as early:
                    state_rows = sb("state_rows", [P, KT, P], F32, early)
                h_prompt = sb("h_prompt", [P, D], F32, mamba)
                with ExitStack() as early:
                    conv_acc = sb("conv_acc", [P, 2, CONV_N], F32, early)
                    conv_th = sb("conv_th", [P, 2, CONV_N], F32, early)
                with ExitStack() as late:
                    h_rows = sb("h_rows", [P, KT, P], F32, late)
                cb = sb("cb", [P, GROUPS, CONV_N], F32, mamba)
                with ExitStack() as early:
                    dt_tmp = sb("dt_tmp", [HEADS, 3, TOK], F32, early)
                with ExitStack() as late:
                    row_exp = sb("row_exp", [P, 2, TOK], F32, late)
                    seg = sb("seg", [P, 2, TOK], F32, late)
                with ExitStack() as late:
                    diag_groups = sb("diag_groups", [P, 12, P], F32, late)
            attn = region.enter_context(ExitStack())
            logit = sb("logit", [P, 2, 576], F32, attn)
            prob_t = sb("prob_t", [P, 2, 512], F32, attn)
            k_c_rows = prob_t[:].rearrange("p c k -> p (c k)")
            with ExitStack() as dsa:
                q_b = sb("q_b", [P, KT, TOK], F32, dsa)
                k_b = sb("k_b", [P, 2, TOK], F32, dsa)
                q_i = sb("q_i", [P, 2, TOK], F32, dsa)
                v_b = sb("v_b", [P, 3, 256], F32, dsa)
                v_b_past = sb("v_b_past", [P, 256], F32, dsa)
                k_b_past = sb("k_b_past", [P, 384], F32, dsa)
                k_b_past_t = sb("k_b_past_t", [P, 3, PAST], F32, dsa)
                k_b_rows = sb("k_b_rows", [P, 3, 320], F32, dsa)
                score = sb("score", [P, 576], F32, dsa)
                score_relu = sb("score_relu", [P, 2, 576], F32, dsa)
                top8 = sb("top8", [P, 8], F32, dsa)
                dsa_mask = sb("dsa_mask", [P, 576], F32, dsa)
            with ExitStack() as band:
                q_c = sb("q_c", [P, KT, TOK], F32, band)
                k_c = sb("k_c", [P, KT, TOK], F32, band)
                v_c = sb("v_c", [P, 3, D], F32, band)
                v_c_past = sb("v_c_past", [P, D], F32, band)
                k_c_past_t = sb("k_c_past_t", [P, KT, PAST], F32, band)

        names = (
            ["loaded0", "loaded1", "loaded2", "w_hi_ready", "w_lo_ready", "chunk_done", "bank_free0", "bank_free1",
             "bank_free2", "rows_loaded", "rows_turned", "cols_ready", "p_ready", "bias_rev_ready", "bias_written", "bias_squared",
             "square_ready", "square_used", "stat_ready", "diag_ready", "row_ready", "split_src", "split_hi",
             "split_lo", "tanh_ready", "silu_ready", "x_ready", "y_ready", "dve_step", "act_step", "pool_step",
             "evac", "z_tanh", "z_done", "tail_turned", "tail_copied", "tail_stored", "conv_ready", "conv_tanh",
             "conv_done", "dt_v", "dt_exp", "dt_done", "decay_done", "rows_cols_turned", "head_cols_ready",
             "state_loaded", "state_turned", "state_ready", "xs_turned", "xdt_ready", "b_turned", "b_ready",
             "cb_ready", "cb_masked", "xdec_ready", "delta_ready", "h1_ready", "bc_ready", "row_exp_ready",
             "seg_ready", "seg_exp", "mt_ready", "head_done", "mixed", "h_final", "h_turned", "h_rows_ready",
             "h_stored", "k_past_loaded", "v_past_loaded", "past_turned", "past_ready", "k_turned",
             "k_rows_ready", "k_stored", "v_stored", "idx_ready", "idx_relu", "idx_used", "mask_ready",
             "scored", "shifted", "exped", "normed", "p_turned", "p_copied", "attended", "attn_hi", "attn_lo",
             "bias_loaded0", "bias_loaded1", "bias_masked", "gate_tanh", "merged", "x_loaded", "x_turned", "y_turned", "y_rows_ready",
             "y_stored", "setup"])
        sem = {name: ctx.enter_context(nc.semaphore(name)) for name in names}
        every = range(min(s.num for s in sem.values()), max(s.num for s in sem.values()) + 1)
        assert len(every) == len(names)
        loaded = [sem[f"loaded{s}"] for s in range(RING)]
        bank_free = [sem[f"bank_free{s}"] for s in range(RING)]

        class Chain:

            def __init__(self, engine, semaphore):
                self.engine, self.semaphore, self.count = engine, semaphore, 0

            def __call__(self, instruction):
                self.count += 1
                instruction.then_inc(self.semaphore, 1)
                self.engine.wait_ge(self.semaphore, self.count)

        with nc.Block() as block:
            @block.sync
            def _(sp):
                sp.dma_start(io_rows[:, 0:2, :], a["x_prompt"][0].rearrange("(t p) d -> p t d", p=P))\
                    .then_inc(sem["x_loaded"], 16)
                sp.dma_start(io_rows[0:DEC, 2, :], a["x_sample"][0]).then_inc(sem["x_loaded"], 16)

            @block.gpsimd
            def _(pool):
                pool.memset(ident[:], 0.0).then_inc(sem["pool_step"], 1)
                pool.memset(ones[:], 1.0).then_inc(sem["pool_step"], 1)
                pool.memset(tri[:], 1.0).then_inc(sem["pool_step"], 1)
                pool.memset(head_rows[:], 0.0).then_inc(sem["pool_step"], 1)
                pool.memset(shift[:], 0.0).then_inc(sem["pool_step"], 1)
                pool.memset(denom[:], 1.0).then_inc(sem["pool_step"], 1)
                pool.wait_ge(sem["pool_step"], 3)
                pool.affine_select(out=ident[:], in_=ident[:], compare_op=ALU.not_equal, fill=1.0, base=0,
                                   pattern=[[-1, P]], channel_multiplier=1).then_inc(sem["setup"], 1)
                pool.affine_select(out=tri[:], in_=tri[:], compare_op=ALU.is_ge, fill=0.0, base=0,
                                   pattern=[[1, P]], channel_multiplier=-1).then_inc(sem["setup"], 1)

            @block.tensor
            def _(pe):
                pe.wait_ge(sem["setup"], 1)
                pe.wait_ge(sem["x_loaded"], 32)
                for k in range(KT):
                    for t, (t0, t1, n) in enumerate(TILES):
                        last = pe.transpose(bank[k][:, t0:t1], io_rows[0:n, t, P * k:P * (k + 1)], ident[0:n, 0:n])
                    last.then_inc(sem["x_turned"], 1)

            @block.vector
            def _(dve):
                for k in range(KT):
                    dve.wait_ge(sem["x_turned"], k + 1)
                    dve.tensor_copy(x[:, k, :], bank[k][:, 0:TOK]).then_inc(sem["dve_step"], 1)

        nc.all_engine_barrier(sems_to_clear=every)

        NORMS = [("ffn0_pre", 8, 1), ("ffn0_post", 8, 1), ("mix_pre", 8, 1), ("ssm", 8, 4), ("mix_post", 8, 1),
                 ("ffn1_pre", 8, 1), ("ffn1_post", 8, 1), ("ple_pre", 8, 1), ("ple_post", 8, 1)]
        NORM = {name: i for i, (name, _, _) in enumerate(NORMS)}
        ROW_BANKS = {1: [7], 4: [0, 1, 2, 3]}
        SPLITS = {}
        count = 0
        for name, n in (("u_ffn0", KT), ("h0", FT), ("u_mix", KT), ("ssm", KT), ("mix", KT), ("u_ffn1", KT),
                        ("h1", FT), ("u_ple", KT)):
            SPLITS[name] = count
            count += n

        def layer_body(layer, block):
            @block.sync
            def _(sp):
                def load_chunk(n, up_tile=None, loop=None):
                    kind, s = CHUNKS[n], n % RING
                    if loop is not None:
                        j = up_tile
                        src = a["ffn_w13"][layer, kind[1]].rearrange("(k p) (h j c) -> p k h j c", p=P, h=2, c=P)
                        parts = [(stage[:, s, 0:SLOT].rearrange("p (k h c) -> p k h c", h=2, c=P)[:, :, h, :],
                                  src[:, :, h, bass.ds(j, 1), :].rearrange("p k j c -> p k (j c)"))
                                 for h in range(2)]
                        sp.wait_ge(sem["w_lo_ready"], n - RING + 1 + RING * loop)
                        for dst, src_part in parts:
                            sp.dma_start(dst, src_part).then_inc(loaded[s], 16)
                        return
                    if n >= RING:
                        sp.wait_ge(sem["w_lo_ready"], n - RING + 1)
                    cols = stage[:, s, 0:SLOT].rearrange("p (k c) -> p k c", c=256)
                    if kind[0] == "up":
                        src = a["ffn_w13"][layer, kind[1]].rearrange("(k p) (h j c) -> p k h j c", p=P, h=2, c=P)
                        dst = stage[:, s, 0:SLOT].rearrange("p (k h c) -> p k h c", h=2, c=P)
                        for h in range(2):
                            sp.dma_start(dst[:, :, h, :], src[:, :, h, kind[2], :]).then_inc(loaded[s], 16)
                    elif kind[0] == "down":
                        src = a["ffn_w2"][layer, kind[1]].rearrange("(k p) (j c) -> p k j c", p=P, c=P)
                        sp.dma_start(stage[:, s, 0:HALF_FT * P].rearrange("p (k c) -> p k c", c=P),
                                     src[:, HALF_FT * kind[3]:HALF_FT * (kind[3] + 1), kind[2], :])\
                            .then_inc(loaded[s], 16)
                    elif kind[0] == "misc":
                        src = a["w_in"][layer].rearrange("(k p) c -> p k c", p=P)
                        for dst, c, w in ((0, KI0, 64), (64, KI0, 64), (128, DT0, 32), (160, WI0, 32), (192, DT0, 64)):
                            sp.dma_start(cols[:, :, dst:dst + w], src[:, :, c:c + w]).then_inc(loaded[s], 16)
                    elif kind[0] == "ple":
                        src = a["w_ple"][layer].rearrange("(k p) (j c) -> p k j c", p=P, c=256)
                        sp.dma_start(cols[:, 0:2, :], src[:, :, kind[1], :]).then_inc(loaded[s], 16)
                    else:
                        if kind[0] == "in":
                            src, c = a["w_in"][layer], kind[1]
                        elif kind[0] == "gate":
                            src, c = a["w_gate"][layer], kind[1] * D + 256 * kind[2]
                        elif kind[0] == "branch":
                            src, c = a["w_branch"][layer, kind[1]], 256 * kind[2]
                        elif kind[0] == "out":
                            src, c = a["w_out"][layer], 256 * kind[1]
                        else:
                            src, c = a["w_ple_gate"][layer], 256 * kind[1]
                        sp.dma_start(cols, src.rearrange("(k p) c -> p k c", p=P)[:, :, c:c + 256])\
                            .then_inc(loaded[s], 16)

                def load_ffn(which):
                    n0 = START[f"up{which}"]
                    for n in range(n0, n0 + RING):
                        load_chunk(n)
                    if which == 0:
                        sp.wait_ge(sem["bias_rev_ready"], 1)
                        sp.dma_start(bias_line, bias_rev[:]).then_inc(sem["bias_written"], 16)
                    with sp.Fori(1, 6) as i:
                        for s in range(RING):
                            load_chunk(n0 + s, up_tile=i * RING + s, loop=i)
                    for n in range(n0 + 6 * RING, START[f"down{which}"] + 2 * KT):
                        load_chunk(n)

                def load_section(name, n_chunks):
                    for n in range(START[name], START[name] + n_chunks):
                        load_chunk(n)

                rows = sem["rows_loaded"]
                sp.dma_start(conv_rows[0:4, :], a["conv_w"][layer]).then_inc(rows, 16)
                sp.dma_start(conv_rows[4:5, :], a["conv_b"][layer].unsqueeze(0)).then_inc(rows, 16)
                sp.dma_start(conv_rows[5:8, :], a["state_conv"][layer, 0]).then_inc(rows, 16)
                sp.dma_start(gain_rows[0:8, :], a["norm_g"][layer]).then_inc(rows, 16)
                sp.dma_start(gain_rows[8:9, :], a["ssm_norm_g"][layer].unsqueeze(0)).then_inc(rows, 16)
                sp.dma_start(gain_rows[9:12, :], a["b_gate"][layer].rearrange("(r c) -> r c", c=D)).then_inc(rows, 16)
                sp.dma_start(p_rows[:, 0:2, :], a["p_prompt"][layer, 0].rearrange("(t p) c -> p t c", p=P))\
                    .then_inc(rows, 16)
                sp.dma_start(p_rows[0:DEC, 2, :], a["p_sample"][layer, 0]).then_inc(rows, 16)
                sp.dma_start(bias_rows[:], a["rel_bias"][layer, 0:512].rearrange("(j p) h -> p j h", p=P))\
                    .then_inc(rows, 16)
                sp.dma_start(dt_bias[:], a["dt_bias"][layer].unsqueeze(1)).then_inc(rows, 16)
                sp.dma_start(neg_a[:], a["a_log"][layer].unsqueeze(1)).then_inc(rows, 16)
                skip = a["d_skip"][layer].rearrange("(i h) -> h i", h=2)
                for half in range(2):
                    sp.dma_start(d_col[64 * half:64 * (half + 1), :], skip[half:half + 1, :].broadcast_to([64, KT]),
                                 allow_slow_non_contiguous=True)\
                        .then_inc(rows, 16)
                load_ffn(0)
                sp.wait_ge(sem["bias_written"], 16)
                sp.dma_start(bias_square, bass.AP(bias_line.tensor, 127, [[512, HEADS], [-1, P], [1, 256]]))\
                    .then_inc(sem["bias_squared"], 16)
                sp.wait_ge(sem["chunk_done"], START["z"])
                sp.dma_start(state_rows[:], a["state_ssm"][layer, 0].rearrange("(i h) d n -> (h d) i n", h=2))\
                    .then_inc(sem["state_loaded"], 16)
                load_section("z", 13)
                load_section("merge0", 2)
                sp.wait_ge(sem["tail_copied"], 4)
                sp.dma_start(conv_p[layer, 0], conv_tail[0:3, :]).then_inc(sem["tail_stored"], 16)
                sp.dma_start(conv_s[layer, 0], conv_tail[67:70, :]).then_inc(sem["tail_stored"], 16)
                for b, dst in enumerate((ssm_p, ssm_s)):
                    sp.wait_ge(sem["h_rows_ready"], 2 * b + 2)
                    sp.dma_start(dst[layer, 0].rearrange("(i h) d n -> (h d) i n", h=2), h_rows[:])\
                        .then_inc(sem["h_stored"], 16)
                sp.wait_ge(sem["h_stored"], 32)
                sp.wait_ge(sem["split_lo"], SPLITS["ssm"] + KT)
                ck = a["cache_dsa_k"][layer, 0].rearrange("t g d -> t (g d)")
                cv = a["cache_dsa_v"][layer, 0].rearrange("t g d -> t (g d)")
                sp.dma_start(k_b_past[:, 0:256], ck).then_inc(sem["k_past_loaded"], 16)
                for c in range(2):
                    sp.dma_start(k_b_past[:, 256 + 64 * c:320 + 64 * c], a["cache_idx_k"][layer, 0])\
                        .then_inc(sem["k_past_loaded"], 16)
                sp.dma_start(v_b_past[:], cv).then_inc(sem["v_past_loaded"], 16)
                for n in range(START["merge0"] + 2, START["merge1"] + 2):
                    load_chunk(n)

                def store_tokens(src, prompt, sample, signal, rows_at=0):
                    sp.dma_start(prompt[layer, 0].rearrange("(t p) c -> p t c", p=P), src[:, 0:2]).then_inc(signal, 16)
                    sp.dma_start(sample[layer, 0], src[rows_at:rows_at + DEC, 2]).then_inc(signal, 16)

                sp.wait_ge(sem["k_rows_ready"], 3)
                store_tokens(k_b_rows[:, :, 0:256], dsa_k_p, dsa_k_s, sem["k_stored"])
                store_tokens(k_b_rows[:, :, 256:320], idx_k_p, idx_k_s, sem["k_stored"])
                sp.wait_ge(sem["evac"], EVAC["vb"] + 1)
                store_tokens(v_b[:], dsa_v_p, dsa_v_s, sem["v_stored"], 64)
                sp.wait_ge(sem["k_stored"], 64)
                sp.wait_ge(sem["v_stored"], 32)
                sp.wait_ge(sem["attended"], KT)
                sp.wait_ge(sem["bias_squared"], 16)
                sp.dma_start(k_c_rows, a["cache_band_k"][layer, 0].rearrange("t h d -> t (h d)"))\
                    .then_inc(sem["k_past_loaded"], 16)
                sp.dma_start(v_c_past[:], a["cache_band_v"][layer, 0].rearrange("t h d -> t (h d)"))\
                    .then_inc(sem["v_past_loaded"], 16)
                for n in range(START["merge1"] + 2, START["qc"]):
                    load_chunk(n)
                for n in range(START["qc"], START["merge2"] + 2):
                    load_chunk(n)
                for t, (_, _, rows_n) in enumerate(TILES):
                    sp.wait_ge(sem["k_rows_ready"], 3 + 2 * (t + 1))
                    dst = band_k_p[layer, 0, P * t:P * (t + 1)] if t < 2 else band_k_s[layer, 0]
                    sp.dma_start(dst, k_c_rows[0:rows_n, :]).then_inc(sem["k_stored"], 16)
                for h in range(HEADS):
                    if h >= 2:
                        sp.wait_ge(sem["shifted"], 8 + h - 1)
                    sp.dma_start(band_bias[:, h % 2, :], bias_square[h])\
                        .then_inc(sem[f"bias_loaded{h % 2}"], 16)
                sp.wait_ge(sem["evac"], EVAC["vc"] + 4)
                store_tokens(v_c[:], band_v_p, band_v_s, sem["v_stored"], 64)
                sp.wait_ge(sem["v_stored"], 64)
                for n in range(START["merge2"] + 2, START["up1"]):
                    load_chunk(n)
                load_ffn(1)
                load_section("ple", 8)
                sp.wait_ge(sem["tail_stored"], 32)
                sp.wait_ge(sem["k_stored"], 112)

            @block.gpsimd
            def _(pool):
                def rest(n, loop=None):
                    s = n % RING
                    size = SIZE[CHUNKS[n][0]]
                    pool.wait_ge(sem["w_hi_ready"], n + 1 if loop is None else n + 1 + RING * loop)
                    pool.tensor_tensor(w_lo[:, s, 0:size], stage[:, s, 0:size], f32(w_hi[:, s, 0:size]), ALU.subtract)\
                        .then_inc(sem["w_lo_ready"], 1)

                def rest_ffn(which):
                    n0 = START[f"up{which}"]
                    for n in range(n0, n0 + RING):
                        rest(n)
                    with pool.Fori(1, 6) as i:
                        for s in range(RING):
                            rest(n0 + s, loop=i)
                    for n in range(n0 + 6 * RING, START[f"down{which}"] + 2 * KT):
                        rest(n)

                rest_ffn(0)
                for n in range(START["z"], START["up1"]):
                    rest(n)
                rest_ffn(1)
                for n in range(START["ple"], N_CHUNKS):
                    rest(n)

            @block.scalar
            def _(act):
                def heads(n, loop=None):
                    if n >= N_CHUNKS:
                        return
                    s = n % RING
                    size = SIZE[CHUNKS[n][0]]
                    if loop is None:
                        act.wait_ge(loaded[s], loaded_count(n))
                        if n >= RING:
                            act.wait_ge(sem["chunk_done"], n - RING + 1)
                    else:
                        act.wait_ge(loaded[s], loaded_count(n) + 32 * loop)
                        act.wait_ge(sem["chunk_done"], n - RING + 1 + RING * loop)
                    act.activation(w_hi[:, s, 0:size], stage[:, s, 0:size], ACT.Copy).then_inc(sem["w_hi_ready"], 1)

                def squares(norm, ready, src, first=1):
                    for k in range(KT):
                        c = KT * NORM[norm] + k
                        if ready is not None:
                            act.wait_ge(sem[ready], first + k)
                        if c >= 2:
                            act.wait_ge(sem["square_used"], c - 1)
                        act.activation(square[:, c % 2, :], src[:, k, :], ACT.Square).then_inc(sem["square_ready"], 1)

                def split_head(q, dst):
                    act.wait_ge(sem["split_src"], q + 1)
                    act.activation(dst, split_tmp[:, q % RING, :], ACT.Copy).then_inc(sem["split_hi"], 1)

                def split_heads(name, dst):
                    for k in range(KT):
                        split_head(SPLITS[name] + k, dst[:, k, :])

                def up_chunk(which, j, loop=None):
                    n = START[f"up{which}"] + j
                    s, more = n % RING, 0 if loop is None else RING * loop
                    act.wait_ge(sem["chunk_done"], n + 1 + more)
                    act.activation(th[:, s, :], bank[2 * s][:, 0:TOK], ACT.Tanh, scale=0.5)\
                        .then_inc(sem["tanh_ready"], 1)
                    q = SPLITS[f"h{which}"] + j
                    act.wait_ge(sem["split_src"], q + 1 + more)
                    dst = h_hi[:, j, :] if loop is None else \
                        h_hi[:, bass.ds(loop * RING + j, 1), :].rearrange("p j t -> p (j t)")
                    act.activation(dst, split_tmp[:, q % RING, :], ACT.Copy).then_inc(sem["split_hi"], 1)

                def ffn(which):
                    n0 = START[f"up{which}"]
                    squares(f"ffn{which}_pre", None if which == 0 else "x_ready", x, XR[f"ffn{which}"] + 1)
                    split_heads(f"u_ffn{which}", u_hi)
                    for j in range(RING):
                        heads(n0 + j + 2)
                        up_chunk(which, j)
                    with act.Fori(1, 6) as i:
                        for j in range(RING):
                            heads(n0 + j + 2, loop=i)
                            up_chunk(which, j, loop=i)
                    for j in range(6 * RING, FT):
                        heads(n0 + j + 2)
                        up_chunk(which, j)
                    n1 = START[f"down{which}"]
                    for n in range(n1, n1 + 2 * KT):
                        heads(n + 2)
                        if (n - n1) % 2 == 1 and n - n1 > 1:
                            square_y(f"ffn{which}_post", (n - n1) // 2 - 1)
                    square_y(f"ffn{which}_post", KT - 1)

                def square_y(norm, k):
                    c = KT * NORM[norm] + k
                    act.wait_ge(sem["y_ready"], YR[norm] + k + 1)
                    act.wait_ge(sem["square_used"], c - 1)
                    act.activation(square[:, c % 2, :], y[:, k, :], ACT.Square).then_inc(sem["square_ready"], 1)

                step = Chain(act, sem["act_step"])

                heads(0)
                heads(1)
                act.wait_ge(sem["rows_turned"], 1)
                for k in range(2):
                    act.activation(p_hi[:, k, :], bank[k][:, 0:TOK], ACT.Copy).then_inc(sem["p_ready"], 1)
                act.activation(bias_rev[:, ::-1], bank[2][0:HEADS, :], ACT.Copy, scale=-1.0).then_inc(sem["bias_rev_ready"], 1)
                act.wait_ge(sem["rows_loaded"], 16 * 13)
                step(act.activation(neg_a[:], neg_a[:], ACT.Exp))
                act.wait_ge(sem["bias_written"], 16)
                ffn(0)

                squares("mix_pre", "x_ready", x, XR["mix"] + 1)
                split_heads("u_mix", u_hi)
                act.wait_ge(sem["state_turned"], 1)
                for b in range(2):
                    act.activation(h_sample[:, 512 * b:512 * (b + 1)], bank[4 + b][:], ACT.Copy)\
                        .then_inc(sem["state_ready"], 1)
                for n in range(START["z"], START["merge0"]):
                    heads(n + 2)
                for b in range(4):
                    act.wait_ge(sem["tail_turned"], b + 1)
                    act.activation(conv_tail[:, 512 * b:512 * (b + 1)], bank[TAIL_BANK[b]][0:70, :], ACT.Copy)\
                        .then_inc(sem["tail_copied"], 1)
                for k in range(KT):
                    if k >= 2:
                        act.wait_ge(sem["z_done"], k - 1)
                    act.wait_ge(sem["evac"], EVAC["z"] + 4)
                    act.activation(conv_th[:, k % 2, 0:TOK], z[:, k, :], ACT.Tanh).then_inc(sem["z_tanh"], 1)
                for i in range(CT):
                    act.wait_ge(sem["conv_ready"], i + 1)
                    if i < 2:
                        act.wait_ge(sem["z_done"], KT)
                    else:
                        act.wait_ge(sem["conv_done"], i - 1)
                    act.activation(conv_th[:, i % 2, :], conv_acc[:, i % 2, :], ACT.Tanh).then_inc(sem["conv_tanh"], 1)
                act.wait_ge(sem["dt_v"], 1)
                step(act.activation(dt_tmp[:, 1, :], dt_tmp[:, 1, :], ACT.Exp))
                act.activation(dt_tmp[:, 1, :], dt_tmp[:, 1, :], ACT.Ln, bias=1.0).then_inc(sem["dt_exp"], 1)
                act.wait_ge(sem["dt_done"], 1)
                for t, (t0, t1, _) in enumerate(TILES):
                    act.activation(head_rows[32:32 + HEADS, t0:t1], head_rows[0:HEADS, t0:t1], ACT.Exp,
                                   bias=head_rows[0:HEADS, t1 - 1:t1], scale=-1.0).then_inc(sem["decay_done"], 1)
                for t, (_, _, n) in enumerate(TILES):
                    act.wait_ge(sem["b_turned"], t + 1)
                    act.activation(b_rows[0:n, t, :], bank[t][0:n, :], ACT.Copy).then_inc(sem["b_ready"], 1)
                act.wait_ge(sem["delta_ready"], 1)
                for b in range(2):
                    act.activation(h_prompt[:, 512 * b:512 * (b + 1)], bank[4 + b][:], ACT.Copy)\
                        .then_inc(sem["h1_ready"], 1)

                def row_exponential(h):
                    act.wait_ge(sem["seg_ready"], h + 1)
                    if h >= 2:
                        act.wait_ge(sem["mt_ready"], h - 1)
                    act.activation(row_exp[:, h % 2, :], bank[h % 2][:, 0:TOK], ACT.Exp)
                    act.activation(chunk_decay[:, h, :], bank[h % 2][:, 255:TOK:64], ACT.Exp)\
                        .then_inc(sem["row_exp_ready"], 1)

                row_exponential(0)
                for h in range(HEADS):
                    act.activation(seg[:, h % 2, 0:SEQ], seg[:, h % 2, 0:SEQ], ACT.Exp)
                    act.activation(seg[0:DEC, h % 2, SEQ:TOK], seg[0:DEC, h % 2, SEQ:TOK], ACT.Exp)\
                        .then_inc(sem["seg_exp"], 1)
                    if h + 1 < HEADS:
                        row_exponential(h + 1)
                for b in range(4):
                    act.wait_ge(sem["h_turned"], b + 1)
                    if b == 2:
                        act.wait_ge(sem["h_stored"], 16)
                    act.activation(h_rows[:, 4 * (b % 2):4 * (b % 2) + 4, :].rearrange("p i n -> p (i n)"),
                                   bank[b][:], ACT.Copy).then_inc(sem["h_rows_ready"], 1)
                squares("ssm", "mixed", z)
                split_heads("ssm", br_hi)

                def merge(b):
                    for c in range(4):
                        n = START[f"merge{b}"] + 2 * c
                        heads(n + 2)
                        s = n % RING
                        act.wait_ge(sem["chunk_done"], n + 1)
                        for half in range(2):
                            g = 8 * b + 2 * c + half
                            if g >= 2:
                                act.wait_ge(sem["merged"], g - 1)
                            ins = act.activation(th[:, g % 2, :], bank[2 * s + half][:, 0:TOK], ACT.Tanh,
                                                 scale=0.5, bias=gain_cols[:, 2 * c + half, 9 + b:10 + b])
                            ins.then_inc(sem["gate_tanh"], 1)
                        heads(n + 3)

                merge(0)

                for n in range(START["qi"], START["merge1"]):
                    heads(n + 2)
                act.wait_ge(sem["past_turned"], 1)
                act.activation(k_b_past_t[:].rearrange("p i t -> p (i t)"), bank[3][:, 0:384], ACT.Copy)\
                    .then_inc(sem["past_ready"], 1)
                for t, (_, _, n) in enumerate(TILES):
                    act.wait_ge(sem["k_turned"], t + 1)
                    act.activation(k_b_rows[0:n, t, :], bank[t][0:n, 0:320], ACT.Copy).then_inc(sem["k_rows_ready"], 1)
                for h in range(4):
                    act.wait_ge(sem["idx_ready"], h + 1)
                    if h >= 2:
                        act.wait_ge(sem["idx_used"], h - 1)
                    act.activation(score_relu[:, h % 2, 0:384], bank[4 + h % 2][:, 0:384], ACT.Relu)
                    act.activation(score_relu[0:DEC, h % 2, 384:576], bank[6 + h % 2][0:DEC, 0:192], ACT.Relu)\
                        .then_inc(sem["idx_relu"], 1)

                def exponentials(c):
                    act.wait_ge(sem["shifted"], c + 1)
                    for j, (r, k0, k1) in enumerate(SPANS):
                        ins = act.activation(logit[0:r, c % 2, k0:k1], logit[0:r, c % 2, k0:k1], ACT.Exp, scale=-1.0,
                                             bias=shift[0:r, c % 2, j:j + 1], accum_out=denom[0:r, c % 2, j:j + 1])
                    ins.then_inc(sem["exped"], 1)

                def attention(first, n_heads, per_tile):
                    exponentials(first)
                    for h in range(n_heads):
                        c = first + h
                        if h + 1 < n_heads:
                            exponentials(c + 1)
                        act.wait_ge(sem["p_turned"], c + 1)
                        if c >= 2:
                            act.wait_ge(sem["attended"], c - 1)
                        act.activation(prob_t[:, c % 2, :], bank[4 + c % 2][:], ACT.Copy).then_inc(sem["p_copied"], 1)
                        if h % per_tile == per_tile - 1:
                            tile = h // per_tile
                            act.wait_ge(sem["attended"], c + 1)
                            act.activation(br_hi[:, tile, :], bank[6 + tile % 2][:, 0:TOK], ACT.Copy)\
                                .then_inc(sem["attn_hi"], 1)

                attention(0, 8, 1)
                merge(1)
                act.wait_ge(sem["past_turned"], 3)
                for b in range(2):
                    act.activation(k_c_past_t[:, 4 * b:4 * b + 4, :].rearrange("p i t -> p (i t)"), bank[6 + b][:],
                                   ACT.Copy).then_inc(sem["past_ready"], 1)
                for n in range(START["kc"], START["merge2"]):
                    heads(n + 2)
                for t, (_, _, rows_n) in enumerate(TILES):
                    for b in range(2):
                        act.wait_ge(sem["k_turned"], 3 + 2 * t + b + 1)
                        if b == 0:
                            if t == 0:
                                act.wait_ge(sem["past_ready"], 3)
                            else:
                                act.wait_ge(sem["k_stored"], 64 + 16 * t)
                        act.activation(k_c_rows[0:rows_n, 512 * b:512 * (b + 1)], bank[(2 * t + b) % 4][0:rows_n, :],
                                       ACT.Copy).then_inc(sem["k_rows_ready"], 1)
                attention(8, 16, 2)
                merge(2)
                split_heads("mix", br_hi)
                for c in range(4):
                    n = START["out"] + c
                    heads(n + 2)
                    if c >= 1:
                        square_y("mix_post", 2 * c - 2)
                        square_y("mix_post", 2 * c - 1)
                square_y("mix_post", 6)
                square_y("mix_post", 7)
                act.wait_ge(sem["k_stored"], 112)
                act.wait_ge(sem["v_stored"], 64)
                ffn(1)
                squares("ple_pre", "x_ready", x, XR["ple"] + 1)
                split_heads("u_ple", u_hi)
                for c in range(4):
                    n = START["ple"] + 2 * c
                    heads(n + 2)
                    heads(n + 3)
                    act.wait_ge(sem["chunk_done"], n + 2)
                    s = (n + 1) % RING
                    for half in range(2):
                        g = 24 + 2 * c + half
                        act.wait_ge(sem["merged"], g - 1)
                        act.activation(th[:, g % 2, :], bank[2 * s + half][:, 0:TOK], ACT.Tanh, scale=0.5)\
                            .then_inc(sem["gate_tanh"], 1)
                    if c >= 1:
                        square_y("ple_post", 2 * c - 2)
                        square_y("ple_post", 2 * c - 1)
                square_y("ple_post", 6)
                square_y("ple_post", 7)

            @block.tensor
            def _(pe):
                def claim(n, loop=None):
                    s = n % RING
                    if loop is None:
                        pe.wait_ge(sem["w_lo_ready"], n + 1)
                        if frees(n) and freed_before(n):
                            pe.wait_ge(bank_free[s], freed_before(n))
                    else:
                        pe.wait_ge(sem["w_lo_ready"], n + 1 + RING * loop)
                        pe.wait_ge(bank_free[s], freed_before(n) + loop)

                def product(out, s, offset, stride, k_tiles, hi, lo, start=True, stop=True, ready=None):
                    for k in range(k_tiles):
                        if ready is not None:
                            ready(k)
                        at = offset + stride * k
                        wh, wl = w_hi[:, s, at:at + P], w_lo[:, s, at:at + P]
                        pe.matmul(out, wh, hi[:, k, :], start=start and k == 0, stop=False)
                        pe.matmul(out, wh, lo[:, k, :], start=False, stop=False)
                        last = pe.matmul(out, wl, hi[:, k, :], start=False, stop=stop and k == k_tiles - 1)
                    return last

                def wide_chunk(n, hi, lo, k_tiles=KT, ready=None, loop=None):
                    claim(n, loop)
                    s = n % RING
                    for half in range(2):
                        last = product(bank[2 * s + half][:, 0:TOK], s, P * half, 2 * P, k_tiles, hi, lo,
                                       ready=ready if half == 0 else None)
                    last.then_inc(sem["chunk_done"], 1)

                def token_chunk(n):
                    claim(n)
                    s = n % RING
                    for t, t0 in enumerate(STAT_TILES):
                        out = bank[2 * s + t // 2][:, 256 * (t % 2):256 * (t % 2) + 256]
                        for k in range(KT):
                            wh, wl = (w[:, s, 256 * k:256 * (k + 1)] for w in (w_hi, w_lo))
                            uh, ul = (u[:, k, t0:t0 + P] for u in (u_hi, u_lo))
                            pe.matmul(out, uh, wh, start=k == 0, stop=False)
                            pe.matmul(out, ul, wh, start=False, stop=False)
                            last = pe.matmul(out, uh, wl, start=False, stop=k == KT - 1)
                    last.then_inc(sem["chunk_done"], 1)

                def split_ready(name):
                    return lambda k: pe.wait_ge(sem["split_lo"], SPLITS[name] + k + 1)

                def square_sum(name, k):
                    i = NORM[name]
                    c, g = KT * i + k, k * NORMS[i][2] // KT
                    pe.wait_ge(sem["square_ready"], c + 1)
                    for t, t0 in enumerate(STAT_TILES):
                        ins = pe.matmul(stat_bank[:, 3 * g + t:3 * g + t + 1], square[:, c % 2, t0:t0 + P],
                                        ones[:, 0:1], start=k == 0 and t == 0, stop=k == KT - 1 and t == 2,
                                        skip_group_check=True)
                    ins.then_inc(sem["square_used"], 1)

                def norm(name, first=0):
                    i = NORM[name]
                    groups = NORMS[i][2]
                    for k in range(first, KT):
                        square_sum(name, k)
                    pe.wait_ge(sem["diag_ready"], i + 1)
                    diagonals = diag if groups == 1 else diag_groups
                    for g, b in enumerate(ROW_BANKS[groups]):
                        for t, t0 in enumerate(STAT_TILES):
                            last = pe.matmul(bank[b][:, t0:t0 + P], ones[:], diagonals[:, 3 * g + t, :], start=True,
                                             stop=True)
                    last.then_inc(sem["row_ready"], 1)

                def ffn(which):
                    norm(f"ffn{which}_pre")
                    n0 = START[f"up{which}"]
                    for j in range(RING):
                        wide_chunk(n0 + j, u_hi, u_lo, ready=split_ready(f"u_ffn{which}") if j == 0 else None)
                    with pe.Fori(1, 6) as i:
                        for j in range(RING):
                            wide_chunk(n0 + j, u_hi, u_lo, loop=i)
                    for j in range(6 * RING, FT):
                        wide_chunk(n0 + j, u_hi, u_lo)
                    n1 = START[f"down{which}"]
                    for j in range(KT):
                        for half in range(2):
                            n = n1 + 2 * j + half
                            claim(n)
                            k0 = HALF_FT * half
                            ready = None
                            if j == 0:
                                def ready(k, k0=k0):
                                    pe.wait_ge(sem["split_lo"], SPLITS[f"h{which}"] + k0 + k + 1)
                            last = product(bank[2 * ((n1 + 2 * j) % RING)][:, 0:TOK], n % RING, 0, P, HALF_FT,
                                           h_hi[:, k0:k0 + HALF_FT, :], h_lo[:, k0:k0 + HALF_FT, :],
                                           start=half == 0, stop=half == 1, ready=ready)
                            last.then_inc(sem["chunk_done"], 1)
                        if j >= 1:
                            square_sum(f"ffn{which}_post", j - 1)
                    norm(f"ffn{which}_post", KT - 1)

                pe.wait_ge(sem["rows_loaded"], 16 * 13)
                for i in range(CT):
                    pe.transpose(bank[6][:, 8 * i:8 * i + 8], conv_rows[:, P * i:P * (i + 1)], ident[0:8, 0:8])
                for k in range(KT):
                    pe.transpose(bank[7][:, 12 * k:12 * k + 12], gain_rows[:, P * k:P * (k + 1)], ident[0:12, 0:12])
                for k in range(2):
                    for t, (t0, t1, n) in enumerate(TILES):
                        pe.transpose(bank[k][:, t0:t1], p_rows[0:n, t, P * k:P * (k + 1)], ident[0:n, 0:n])
                for j in range(4):
                    last = pe.transpose(bank[2][0:HEADS, P * j:P * (j + 1)], bias_rows[:, j, :], ident[:])
                last.then_inc(sem["rows_turned"], 1)
                pe.wait_ge(sem["cols_ready"], 1)
                pe.wait_ge(sem["bias_rev_ready"], 1)
                ffn(0)

                norm("mix_pre")
                pe.wait_ge(sem["state_loaded"], 16)
                for i in range(KT):
                    last = pe.transpose(bank[4 + i // 4][:, P * (i % 4):P * (i % 4 + 1)], state_rows[:, i, :], ident[:])
                last.then_inc(sem["state_turned"], 1)
                pe.wait_ge(sem["state_ready"], 2)
                for n in range(START["z"], START["merge0"]):
                    wide_chunk(n, u_hi, u_lo, ready=split_ready("u_mix") if n == START["z"] else None)
                pe.wait_ge(sem["evac"], EVAC["misc"] + 1)
                for b in range(4):
                    for i in range(4):
                        last = pe.transpose(bank[TAIL_BANK[b]][0:70, P * i:P * (i + 1)], xbc[:, 4 * b + i, 256:326],
                                            ident[:])
                    last.then_inc(sem["tail_turned"], 1)
                pe.wait_ge(sem["decay_done"], 3)
                pe.wait_ge(sem["dt_done"], 1)
                for t, (t0, t1, n) in enumerate(TILES):
                    last = pe.transpose(bank[6][0:n, P * t:P * (t + 1)], head_rows[:, t0:t1], ident[:])
                last.then_inc(sem["rows_cols_turned"], 1)
                pe.wait_ge(sem["conv_done"], CT)
                pe.wait_ge(sem["tail_copied"], 4)
                for t, (t0, t1, n) in enumerate(TILES):
                    for b in range(2):
                        for i in range(4):
                            last = pe.transpose(bank[2 * t + b][0:n, P * i:P * (i + 1)], xbc[:, 4 * b + i, t0:t1],
                                                ident[:])
                        last.then_inc(sem["xs_turned"], 1)
                for t, (t0, t1, n) in enumerate(TILES):
                    pe.wait_ge(sem["xdt_ready"], min(6, t + 1))
                    for g in range(GROUPS):
                        last = pe.transpose(bank[t][0:n, P * g:P * (g + 1)], xbc[:, 8 + g, t0:t1], ident[:])
                    last.then_inc(sem["b_turned"], 1)
                pe.wait_ge(sem["xdt_ready"], 6)
                pe.wait_ge(sem["head_cols_ready"], 1)
                for g in range(GROUPS):
                    for t, (t0, t1, n) in enumerate(TILES):
                        last = pe.matmul(bank[3 + g][0:n, t0:t1], xbc[:, 8 + g, t0:t1], xbc[:, 12 + g, t0:t1],
                                         start=True, stop=True)
                    last.then_inc(sem["cb_ready"], 1)

                def state_delta(t):
                    n = TILES[t][2]
                    pe.wait_ge(sem["xdec_ready"], t + 1)
                    for g in range(GROUPS):
                        last = pe.matmul(bank[4 + g // 2][:, 256 * (g % 2):256 * (g % 2) + 256],
                                         b_rows[0:n, t, P * g:P * (g + 1)], xdec[0:n, 256 * g:256 * (g + 1)],
                                         start=True, stop=True)
                    last.then_inc(sem["delta_ready"], 1)

                pe.wait_ge(sem["b_ready"], 3)
                pe.wait_ge(sem["cb_masked"], 4)
                state_delta(0)

                def head_row(h):
                    if h >= 2:
                        pe.wait_ge(sem["row_exp_ready"], h - 1)
                        pe.wait_ge(sem["seg_ready"], h - 1)
                    pe.matmul(bank[h % 2][:, 0:TOK], ident[0:HEADS, h:h + 1].broadcast_to([HEADS, P]),
                              head_rows[0:HEADS, :], start=True, stop=True).then_inc(sem["bc_ready"], 1)

                pe.wait_ge(sem["b_ready"], 3)
                head_row(0)
                pe.wait_ge(sem["h1_ready"], 2)
                for h in range(HEADS):
                    if h + 1 < HEADS:
                        head_row(h + 1)
                    pe.wait_ge(sem["mt_ready"], h + 1)
                    i, r0 = h // 2, 64 * (h % 2)
                    if i >= 2:
                        pe.wait_ge(sem["mixed"], i - 1)
                    out = bank[2 + i % 2]
                    f = slice(64 * h, 64 * h + 64)
                    pe.matmul(out[r0:r0 + 64, 0:128], xdt[:, 0, f], seg[:, h % 2, 0:128], start=True, stop=True)
                    pe.matmul(out[r0:r0 + 64, 128:256], xdt[:, 1, f], seg[:, h % 2, 128:256], start=True, stop=False)
                    pe.matmul(out[r0:r0 + 64, 128:256], h_prompt[:, f], row_exp[:, h % 2, 128:256], start=False,
                              stop=True)
                    pe.matmul(out[r0:r0 + 64, 256:320], xdt[0:DEC, 2, f], seg[0:DEC, h % 2, 256:320], start=True,
                              stop=False)
                    pe.matmul(out[r0:r0 + 64, 256:320], h_sample[:, f], row_exp[:, h % 2, 256:320], start=False,
                              stop=True).then_inc(sem["head_done"], 1)
                for t in (1, 2):
                    if t == 2:
                        pe.wait_ge(sem["h_final"], 1)
                    state_delta(t)
                pe.wait_ge(sem["h_final"], 2)
                pe.wait_ge(sem["mixed"], KT)
                for b in range(4):
                    src = h_prompt if b < 2 else h_sample
                    for i in range(4):
                        at = 512 * (b % 2) + P * i
                        last = pe.transpose(bank[b][:, P * i:P * (i + 1)], src[:, at:at + P], ident[:])
                    last.then_inc(sem["h_turned"], 1)
                pe.wait_ge(sem["h_rows_ready"], 4)
                norm("ssm")

                def merge(b, wait):
                    n0 = START[f"merge{b}"]
                    for c in range(4):
                        wide_chunk(n0 + 2 * c, u_hi, u_lo)
                        wide_chunk(n0 + 2 * c + 1, br_hi, br_lo, ready=wait if c == 0 else None)

                pe.wait_ge(sem["split_lo"], SPLITS["ssm"] + KT)
                merge(0, None)

                for name, cnt in (("qi", 1), ("kb", 1)):
                    wide_chunk(START[name], u_hi, u_lo)
                token_chunk(START["vb"])
                for c in range(4):
                    wide_chunk(START["qb"] + c, u_hi, u_lo)
                pe.wait_ge(sem["evac"], EVAC["qb"] + 4)
                pe.wait_ge(sem["k_past_loaded"], 48)
                for i in range(3):
                    last = pe.transpose(bank[3][:, P * i:P * (i + 1)], k_b_past[:, P * i:P * (i + 1)], ident[:])
                last.then_inc(sem["past_turned"], 1)
                for t, (t0, t1, n) in enumerate(TILES):
                    for i in range(2):
                        pe.transpose(bank[t][0:n, P * i:P * (i + 1)], k_b[:, i, t0:t1], ident[:])
                    pe.transpose(bank[t][0:n, 256:320], ki[0:64, t0:t1], ident[0:64, 0:64])\
                        .then_inc(sem["k_turned"], 1)

                def scores(q, qp, k, k_past, wide, narrow):
                    pe.matmul(wide[:, 0:128], q[qp, 0:128], k[qp, 0:128], start=True, stop=True)
                    pe.matmul(wide[:, 128:384], q[qp, 128:256], k[qp, 0:256], start=True, stop=True)
                    pe.matmul(narrow[0:DEC, 0:128], q[qp, 256:320], k_past[qp, :], start=True, stop=True)
                    return pe.matmul(narrow[0:DEC, 128:192], q[qp, 256:320], k[qp, 256:320], start=True, stop=True)

                pe.wait_ge(sem["past_ready"], 1)
                for h in range(4):
                    if h >= 2:
                        pe.wait_ge(sem["idx_relu"], h - 1)
                    qp = slice(64 * (h % 2), 64 * (h % 2) + 64)
                    scores(q_i[:, h // 2, :], qp, ki[:], k_b_past_t[:, 2, :], bank[4 + h % 2], bank[6 + h % 2])\
                        .then_inc(sem["idx_ready"], 1)

                def attention(first, n_heads, per_tile, q, k, k_past, v, v_past, d, q_per_kv):
                    def score_head(h):
                        c = first + h
                        if c >= 2:
                            pe.wait_ge(sem["shifted"], c - 1)
                        qp = slice(d * (h % per_tile), d * (h % per_tile) + d)
                        kt = h // q_per_kv // per_tile
                        scores(q[:, h // per_tile, :], qp, k[:, kt, :], k_past[:, kt, :], bank[c % 2],
                               bank[2 + c % 2]).then_inc(sem["scored"], 1)

                    score_head(0)
                    for h in range(n_heads):
                        c = first + h
                        if h + 1 < n_heads:
                            score_head(h + 1)
                        pe.wait_ge(sem["normed"], c + 1)
                        if c >= 2:
                            pe.wait_ge(sem["p_copied"], c - 1)
                        tb = bank[4 + c % 2]
                        for dst, r, k0 in ((0, 128, 0), (128, 128, 128), (256, 128, 256), (384, 64, 384), (448, 64, 448)):
                            last = pe.transpose(tb[:, dst:dst + r], logit[0:r, c % 2, k0:k0 + P], ident[0:r, 0:r])
                        last.then_inc(sem["p_turned"], 1)
                        tile = h // per_tile
                        all_tile = TILE0[first] + tile
                        if h % per_tile == 0 and tile >= 2:
                            pe.wait_ge(sem["attn_lo"], all_tile - 1)
                        pe.wait_ge(sem["p_copied"], c + 1)
                        r0 = d * (h % per_tile)
                        ob, pt = bank[6 + tile % 2][r0:r0 + d], prob_t[:, c % 2]
                        f = slice(d * (h // q_per_kv), d * (h // q_per_kv) + d)
                        pe.matmul(ob[:, 0:128], v[:, 0, f], pt[:, 0:128], start=True, stop=True)
                        pe.matmul(ob[:, 128:256], v[:, 0, f], pt[:, 128:256], start=True, stop=False)
                        pe.matmul(ob[:, 128:256], v[:, 1, f], pt[:, 256:384], start=False, stop=True)
                        pe.matmul(ob[:, 256:320], v_past[:, f], pt[:, 384:448], start=True, stop=False)
                        pe.matmul(ob[:, 256:320], v[64:128, 2, f], pt[64:128, 448:512], start=False, stop=True)\
                            .then_inc(sem["attended"], 1)

                pe.wait_ge(sem["k_rows_ready"], 3)
                pe.wait_ge(sem["idx_relu"], 4)
                pe.wait_ge(sem["v_past_loaded"], 16)
                attention(0, 8, 1, q_b, k_b, k_b_past_t, v_b, v_b_past, 128, 4)
                pe.wait_ge(sem["attn_lo"], 8)
                merge(1, None)
                pe.wait_ge(sem["k_past_loaded"], 64)
                for i in range(KT):
                    last = pe.transpose(bank[6 + i // 4][:, P * (i % 4):P * (i % 4 + 1)], k_c_rows[:, P * i:P * (i + 1)],
                                        ident[:])
                    if i % 4 == 3:
                        last.then_inc(sem["past_turned"], 1)
                for c in range(4):
                    wide_chunk(START["kc"] + c, u_hi, u_lo)
                for c in range(4):
                    token_chunk(START["vc"] + c)
                for c in range(4):
                    wide_chunk(START["qc"] + c, u_hi, u_lo)
                pe.wait_ge(sem["evac"], EVAC["qc"] + 4)
                for t, (t0, t1, n) in enumerate(TILES):
                    for b in range(2):
                        if t == 2:
                            pe.wait_ge(sem["k_rows_ready"], 3 + b + 1)
                        for i in range(4):
                            last = pe.transpose(bank[(2 * t + b) % 4][0:n, P * i:P * (i + 1)], k_c[:, 4 * b + i, t0:t1],
                                                ident[:])
                        last.then_inc(sem["k_turned"], 1)
                pe.wait_ge(sem["k_rows_ready"], 9)
                pe.wait_ge(sem["past_ready"], 3)
                pe.wait_ge(sem["v_past_loaded"], 32)
                attention(8, 16, 2, q_c, k_c, k_c_past_t, v_c, v_c_past, 64, 1)
                pe.wait_ge(sem["attn_lo"], 16)
                merge(2, None)
                for c in range(4):
                    wide_chunk(START["out"] + c, br_hi, br_lo, ready=split_ready("mix") if c == 0 else None)
                    if c >= 1:
                        square_sum("mix_post", 2 * c - 2)
                        square_sum("mix_post", 2 * c - 1)
                norm("mix_post", 6)
                ffn(1)
                norm("ple_pre")
                for c in range(4):
                    wide_chunk(START["ple"] + 2 * c, p_hi, p_lo, k_tiles=2)
                    wide_chunk(START["ple"] + 2 * c + 1, u_hi, u_lo, ready=split_ready("u_ple") if c == 0 else None)
                    if c >= 1:
                        square_sum("ple_post", 2 * c - 2)
                        square_sum("ple_post", 2 * c - 1)
                norm("ple_post", 6)

            @block.vector
            def _(dve):
                step = Chain(dve, sem["dve_step"])

                def norm_rows(name, scale=1.0):
                    i = NORM[name]
                    _, tiles, groups = NORMS[i]
                    w = 3 * groups
                    v, r, t = rs[:, 0, 0:w], rs[:, 1, 0:w], rs[:, 2, 0:w]
                    dve.wait_ge(sem["square_used"], KT * (i + 1))
                    step(dve.tensor_scalar(v, stat_bank[:, 0:w], groups / D, EPS, ALU.mult, ALU.add))
                    step(dve.tensor_scalar(r.bitcast(I32), v.bitcast(I32), -0.5, RSQRT_SEED, ALU.mult, ALU.add))
                    for _ in range(3):
                        step(dve.tensor_tensor(t, r, r, ALU.mult))
                        step(dve.scalar_tensor_tensor(out=t, in0=t, scalar=-0.5, in1=v, op0=ALU.mult, op1=ALU.mult))
                        step(dve.scalar_tensor_tensor(out=r, in0=t, scalar=1.5, in1=r, op0=ALU.add, op1=ALU.mult))
                    diagonals = diag if groups == 1 else diag_groups
                    for c in range(w):
                        last = dve.tensor_scalar(diagonals[:, c, :], ident[:], r[:, c:c + 1], scale, ALU.mult, ALU.mult)
                    last.then_inc(sem["diag_ready"], 1)
                    dve.wait_ge(sem["row_ready"], i + 1)

                def split_rest(q, dst_hi, dst_lo):
                    dve.wait_ge(sem["split_hi"], q + 1)
                    dve.tensor_tensor(dst_lo, split_tmp[:, q % RING, :], f32(dst_hi), ALU.subtract)\
                        .then_inc(sem["split_lo"], 1)

                def split_source(q, write):
                    if q >= RING:
                        dve.wait_ge(sem["split_lo"], q - RING + 1)
                    write(split_tmp[:, q % RING, :]).then_inc(sem["split_src"], 1)

                def norm_split(name, split, src, gain, hi, lo):
                    groups = NORMS[NORM[name]][2]
                    banks = ROW_BANKS[groups]
                    q0 = SPLITS[split]
                    norm_rows(name)
                    for k in range(KT + 1):
                        if k < KT:
                            row = bank[banks[k * groups // KT]][:, 0:TOK]
                            split_source(q0 + k, lambda dst: dve.scalar_tensor_tensor(
                                out=dst, in0=src[:, k, :], scalar=gain_cols[:, k, gain:gain + 1], in1=row,
                                op0=ALU.mult, op1=ALU.mult))
                        if k >= 1:
                            split_rest(q0 + k - 1, hi[:, k - 1, :], lo[:, k - 1, :])

                def add_normed(name, gain, scale):
                    norm_rows(name, scale)
                    for k in range(KT + 1):
                        if k < KT:
                            dve.scalar_tensor_tensor(out=y[:, k, :], in0=y[:, k, :],
                                                     scalar=gain_cols[:, k, gain:gain + 1], in1=bank[7][:, 0:TOK],
                                                     op0=ALU.mult, op1=ALU.mult).then_inc(sem["dve_step"], 1)
                            step.count += 1
                        if k >= 1:
                            dve.wait_ge(sem["dve_step"], step.count - (1 if k < KT else 0))
                            dve.tensor_tensor(x[:, k - 1, :], x[:, k - 1, :], y[:, k - 1, :], ALU.add)\
                                .then_inc(sem["x_ready"], 1)

                def up_chunk(which, j, loop=None):
                    n = START[f"up{which}"] + j
                    s, more = n % RING, 0 if loop is None else RING * loop
                    q = SPLITS[f"h{which}"] + j
                    tmp = split_tmp[:, q % RING, :]
                    dve.wait_ge(sem["tanh_ready"], FT * which + j + 1 + more)
                    dve.scalar_tensor_tensor(out=tmp, in0=th[:, s, :], scalar=1.0, in1=bank[2 * s][:, 0:TOK],
                                             op0=ALU.add, op1=ALU.mult).then_inc(sem["silu_ready"], 1)
                    dve.wait_ge(sem["silu_ready"], FT * which + j + 1 + more)
                    dve.scalar_tensor_tensor(out=tmp, in0=tmp, scalar=0.5, in1=bank[2 * s + 1][:, 0:TOK],
                                             op0=ALU.mult, op1=ALU.mult).then_inc(sem["split_src"], 1)
                    dve.wait_ge(sem["split_hi"], q + 1 + more)
                    if loop is None:
                        hi, lo = h_hi[:, j, :], h_lo[:, j, :]
                    else:
                        hi, lo = (h[:, bass.ds(loop * RING + j, 1), :].rearrange("p j t -> p (j t)")
                                  for h in (h_hi, h_lo))
                    dve.tensor_tensor(lo, tmp, f32(hi), ALU.subtract).then_inc(sem["split_lo"], 1)
                    dve.wait_ge(sem["split_lo"], q + 1 + more)
                    dve.sem_inc(bank_free[s], 1)

                def ffn(which):
                    norm_split(f"ffn{which}_pre", f"u_ffn{which}", x, 4 * which, u_hi, u_lo)
                    for j in range(RING):
                        up_chunk(which, j)
                    with dve.Fori(1, 6) as i:
                        for j in range(RING):
                            up_chunk(which, j, loop=i)
                    for j in range(6 * RING, FT):
                        up_chunk(which, j)
                    n1 = START[f"down{which}"]
                    for j in range(KT):
                        dve.wait_ge(sem["chunk_done"], n1 + 2 * j + 2)
                        s = (n1 + 2 * j) % RING
                        step(dve.tensor_copy(y[:, j, :], bank[2 * s][:, 0:TOK]))
                        dve.sem_inc(bank_free[s], 1)
                        dve.sem_inc(sem["y_ready"], 1)
                    add_normed(f"ffn{which}_post", 4 * which + 1, 0.5)

                def give_back(n):
                    dve.sem_inc(bank_free[n % RING], 1)

                def evacuate(n, writes):
                    s = n % RING
                    dve.wait_ge(sem["chunk_done"], n + 1)
                    for write in writes(bank[2 * s], bank[2 * s + 1]):
                        last = write
                    last.then_inc(sem["evac"], 1)
                    dve.wait_ge(sem["evac"], EVAC_OF[n] + 1)
                    give_back(n)

                dve.wait_ge(sem["rows_turned"], 1)
                cc = bank[6][:, 0:8 * CT].rearrange("p (i r) -> p i r", r=8)
                gc = bank[7][:, 0:12 * KT].rearrange("p (i r) -> p i r", r=12)
                dve.tensor_scalar(conv_cols[:, :, 0:5], cc[:, :, 0:5], 0.5, None, ALU.mult)
                dve.tensor_copy(conv_cols[:, :, 5:8], cc[:, :, 5:8])
                dve.tensor_copy(gain_cols[:, :, 0:9], gc[:, :, 0:9])
                step(dve.tensor_scalar(gain_cols[:, :, 9:12], gc[:, :, 9:12], 0.5, None, ALU.mult))
                for k in range(2):
                    dve.wait_ge(sem["p_ready"], k + 1)
                    last = dve.tensor_tensor(p_lo[:, k, :], bank[k][:, 0:TOK], f32(p_hi[:, k, :]), ALU.subtract)
                last.then_inc(sem["cols_ready"], 1)
                ffn(0)

                norm_split("mix_pre", "u_mix", x, 2, u_hi, u_lo)
                dve.memset(xbc[:, :, 0:3], 0.0)
                step(dve.tensor_copy(xbc[:, :, SEQ + 3:SEQ + 6], conv_cols[:, :, 5:8]))
                for c in range(4):
                    evacuate(START["z"] + c, lambda b0, b1: (
                        dve.tensor_scalar(z[:, 2 * c + half, :], b[:, 0:TOK], 0.5, None, ALU.mult)
                        for half, b in enumerate((b0, b1))))
                for c in range(8):
                    evacuate(START["xbc"] + c, lambda b0, b1: (
                        dve.tensor_copy(xbc[:, 2 * c + half, at:at + w], b[:, t0:t0 + w])
                        for half, b in enumerate((b0, b1)) for at, t0, w in ((3, 0, SEQ), (SEQ + 6, SEQ, DEC))))
                evacuate(START["misc"], lambda b0, b1: (
                    dve.tensor_copy(ki[:], b0[:, 0:TOK]),
                    dve.tensor_scalar(dt_tmp[:, 0, :], b1[0:HEADS, 0:TOK], dt_bias[:], None, ALU.add),
                    dve.tensor_scalar(head_rows[96:100, :], b1[32:36, 0:TOK], 0.5, None, ALU.mult)))
                dve.scalar_tensor_tensor(out=dt_tmp[:, 1, :], in0=dt_tmp[:, 0, :], scalar=-1.0, in1=dt_tmp[:, 0, :],
                                         op0=ALU.mult, op1=ALU.min).then_inc(sem["dt_v"], 1)
                for k in range(KT):
                    dve.wait_ge(sem["z_tanh"], k + 1)
                    dve.scalar_tensor_tensor(out=z[:, k, :], in0=conv_th[:, k % 2, 0:TOK], scalar=1.0, in1=z[:, k, :],
                                             op0=ALU.add, op1=ALU.mult).then_inc(sem["z_done"], 1)

                def conv_silu(i):
                    dve.wait_ge(sem["conv_tanh"], i + 1)
                    if i % 4 == 0:
                        dve.wait_ge(sem["tail_turned"], i // 4 + 1)
                    for out0, t0, w in ((0, 0, SEQ), (SEQ, SEQ + 3, DEC)):
                        last = dve.scalar_tensor_tensor(out=xbc[:, i, out0:out0 + w], in0=conv_th[:, i % 2, t0:t0 + w],
                                                        scalar=1.0, in1=conv_acc[:, i % 2, t0:t0 + w], op0=ALU.add,
                                                        op1=ALU.mult)
                    last.then_inc(sem["conv_done"], 1)

                for i in range(CT):
                    if i >= 2:
                        dve.wait_ge(sem["conv_done"], i - 1)
                    acc = conv_acc[:, i % 2, :]
                    step(dve.tensor_scalar(acc, xbc[:, i, 0:CONV_N], conv_cols[:, i, 0:1], conv_cols[:, i, 4:5],
                                           ALU.mult, ALU.add))
                    for k in range(1, 4):
                        ins = dve.scalar_tensor_tensor(out=acc, in0=xbc[:, i, k:k + CONV_N],
                                                       scalar=conv_cols[:, i, k:k + 1], in1=acc, op0=ALU.mult,
                                                       op1=ALU.add)
                        if k < 3:
                            step(ins)
                        else:
                            ins.then_inc(sem["conv_ready"], 1)
                    dve.wait_ge(sem["conv_ready"], i + 1)
                    if i >= 1:
                        conv_silu(i - 1)
                conv_silu(CT - 1)
                dve.wait_ge(sem["dt_exp"], 1)
                dt_rows = dt_tmp[:, 0, :]
                step(dve.scalar_tensor_tensor(out=dt_rows, in0=dt_rows, scalar=0.0, in1=dt_tmp[:, 1, :],
                                              op0=ALU.max, op1=ALU.add))
                dve.tensor_copy(head_rows[64:64 + HEADS, :], dt_rows)
                dve.memset(dt_tmp[:, 1, :], 1.0)
                step(dve.tensor_scalar(dt_tmp[:, 2, :], dt_rows, neg_a[:], -1.0, ALU.mult, ALU.mult))
                for t0, t1, _ in TILES:
                    last = dve.tensor_tensor_scan(head_rows[0:HEADS, t0:t1], dt_tmp[:, 1, t0:t1], dt_tmp[:, 2, t0:t1],
                                                  0.0, ALU.mult, ALU.add)
                last.then_inc(sem["dt_done"], 1)
                dve.wait_ge(sem["rows_cols_turned"], 1)
                dve.tensor_copy(head_cols[:, 0:2, :].rearrange("p t c -> p (t c)"), bank[6][:, 0:256])
                dve.tensor_copy(head_cols[0:DEC, 2, :], bank[6][0:DEC, 256:384]).then_inc(sem["head_cols_ready"], 1)
                dve.wait_ge(sem["head_cols_ready"], 1)
                dve.wait_ge(sem["tail_stored"], 32)
                for t, (_, _, n) in enumerate(TILES):
                    for b in range(2):
                        dve.wait_ge(sem["xs_turned"], 2 * t + b + 1)
                        dve.tensor_tensor(
                            xdt[0:n, t, 512 * b:512 * (b + 1)].rearrange("p (h d) -> p h d", d=64),
                            bank[2 * t + b][0:n, :].rearrange("p (h d) -> p h d", d=64),
                            head_cols[0:n, t, 64 + 8 * b:72 + 8 * b].unsqueeze(2).broadcast_to([n, 8, 64]), ALU.mult)\
                            .then_inc(sem["xdt_ready"], 1)
                for g in range(GROUPS):
                    dve.wait_ge(sem["cb_ready"], g + 1)
                    for t, (t0, t1, n) in enumerate(TILES):
                        last = dve.tensor_tensor(cb[0:n, g, t0:t1], bank[3 + g][0:n, t0:t1], tri[0:n, 0:n], ALU.mult)
                    last.then_inc(sem["cb_masked"], 1)

                def decayed(t):
                    n = TILES[t][2]
                    if t >= 1:
                        dve.wait_ge(sem["delta_ready"], t)
                    dve.tensor_tensor(xdec[0:n, :].rearrange("p (h d) -> p h d", d=64),
                                      xdt[0:n, t, :].rearrange("p (h d) -> p h d", d=64),
                                      head_cols[0:n, t, 32:32 + HEADS].unsqueeze(2).broadcast_to([n, HEADS, 64]),
                                      ALU.mult).then_inc(sem["xdec_ready"], 1)

                dve.wait_ge(sem["xdt_ready"], 6)
                decayed(0)

                def segments(h):
                    dve.wait_ge(sem["bc_ready"], h + 1)
                    if h >= 2:
                        dve.wait_ge(sem["head_done"], h - 1)
                    for t, (t0, t1, n) in enumerate(TILES):
                        last = dve.tensor_scalar(seg[0:n, h % 2, t0:t1], bank[h % 2][0:n, t0:t1],
                                                 head_cols[0:n, t, h:h + 1], 0.0, ALU.subtract, ALU.min)
                    last.then_inc(sem["seg_ready"], 1)

                def mix_tile(i):
                    dve.wait_ge(sem["head_done"], 2 * i + 2)
                    step(dve.scalar_tensor_tensor(out=th[:, 2, :], in0=xbc[:, i, 0:TOK], scalar=d_col[:, i:i + 1],
                                                  in1=bank[2 + i % 2][:, 0:TOK], op0=ALU.mult, op1=ALU.add))
                    dve.tensor_tensor(z[:, i, :], z[:, i, :], th[:, 2, :], ALU.mult).then_inc(sem["mixed"], 1)
                    dve.wait_ge(sem["mixed"], i + 1)

                dve.wait_ge(sem["conv_done"], CT)
                dve.wait_ge(sem["cb_masked"], 4)
                segments(0)
                for h in range(HEADS):
                    if h + 1 < HEADS:
                        segments(h + 1)
                    g = h // (HEADS // GROUPS)
                    dve.wait_ge(sem["seg_exp"], h + 1)
                    dve.tensor_tensor(seg[:, h % 2, 0:SEQ], seg[:, h % 2, 0:SEQ], cb[:, g, 0:SEQ], ALU.mult)
                    dve.tensor_tensor(seg[0:DEC, h % 2, SEQ:TOK], seg[0:DEC, h % 2, SEQ:TOK], cb[0:DEC, g, SEQ:TOK],
                                      ALU.mult)
                    dve.wait_ge(sem["row_exp_ready"], h + 1)
                    dve.tensor_tensor(row_exp[:, h % 2, 128:TOK], row_exp[:, h % 2, 128:TOK], xbc[:, 12 + g, 128:TOK],
                                      ALU.mult).then_inc(sem["mt_ready"], 1)
                    if h % 2 == 0 and h >= 2:
                        mix_tile(h // 2 - 1)
                mix_tile(KT - 1)
                dve.wait_ge(sem["head_done"], HEADS)
                for t, state in ((1, h_prompt), (2, h_sample)):
                    decayed(t)
                    dve.wait_ge(sem["delta_ready"], t + 1)
                    for h in range(HEADS):
                        f = slice(64 * h, 64 * h + 64)
                        last = dve.scalar_tensor_tensor(out=state[:, f], in0=state[:, f],
                                                        scalar=chunk_decay[:, h, t - 1:t],
                                                        in1=bank[4 + h // 8][:, 64 * (h % 8):64 * (h % 8) + 64],
                                                        op0=ALU.mult, op1=ALU.add)
                    last.then_inc(sem["h_final"], 1)
                norm_split("ssm", "ssm", z, 8, br_hi, br_lo)

                def merge(b):
                    for c in range(4):
                        n = START[f"merge{b}"] + 2 * c
                        dve.wait_ge(sem["gate_tanh"], 8 * b + 2 * c + 2)
                        give_back(n)
                        dve.wait_ge(sem["chunk_done"], n + 2)
                        s = (n + 1) % RING
                        for half in range(2):
                            g = 8 * b + 2 * c + half
                            k = 2 * c + half
                            out = y[:, k, :] if b == 0 else th[:, g % 2, :]
                            ins = dve.scalar_tensor_tensor(out=out, in0=th[:, g % 2, :], scalar=1.0,
                                                           in1=bank[2 * s + half][:, 0:TOK], op0=ALU.add,
                                                           op1=ALU.mult)
                            if b > 0:
                                step(ins)
                                ins = dve.tensor_tensor(y[:, k, :], y[:, k, :], th[:, g % 2, :], ALU.add)
                            ins.then_inc(sem["merged"], 1)
                        dve.wait_ge(sem["merged"], 8 * b + 2 * c + 2)
                        give_back(n + 1)

                merge(0)

                def copies(dst, k0, scale):
                    def writes(b0, b1):
                        for half, b in enumerate((b0, b1)):
                            if scale is None:
                                yield dve.tensor_copy(dst[:, k0 + half, :], b[:, 0:TOK])
                            else:
                                yield dve.tensor_scalar(dst[:, k0 + half, :], b[:, 0:TOK], scale, None, ALU.mult)
                    return writes

                def values(dst, c0):
                    def writes(b0, b1):
                        yield dve.tensor_copy(dst[:, 0:2, c0:c0 + 256], b0[:].rearrange("p (t c) -> p t c", c=256))
                        yield dve.tensor_copy(dst[:, 2, c0:c0 + 256], b1[:, 0:256])
                    return writes

                dve.wait_ge(sem["h_rows_ready"], 4)
                dve.wait_ge(sem["h_stored"], 32)
                evacuate(START["qi"], copies(q_i, 0, 0.125))
                evacuate(START["kb"], copies(k_b, 0, None))
                evacuate(START["vb"], values(v_b, 0))
                for c in range(4):
                    evacuate(START["qb"] + c, copies(q_b, 2 * c, -float(128) ** -0.5))
                for h in range(4):
                    dve.wait_ge(sem["idx_relu"], h + 1)
                    for j, (r, k0, k1) in enumerate(SPANS):
                        weight = head_cols[0:r, j, 96 + h:97 + h]
                        if h == 0:
                            last = dve.tensor_scalar(score[0:r, k0:k1], score_relu[0:r, 0, k0:k1], weight, None,
                                                     ALU.mult)
                        else:
                            last = dve.scalar_tensor_tensor(out=score[0:r, k0:k1], in0=score_relu[0:r, h % 2, k0:k1],
                                                            scalar=weight, in1=score[0:r, k0:k1], op0=ALU.mult,
                                                            op1=ALU.add)
                    last.then_inc(sem["idx_used"], 1)
                    dve.wait_ge(sem["idx_used"], h + 1)
                dve.memset(score[0:64, 64:128], -BIG)
                step(dve.memset(score[0:64, 320:384], -BIG))
                for r, k0, k1, rounds in ((128, 0, 128, 8), (128, 128, 384, 8), (64, 384, 576, 6)):
                    for _ in range(rounds):
                        step(dve.max(top8[0:r, :], score[0:r, k0:k1]))
                        step(dve.match_replace(score[0:r, k0:k1], top8[0:r, :], score[0:r, k0:k1], GONE))
                for r, k0, k1 in ((128, 0, 384), (64, 384, 576)):
                    last = dve.tensor_scalar(dsa_mask[0:r, k0:k1], score[0:r, k0:k1], GONE / 2, BIG, ALU.is_gt,
                                             ALU.mult)
                last.then_inc(sem["mask_ready"], 1)
                dve.wait_ge(sem["mask_ready"], 1)

                def shifted(c, bias_of):
                    dve.wait_ge(sem["scored"], c + 1)
                    if c >= 2:
                        dve.wait_ge(sem["p_turned"], c - 1)
                    for j, (r, k0, k1) in enumerate(SPANS):
                        src = bank[c % 2][:, k0:k1] if j < 2 else bank[2 + c % 2][0:r, 0:k1 - k0]
                        last = dve.tensor_tensor_reduce(out=logit[0:r, c % 2, k0:k1], in0=src, in1=bias_of(j, r, k0, k1),
                                                        scale=1.0, scalar=3e38, op0=ALU.add, op1=ALU.min,
                                                        accum_out=shift[0:r, c % 2, j:j + 1])
                    last.then_inc(sem["shifted"], 1)

                def attention(first, n_heads, per_tile, bias):
                    shifted(first, bias(0))
                    for h in range(n_heads):
                        c = first + h
                        if h + 1 < n_heads:
                            shifted(c + 1, bias(h + 1))
                        dve.wait_ge(sem["exped"], c + 1)
                        step(dve.reciprocal(denom[:, c % 2, :], denom[:, c % 2, :]))
                        for j, (r, k0, k1) in enumerate(SPANS):
                            last = dve.tensor_scalar(logit[0:r, c % 2, k0:k1], logit[0:r, c % 2, k0:k1],
                                                     denom[0:r, c % 2, j:j + 1], None, ALU.mult)
                        last.then_inc(sem["normed"], 1)
                        if h % per_tile == 0 and h >= per_tile:
                            attn_rest(first, h // per_tile - 1)
                    attn_rest(first, n_heads // per_tile - 1)

                def attn_rest(first, tile):
                    dve.wait_ge(sem["attn_hi"], TILE0[first] + tile + 1)
                    dve.tensor_tensor(br_lo[:, tile, :], bank[6 + tile % 2][:, 0:TOK], f32(br_hi[:, tile, :]),
                                      ALU.subtract).then_inc(sem["attn_lo"], 1)

                dve.wait_ge(sem["chunk_done"], START["merge1"])
                attention(0, 8, 1, lambda h: lambda j, r, k0, k1: dsa_mask[0:r, k0:k1])
                merge(1)
                dve.wait_ge(sem["attended"], 8)
                dve.wait_ge(sem["k_stored"], 64)
                dve.wait_ge(sem["v_stored"], 32)
                for c in range(4):
                    evacuate(START["kc"] + c, copies(k_c, 2 * c, None))
                for c in range(4):
                    evacuate(START["vc"] + c, values(v_c, 256 * c))
                for c in range(4):
                    evacuate(START["qc"] + c, copies(q_c, 2 * c, -0.125))

                def band(h):
                    at = (128, 0, 0)
                    dve.wait_ge(sem[f"bias_loaded{h % 2}"], 16 * (h // 2 + 1))
                    step(dve.memset(band_bias[0:64, h % 2, 192:256], BIG))
                    return lambda j, r, k0, k1: band_bias[0:r, h % 2, at[j]:at[j] + k1 - k0]

                attention(8, 16, 2, band)
                merge(2)
                for k in range(KT + 1):
                    q = SPLITS["mix"] + k
                    if k < KT:
                        split_source(q, lambda dst: dve.tensor_scalar(dst, y[:, k, :], 0.5, None, ALU.mult))
                    if k >= 1:
                        if k == 1:
                            dve.wait_ge(sem["chunk_done"], START["out"])
                        split_rest(q - 1, br_hi[:, k - 1, :], br_lo[:, k - 1, :])
                for c in range(4):
                    n = START["out"] + c
                    dve.wait_ge(sem["chunk_done"], n + 1)
                    for half in range(2):
                        last = dve.tensor_copy(y[:, 2 * c + half, :], bank[2 * (n % RING) + half][:, 0:TOK])
                        last.then_inc(sem["y_ready"], 1)
                    dve.wait_ge(sem["y_ready"], YR["mix_post"] + 2 * c + 2)
                    give_back(n)
                add_normed("mix_post", 3, 1.0)
                ffn(1)
                norm_split("ple_pre", "u_ple", x, 6, u_hi, u_lo)
                for c in range(4):
                    n = START["ple"] + 2 * c
                    evacuate(n, copies(y, 2 * c, 0.5))
                    s = (n + 1) % RING
                    for half in range(2):
                        k, g = 2 * c + half, 24 + 2 * c + half
                        dve.wait_ge(sem["gate_tanh"], g + 1)
                        step(dve.scalar_tensor_tensor(out=y[:, k, :], in0=th[:, g % 2, :], scalar=1.0, in1=y[:, k, :],
                                                      op0=ALU.add, op1=ALU.mult))
                        dve.sem_inc(sem["merged"], 1)
                        dve.sem_inc(sem["y_ready"], 1)
                    give_back(n + 1)
                add_normed("ple_post", 7, 1.0)

        SIZE = {"up": SLOT, "down": HALF_FT * P, "in": SLOT, "misc": SLOT, "gate": SLOT, "branch": SLOT, "out": SLOT,
                "ple": 512, "plegate": SLOT}
        XR = {"ffn0": 0, "mix": 0, "ffn1": 8, "ple": 16}
        YR = {"ffn0_post": 0, "mix_post": 8, "ffn1_post": 16, "ple_post": 24}
        EVAC_ORDER = [n for name, cnt in (("z", 4), ("xbc", 8), ("misc", 1), ("qi", 1), ("kb", 1), ("vb", 1), ("qb", 4),
                                          ("kc", 4), ("vc", 4), ("qc", 4)) for n in range(START[name], START[name] + cnt)]
        EVAC_ORDER += [START["ple"] + 2 * c for c in range(4)]
        EVAC_OF = {n: i for i, n in enumerate(EVAC_ORDER)}
        EVAC = {name: EVAC_OF[START[name]] for name in ("z", "xbc", "misc", "qi", "kb", "vb", "qb", "kc", "vc", "qc")}
        TAIL_BANK = [0, 1, 2, 3]
        SPANS = ((128, 0, 128), (128, 128, 384), (64, 384, 576))
        TILE0 = {0: 0, 8: 8}

        with nc.Fori(0, DEPTH) as layer:
            with nc.Block() as block:
                layer_body(layer, block)
            nc.all_engine_barrier(sems_to_clear=every)

        with nc.Block() as block:
            @block.tensor
            def _(pe):
                for t, (t0, t1, n) in enumerate(TILES):
                    for b in range(2):
                        for i in range(4):
                            last = pe.transpose(bank[2 * t + b][0:n, P * i:P * (i + 1)], x[:, 4 * b + i, t0:t1],
                                                ident[:])
                        last.then_inc(sem["y_turned"], 1)

            @block.vector
            def _(dve):
                for t, (_, _, n) in enumerate(TILES):
                    for b in range(2):
                        dve.wait_ge(sem["y_turned"], 2 * t + b + 1)
                        dve.tensor_copy(io_rows[0:n, t, 512 * b:512 * (b + 1)], bank[2 * t + b][0:n, :])\
                            .then_inc(sem["y_rows_ready"], 1)

            @block.sync
            def _(sp):
                for t, (_, _, n) in enumerate(TILES):
                    sp.wait_ge(sem["y_rows_ready"], 2 * t + 2)
                    dst = y_p[0, P * t:P * (t + 1)] if t < 2 else y_s[0]
                    sp.dma_start(dst, io_rows[0:n, t, :]).then_inc(sem["y_stored"], 16)
                sp.wait_ge(sem["y_stored"], 48)


INPUTS = ["x_prompt", "x_sample", "p_prompt", "p_sample", "cache_dsa_k", "cache_dsa_v", "cache_idx_k",
          "cache_band_k", "cache_band_v", "state_ssm", "state_conv", "norm_g", "ffn_w13", "ffn_w2", "w_in", "conv_w",
          "conv_b", "dt_bias", "a_log", "d_skip", "ssm_norm_g", "rel_bias", "w_gate", "b_gate", "w_branch", "w_out",
          "w_ple", "w_ple_gate"]
OUTPUTS = [
    ("y_prompt", (1, SEQ, D), (1, SEQ, D)), ("y_sample", (1, DEC, D), (1, DEC, D)),
    ("dsa_k_p", (DEPTH, 1, SEQ, 256), (DEPTH, 1, SEQ, 2, 128)), ("dsa_v_p", (DEPTH, 1, SEQ, 256), (DEPTH, 1, SEQ, 2, 128)),
    ("idx_k_p", (DEPTH, 1, SEQ, 64), (DEPTH, 1, SEQ, 64)),
    ("band_k_p", (DEPTH, 1, SEQ, D), (DEPTH, 1, SEQ, 16, 64)), ("band_v_p", (DEPTH, 1, SEQ, D), (DEPTH, 1, SEQ, 16, 64)),
    ("ssm_p", (DEPTH, 1, 16, 64, 128), (DEPTH, 1, 16, 64, 128)), ("conv_p", (DEPTH, 1, 3, CONV_CH), (DEPTH, 1, 3, CONV_CH)),
    ("dsa_k_s", (DEPTH, 1, DEC, 256), (DEPTH, 1, DEC, 2, 128)), ("dsa_v_s", (DEPTH, 1, DEC, 256), (DEPTH, 1, DEC, 2, 128)),
    ("idx_k_s", (DEPTH, 1, DEC, 64), (DEPTH, 1, DEC, 64)),
    ("band_k_s", (DEPTH, 1, DEC, D), (DEPTH, 1, DEC, 16, 64)), ("band_v_s", (DEPTH, 1, DEC, D), (DEPTH, 1, DEC, 16, 64)),
    ("ssm_s", (DEPTH, 1, 16, 64, 128), (DEPTH, 1, 16, 64, 128)), ("conv_s", (DEPTH, 1, 3, CONV_CH), (DEPTH, 1, 3, CONV_CH)),
]


def kernel(**inputs):
    import concourse.bacc as bacc
    from concourse.bass_utils import run_bass_kernel_spmd

    nc = bacc.Bacc("TRN2", target_bir_lowering=False, num_devices=1)
    arrays, aps = {}, {}
    for name in INPUTS:
        array = np.ascontiguousarray(inputs[name])
        arrays[f"in_{name}"] = array
        aps[name] = nc.dram_tensor(f"in_{name}", array.shape, mybir.dt.from_np(array.dtype), kind="ExternalInput").ap()
    outs = [nc.dram_tensor(f"out_{name}", shape, F32, kind="ExternalOutput").ap() for name, shape, _ in OUTPUTS]
    bias_line = nc.dram_tensor("bias_line", (HEADS, 512), F32).ap()
    bias_square = nc.dram_tensor("bias_square", (HEADS, P, 256), F32).ap()
    build(nc, aps, outs, bias_line, bias_square)
    r = run_bass_kernel_spmd(nc, [arrays], core_ids=[0])
    return tuple(r.results[0][f"out_{name}"].reshape(final) for name, _, final in OUTPUTS)
```

```python
from contextlib import ExitStack

import numpy as np
import concourse.bass as bass
from concourse import mybir

F32 = mybir.dt.float32
F32R = mybir.dt.float32r
I32 = mybir.dt.int32
ALU = mybir.AluOpType
ACT = mybir.ActivationFunctionType

P = 128
DEPTH, SEQ, DEC, PAST, D = 2, 256, 64, 128, 1024
TOK = SEQ + DEC
KT = D // P
D_FF = 2816
FT = D_FF // P
HALF_FT = FT // 2
PLE = 256
CONV_CH = 2048
CT = CONV_CH // P
HEADS = 16
D_STATE = 128
GROUPS = 4
IN_W = 8020
Z0, XBC0, DT0, QB0, KB0, VB0, QI0, KI0, WI0, QC0, KC0, VC0 = (
    0, 1024, 3072, 3088, 4112, 4368, 4624, 4880, 4944, 4948, 5972, 6996)
XP = SEQ + 3 + DEC + 3
CONV_N = XP - 3
RING = 3
SLOT = 2048
EPS = 1e-6
BIG = 1e30
GONE = -3e38
RSQRT_SEED = 1597463007.0
TILES = ((0, 128, 128), (128, 256, 128), (256, 320, 64))
STAT_TILES = (0, 128, 192)


def f32(ap):
    return ap.bitcast(F32)


def plan_chunks():
    chunks, start = [], {}

    def section(name, items):
        start[name] = len(chunks)
        chunks.extend(items)

    def ffn(which):
        section(f"up{which}", [("up", which, j) for j in range(FT)])
        section(f"down{which}", [("down", which, j, half) for j in range(KT) for half in range(2)])

    ffn(0)
    section("misc", [("misc",)])
    section("xbc", [("in", XBC0 + 256 * c) for c in range(8)])
    section("z", [("in", Z0 + 256 * c) for c in range(4)])
    section("gate0", [("gate", 0, c) for c in range(2)])
    section("qi", [("in", QI0)])
    section("kb", [("in", KB0)])
    section("qb", [("in", QB0 + 256 * c) for c in range(4)])
    section("gate0b", [("gate", 0, c) for c in (2, 3)])
    section("branch0", [("branch", 0, c) for c in range(4)])
    section("vb", [("in", VB0)])
    section("gate1", [("gate", 1, c) for c in range(4)])
    section("branch1", [("branch", 1, c) for c in range(4)])
    section("kc", [("in", KC0 + 256 * c) for c in range(4)])
    section("vc", [("in", VC0 + 256 * c) for c in range(4)])
    section("qc", [("in", QC0 + 256 * c) for c in range(4)])
    section("gate2", [("gate", 2, c) for c in range(4)])
    section("branch2", [("branch", 2, c) for c in range(4)])
    section("out", [("out", c) for c in range(4)])
    ffn(1)
    section("ple", [(kind, c) for c in range(4) for kind in ("ple", "plegate")])
    return chunks, start


CHUNKS, START = plan_chunks()
N_CHUNKS = len(CHUNKS)


def loads_of(n):
    return {"up": 2, "misc": 5}.get(CHUNKS[n][0], 1)


def loaded_count(n):
    return 16 * sum(loads_of(m) for m in range(n % RING, n + 1, RING))


def pair_of(n):
    if CHUNKS[n][0] in ("up", "down"):
        return n % RING
    if START["gate0"] <= n < START["branch0"] or START["vb"] <= n < START["branch1"] \
            or START["gate2"] <= n < START["branch2"]:
        return 0
    return n % 2


def frees(n):
    return not (CHUNKS[n][0] == "down" and CHUNKS[n][3] == 1)


def freed_before(n):
    return sum(frees(m) for m in range(n) if pair_of(m) == pair_of(n))


def build(nc, a, outs, bias_line, bias_square):
    (y_p, y_s, dsa_k_p, dsa_v_p, idx_k_p, band_k_p, band_v_p, ssm_p, conv_p,
     dsa_k_s, dsa_v_s, idx_k_s, band_k_s, band_v_s, ssm_s, conv_s) = outs
    with ExitStack() as ctx:
        def sb(name, shape, dt=F32, stack=ctx):
            return stack.enter_context(nc.sbuf_tensor(name, shape, dt))

        bank = [ctx.enter_context(nc.psum_tensor(f"bank{i}", [P, 512], F32)) for i in range(8)]
        stat_bank, row_bank = bank[6], bank[7]

        stage = sb("stage", [P, RING, SLOT])
        w_hi = sb("w_hi", [P, RING, SLOT], F32R)
        w_lo = sb("w_lo", [P, RING, SLOT], F32R)
        x = sb("x", [P, KT, TOK])
        y = sb("y", [P, KT, TOK])
        u_hi = sb("u_hi", [P, KT, TOK], F32R)
        u_lo = sb("u_lo", [P, KT, TOK], F32R)
        ident = sb("ident", [P, P])
        ones = sb("ones", [P, P])
        tri = sb("tri", [P, P])
        conv_cols = sb("conv_cols", [P, CT, 8])
        gain_cols = sb("gain_cols", [P, KT, 12])
        head_rows = sb("head_rows", [P, TOK])
        head_cols = sb("head_cols", [P, 3, P])
        d_col = sb("d_col", [P, KT])
        dt_bias = sb("dt_bias", [HEADS, 1])
        neg_a = sb("neg_a", [HEADS, 1])
        square = sb("square", [P, 2, TOK])
        split_tmp = sb("split_tmp", [P, RING, TOK])
        rs = sb("rs", [P, 5, 12])
        diag = sb("diag", [P, 3, P])
        shift = sb("shift", [P, 2, 3])
        denom = sb("denom", [P, 2, 3])
        chunk_decay = sb("chunk_decay", [P, HEADS, 2])

        with ExitStack() as region:
            h_hi = sb("h_hi", [P, FT, TOK], F32R, region)
            h_lo = sb("h_lo", [P, FT, TOK], F32R, region)
            th = sb("th", [P, RING, TOK], F32, region)
            p_rows = sb("p_rows", [P, 3, PLE], F32, region)
            p_hi = sb("p_hi", [P, 2, TOK], F32R, region)
            p_lo = sb("p_lo", [P, 2, TOK], F32R, region)
        with ExitStack() as region:
            conv_rows = sb("conv_rows", [8, CONV_CH], F32, region)
            gain_rows = sb("gain_rows", [12, D], F32, region)
            bias_rows = sb("bias_rows", [P, 4, HEADS], F32, region)
            bias_rev = sb("bias_rev", [HEADS, 512], F32, region)
        with ExitStack() as region:
            io_rows = sb("io_rows", [P, 3, D], F32, region)
        with ExitStack() as region:
            ki = sb("ki", [P, TOK], F32, region)
            with ExitStack() as over:
                br_hi = sb("br_hi", [P, KT, TOK], F32R, over)
                br_lo = sb("br_lo", [P, KT, TOK], F32R, over)
                band_bias = sb("band_bias", [P, 2, 256], F32, over)
            with ExitStack() as mamba:
                conv_tail = sb("conv_tail", [70, CONV_CH], F32, mamba)
            xdt = sb("xdt", [P, 3, D], F32, region)
            b_rows = sb("b_rows", [P, 3, GROUPS * D_STATE], F32, region)
            xdec = sb("xdec", [P, D], F32, region)
            with ExitStack() as mamba:
                z = sb("z", [P, KT, TOK], F32, mamba)
                xbc = sb("xbc", [P, CT, XP], F32, mamba)
                h_sample = sb("h_sample", [P, D], F32, mamba)
                with ExitStack() as early:
                    state_rows = sb("state_rows", [P, KT, P], F32, early)
                with ExitStack() as early:
                    conv_acc = sb("conv_acc", [P, 2, CONV_N], F32, early)
                    conv_th = sb("conv_th", [P, 2, CONV_N], F32, early)
                    dt_tmp = sb("dt_tmp", [HEADS, 3, TOK], F32, early)
                h_prompt = sb("h_prompt", [P, D], F32, mamba)
                with ExitStack() as late:
                    diag_groups = sb("diag_groups", [P, 9, P], F32, late)
                row_exp = sb("row_exp", [P, 2, TOK], F32, mamba)
                seg = sb("seg", [P, 2, TOK], F32, mamba)
                cb = xbc[:, CT - 2 * GROUPS:CT - GROUPS, :]
                h_rows = cb[:, :, 0:2 * P]
                q_b = sb("q_b", [P, KT, TOK], F32, mamba)
                k_b = sb("k_b", [P, 2, TOK], F32, mamba)
                q_i = sb("q_i", [P, 2, TOK], F32, mamba)
            attn = region.enter_context(ExitStack())
            logit = sb("logit", [P, 2, 576], F32, attn)
            prob_t = sb("prob_t", [P, 2, 512], F32, attn)
            gates = sb("gates", [P, KT, TOK], F32, attn)
            k_c_rows = prob_t[:].rearrange("p c k -> p (c k)")
            with ExitStack() as dsa:
                v_b = sb("v_b", [P, 3, 256], F32, dsa)
                v_b_past = sb("v_b_past", [P, 256], F32, dsa)
                k_b_past = sb("k_b_past", [P, 384], F32, dsa)
                k_b_past_t = sb("k_b_past_t", [P, 3, PAST], F32, dsa)
                k_b_rows = sb("k_b_rows", [P, 3, 320], F32, dsa)
                score = sb("score", [P, 576], F32, dsa)
                score_relu = sb("score_relu", [P, 2, 576], F32, dsa)
                top8 = sb("top8", [P, 8], F32, dsa)
                dsa_mask = sb("dsa_mask", [P, 576], F32, dsa)
            with ExitStack() as band:
                q_c = sb("q_c", [P, KT, TOK], F32, band)
                k_c = sb("k_c", [P, KT, TOK], F32, band)
                v_c = sb("v_c", [P, 3, D], F32, band)
                v_c_past = sb("v_c_past", [P, D], F32, band)
                k_c_past_t = sb("k_c_past_t", [P, KT, PAST], F32, band)

        names = (
            ["loaded0", "loaded1", "loaded2", "w_hi_ready", "w_lo_ready", "chunk_done", "bank_free0", "bank_free1",
             "bank_free2", "rows_loaded", "p_loaded", "per_layer_turned", "rows_turned", "cols_ready", "p_ready", "bias_rev_ready", "bias_written", "bias_squared",
             "square_ready", "square_used", "stat_ready", "diag_ready", "row_ready", "split_src", "split_hi",
             "split_lo", "tanh_ready", "silu_ready", "x_ready", "y_ready", "dve_step", "act_step", "pool_step",
             "evac", "z_tanh", "z_done", "tail_turned", "tail_copied", "tail_stored", "conv_base", "conv_ready", "conv_tanh",
             "conv_done", "dt_v", "dt_exp", "dt_done", "decay_done", "rows_cols_turned", "head_cols_ready",
             "state_loaded", "state_turned", "state_ready", "xs_turned", "xdt_ready", "b_turned", "b_ready",
             "cb_ready", "cb_masked", "xdec_ready", "delta_ready", "h1_ready", "bc_ready", "row_exp_ready",
             "seg_ready", "seg_exp", "mt_ready", "head_done", "mixed", "h_final", "h_turned", "h_rows_ready",
             "h_stored", "k_past_loaded", "v_past_loaded", "past_turned", "past_ready", "k_turned",
             "k_rows_ready", "k_stored", "v_stored", "idx_ready", "idx_relu", "idx_used", "mask_ready",
             "scored", "shifted", "exped", "normed", "p_turned", "p_copied", "attended", "attn_hi", "attn_lo",
             "bias_loaded0", "bias_loaded1", "bias_masked", "gate_tanh", "merged", "x_loaded", "x_turned", "y_turned", "y_rows_ready",
             "y_stored", "setup"])
        sem = {name: ctx.enter_context(nc.semaphore(name)) for name in names}
        every = range(min(s.num for s in sem.values()), max(s.num for s in sem.values()) + 1)
        assert len(every) == len(names)
        loaded = [sem[f"loaded{s}"] for s in range(RING)]
        bank_free = [sem[f"bank_free{s}"] for s in range(RING)]

        def diagonal(c):
            return diag[:, c, :] if c < 3 else diag_groups[:, c - 3, :]

        class Chain:

            def __init__(self, engine, semaphore):
                self.engine, self.semaphore, self.count = engine, semaphore, 0

            def __call__(self, instruction):
                self.count += 1
                instruction.then_inc(self.semaphore, 1)
                self.engine.wait_ge(self.semaphore, self.count)

        with nc.Block() as block:
            @block.sync
            def _(sp):
                sp.dma_start(io_rows[:, 0:2, :], a["x_prompt"][0].rearrange("(t p) d -> p t d", p=P))\
                    .then_inc(sem["x_loaded"], 16)
                sp.dma_start(io_rows[0:DEC, 2, :], a["x_sample"][0]).then_inc(sem["x_loaded"], 16)

            @block.gpsimd
            def _(pool):
                pool.memset(ident[:], 0.0).then_inc(sem["pool_step"], 1)
                pool.memset(ones[:], 1.0).then_inc(sem["pool_step"], 1)
                pool.memset(tri[:], 1.0).then_inc(sem["pool_step"], 1)
                pool.memset(head_rows[:], 0.0).then_inc(sem["pool_step"], 1)
                pool.memset(shift[:], 0.0).then_inc(sem["pool_step"], 1)
                pool.memset(denom[:], 1.0).then_inc(sem["pool_step"], 1)
                pool.wait_ge(sem["pool_step"], 3)
                pool.affine_select(out=ident[:], in_=ident[:], compare_op=ALU.not_equal, fill=1.0, base=0,
                                   pattern=[[-1, P]], channel_multiplier=1).then_inc(sem["setup"], 1)
                pool.affine_select(out=tri[:], in_=tri[:], compare_op=ALU.is_ge, fill=0.0, base=0,
                                   pattern=[[1, P]], channel_multiplier=-1).then_inc(sem["setup"], 1)

            @block.tensor
            def _(pe):
                pe.wait_ge(sem["setup"], 1)
                pe.wait_ge(sem["x_loaded"], 32)
                for k in range(KT):
                    for t, (t0, t1, n) in enumerate(TILES):
                        last = pe.transpose(bank[k][:, t0:t1], io_rows[0:n, t, P * k:P * (k + 1)], ident[0:n, 0:n])
                    last.then_inc(sem["x_turned"], 1)

            @block.vector
            def _(dve):
                for k in range(KT):
                    dve.wait_ge(sem["x_turned"], k + 1)
                    dve.tensor_copy(x[:, k, :], bank[k][:, 0:TOK]).then_inc(sem["dve_step"], 1)

        nc.all_engine_barrier(sems_to_clear=every)

        NORMS = [("ffn0_pre", 8, 1), ("ffn0_post", 8, 1), ("mix_pre", 8, 1), ("ssm", 8, 4), ("mix_post", 8, 1),
                 ("ffn1_pre", 8, 1), ("ffn1_post", 8, 1), ("ple_pre", 8, 1), ("ple_post", 8, 1)]
        NORM = {name: i for i, (name, _, _) in enumerate(NORMS)}
        ROW_BANKS = {1: [7], 4: [2, 3, 4, 5]}
        SPLITS = {}
        count = 0
        for name, n in (("u_ffn0", KT), ("h0", FT), ("u_mix", KT), ("ssm", KT), ("mix", KT), ("u_ffn1", KT),
                        ("h1", FT), ("u_ple", KT)):
            SPLITS[name] = count
            count += n

        def layer_body(layer, block):
            @block.sync
            def _(sp):
                def load_chunk(n, up_tile=None, loop=None):
                    kind, s = CHUNKS[n], n % RING
                    if loop is not None:
                        j = up_tile
                        src = a["ffn_w13"][layer, kind[1]].rearrange("(k p) (h j c) -> p k h j c", p=P, h=2, c=P)
                        parts = [(stage[:, s, 0:SLOT].rearrange("p (k h c) -> p k h c", h=2, c=P)[:, :, h, :],
                                  src[:, :, h, bass.ds(j, 1), :].rearrange("p k j c -> p k (j c)"))
                                 for h in range(2)]
                        sp.wait_ge(sem["w_lo_ready"], n - RING + 1 + RING * loop)
                        for dst, src_part in parts:
                            sp.dma_start(dst, src_part).then_inc(loaded[s], 16)
                        return
                    if n >= RING:
                        sp.wait_ge(sem["w_lo_ready"], n - RING + 1)
                    cols = stage[:, s, 0:SLOT].rearrange("p (k c) -> p k c", c=256)
                    if kind[0] == "up":
                        src = a["ffn_w13"][layer, kind[1]].rearrange("(k p) (h j c) -> p k h j c", p=P, h=2, c=P)
                        dst = stage[:, s, 0:SLOT].rearrange("p (k h c) -> p k h c", h=2, c=P)
                        for h in range(2):
                            sp.dma_start(dst[:, :, h, :], src[:, :, h, kind[2], :]).then_inc(loaded[s], 16)
                    elif kind[0] == "down":
                        src = a["ffn_w2"][layer, kind[1]].rearrange("(k p) (j c) -> p k j c", p=P, c=P)
                        sp.dma_start(stage[:, s, 0:HALF_FT * P].rearrange("p (k c) -> p k c", c=P),
                                     src[:, HALF_FT * kind[3]:HALF_FT * (kind[3] + 1), kind[2], :])\
                            .then_inc(loaded[s], 16)
                    elif kind[0] == "misc":
                        src = a["w_in"][layer].rearrange("(k p) c -> p k c", p=P)
                        for dst, c, w in ((0, KI0, 64), (64, KI0, 64), (128, DT0, 32), (160, WI0, 32), (192, DT0, 64)):
                            sp.dma_start(cols[:, :, dst:dst + w], src[:, :, c:c + w]).then_inc(loaded[s], 16)
                    elif kind[0] == "ple":
                        src = a["w_ple"][layer].rearrange("(k p) (j c) -> p k j c", p=P, c=256)
                        sp.dma_start(cols[:, 0:2, :], src[:, :, kind[1], :]).then_inc(loaded[s], 16)
                    else:
                        if kind[0] == "in":
                            src, c = a["w_in"][layer], kind[1]
                        elif kind[0] == "gate":
                            src, c = a["w_gate"][layer], kind[1] * D + 256 * kind[2]
                        elif kind[0] == "branch":
                            src, c = a["w_branch"][layer, kind[1]], 256 * kind[2]
                        elif kind[0] == "out":
                            src, c = a["w_out"][layer], 256 * kind[1]
                        else:
                            src, c = a["w_ple_gate"][layer], 256 * kind[1]
                        sp.dma_start(cols, src.rearrange("(k p) c -> p k c", p=P)[:, :, c:c + 256])\
                            .then_inc(loaded[s], 16)

                def load_ffn(which):
                    n0 = START[f"up{which}"]
                    for n in range(n0, n0 + RING):
                        load_chunk(n)
                    if which == 1:
                        sp.wait_ge(sem["chunk_done"], START["up1"])
                        sp.wait_ge(sem["v_stored"], 64)
                        sp.wait_ge(sem["k_stored"], 112)
                        sp.dma_start(p_rows[:, 0:2, :], a["p_prompt"][layer, 0].rearrange("(t p) c -> p t c", p=P))\
                            .then_inc(sem["p_loaded"], 16)
                        sp.dma_start(p_rows[0:DEC, 2, :], a["p_sample"][layer, 0]).then_inc(sem["p_loaded"], 16)
                    if which == 0:
                        sp.wait_ge(sem["bias_rev_ready"], 1)
                        sp.dma_start(bias_line, bias_rev[:]).then_inc(sem["bias_written"], 16)
                    with sp.Fori(1, 6) as i:
                        for s in range(RING):
                            load_chunk(n0 + s, up_tile=i * RING + s, loop=i)
                    for n in range(n0 + 6 * RING, START[f"down{which}"] + 2 * KT):
                        load_chunk(n)

                rows = sem["rows_loaded"]
                sp.dma_start(conv_rows[0:4, :], a["conv_w"][layer]).then_inc(rows, 16)
                sp.dma_start(conv_rows[4:5, :], a["conv_b"][layer].unsqueeze(0)).then_inc(rows, 16)
                sp.dma_start(conv_rows[5:8, :], a["state_conv"][layer, 0]).then_inc(rows, 16)
                sp.dma_start(gain_rows[0:8, :], a["norm_g"][layer]).then_inc(rows, 16)
                sp.dma_start(gain_rows[8:9, :], a["ssm_norm_g"][layer].unsqueeze(0)).then_inc(rows, 16)
                sp.dma_start(gain_rows[9:12, :], a["b_gate"][layer].rearrange("(r c) -> r c", c=D)).then_inc(rows, 16)
                sp.dma_start(bias_rows[:], a["rel_bias"][layer, 0:512].rearrange("(j p) h -> p j h", p=P))\
                    .then_inc(rows, 16)
                sp.dma_start(dt_bias[:], a["dt_bias"][layer].unsqueeze(1)).then_inc(rows, 16)
                sp.dma_start(neg_a[:], a["a_log"][layer].unsqueeze(1)).then_inc(rows, 16)
                skip = a["d_skip"][layer].rearrange("(i h) -> h i", h=2)
                for half in range(2):
                    sp.dma_start(d_col[64 * half:64 * (half + 1), :], skip[half:half + 1, :].broadcast_to([64, KT]),
                                 allow_slow_non_contiguous=True)\
                        .then_inc(rows, 16)
                load_ffn(0)
                sp.wait_ge(sem["bias_written"], 16)
                sp.dma_start(bias_square, bass.AP(bias_line.tensor, 127, [[512, HEADS], [-1, P], [1, 256]]))\
                    .then_inc(sem["bias_squared"], 16)
                sp.wait_ge(sem["chunk_done"], START["misc"])
                sp.dma_start(state_rows[:], a["state_ssm"][layer, 0].rearrange("(i h) d n -> (h d) i n", h=2))\
                    .then_inc(sem["state_loaded"], 16)
                for n in range(START["misc"], START["gate0"] + 2):
                    load_chunk(n)
                sp.wait_ge(sem["tail_copied"], 4)
                sp.dma_start(conv_p[layer, 0], conv_tail[0:3, :]).then_inc(sem["tail_stored"], 16)
                sp.dma_start(conv_s[layer, 0], conv_tail[67:70, :]).then_inc(sem["tail_stored"], 16)
                for n in range(START["gate0"] + 2, START["branch0"] + 2):
                    load_chunk(n)
                for b, dst in enumerate((ssm_p, ssm_s)):
                    sp.wait_ge(sem["h_rows_ready"], 2 * b + 2)
                    for i in range(2):
                        sp.dma_start(dst[layer, 0].rearrange("(c i h) d n -> i (h d) c n", c=GROUPS, h=2)[i],
                                     h_rows[:, :, P * i:P * (i + 1)]).then_inc(sem["h_stored"], 16)
                sp.wait_ge(sem["h_stored"], 64)
                sp.wait_ge(sem["split_lo"], SPLITS["ssm"] + KT)
                ck = a["cache_dsa_k"][layer, 0].rearrange("t g d -> t (g d)")
                cv = a["cache_dsa_v"][layer, 0].rearrange("t g d -> t (g d)")
                sp.dma_start(k_b_past[:, 0:256], ck).then_inc(sem["k_past_loaded"], 16)
                for c in range(2):
                    sp.dma_start(k_b_past[:, 256 + 64 * c:320 + 64 * c], a["cache_idx_k"][layer, 0])\
                        .then_inc(sem["k_past_loaded"], 16)
                sp.dma_start(v_b_past[:], cv).then_inc(sem["v_past_loaded"], 16)
                for n in range(START["branch0"] + 2, START["gate1"] + 2):
                    load_chunk(n)

                def store_tokens(src, prompt, sample, signal, rows_at=0):
                    sp.dma_start(prompt[layer, 0].rearrange("(t p) c -> p t c", p=P), src[:, 0:2]).then_inc(signal, 16)
                    sp.dma_start(sample[layer, 0], src[rows_at:rows_at + DEC, 2]).then_inc(signal, 16)

                sp.wait_ge(sem["k_rows_ready"], 3)
                store_tokens(k_b_rows[:, :, 0:256], dsa_k_p, dsa_k_s, sem["k_stored"])
                store_tokens(k_b_rows[:, :, 256:320], idx_k_p, idx_k_s, sem["k_stored"])
                sp.wait_ge(sem["evac"], EVAC["vb"] + 1)
                store_tokens(v_b[:], dsa_v_p, dsa_v_s, sem["v_stored"], 64)
                for n in range(START["gate1"] + 2, START["branch1"] + 2):
                    load_chunk(n)
                sp.wait_ge(sem["k_stored"], 64)
                sp.wait_ge(sem["v_stored"], 32)
                sp.wait_ge(sem["attended"], KT)
                sp.wait_ge(sem["bias_squared"], 16)
                sp.dma_start(k_c_rows, a["cache_band_k"][layer, 0].rearrange("t h d -> t (h d)"))\
                    .then_inc(sem["k_past_loaded"], 16)
                sp.dma_start(v_c_past[:], a["cache_band_v"][layer, 0].rearrange("t h d -> t (h d)"))\
                    .then_inc(sem["v_past_loaded"], 16)
                for n in range(START["branch1"] + 2, START["gate2"] + 2):
                    load_chunk(n)
                for t, (_, _, rows_n) in enumerate(TILES):
                    sp.wait_ge(sem["k_rows_ready"], 3 + 2 * (t + 1))
                    dst = band_k_p[layer, 0, P * t:P * (t + 1)] if t < 2 else band_k_s[layer, 0]
                    sp.dma_start(dst, k_c_rows[0:rows_n, :]).then_inc(sem["k_stored"], 16)
                for h in range(HEADS):
                    if h >= 2:
                        sp.wait_ge(sem["shifted"], 8 + h - 1)
                    sp.dma_start(band_bias[:, h % 2, :], bias_square[h]).then_inc(sem[f"bias_loaded{h % 2}"], 16)
                    if h % 4 == 3:
                        load_chunk(START["gate2"] + 2 + h // 4)
                store_tokens(v_c[:], band_v_p, band_v_s, sem["v_stored"], 64)
                for n in range(START["gate2"] + 6, START["up1"]):
                    load_chunk(n)
                load_ffn(1)
                for n in range(START["ple"], N_CHUNKS):
                    load_chunk(n)
                sp.wait_ge(sem["tail_stored"], 32)
                sp.wait_ge(sem["k_stored"], 112)

            @block.gpsimd
            def _(pool):
                def rest(n, loop=None):
                    s = n % RING
                    size = SIZE[CHUNKS[n][0]]
                    pool.wait_ge(sem["w_hi_ready"], n + 1 if loop is None else n + 1 + RING * loop)
                    pool.tensor_tensor(w_lo[:, s, 0:size], stage[:, s, 0:size], f32(w_hi[:, s, 0:size]), ALU.subtract)\
                        .then_inc(sem["w_lo_ready"], 1)

                def rest_ffn(which):
                    n0 = START[f"up{which}"]
                    for n in range(n0, n0 + RING):
                        rest(n)
                    with pool.Fori(1, 6) as i:
                        for s in range(RING):
                            rest(n0 + s, loop=i)
                    for n in range(n0 + 6 * RING, START[f"down{which}"] + 2 * KT):
                        rest(n)

                rest_ffn(0)
                for n in range(START["misc"], START["up1"]):
                    rest(n)
                rest_ffn(1)
                for n in range(START["ple"], N_CHUNKS):
                    rest(n)

            @block.scalar
            def _(act):
                def heads(n, loop=None):
                    if n >= N_CHUNKS:
                        return
                    s = n % RING
                    size = SIZE[CHUNKS[n][0]]
                    if loop is None:
                        act.wait_ge(loaded[s], loaded_count(n))
                        if n >= RING:
                            act.wait_ge(sem["chunk_done"], n - RING + 1)
                    else:
                        act.wait_ge(loaded[s], loaded_count(n) + 32 * loop)
                        act.wait_ge(sem["chunk_done"], n - RING + 1 + RING * loop)
                    act.activation(w_hi[:, s, 0:size], stage[:, s, 0:size], ACT.Copy).then_inc(sem["w_hi_ready"], 1)

                def squares(norm, ready, src, first=1):
                    for k in range(KT):
                        c = KT * NORM[norm] + k
                        if ready is not None:
                            act.wait_ge(sem[ready], first + k)
                        if c >= 2:
                            act.wait_ge(sem["square_used"], c - 1)
                        act.activation(square[:, c % 2, :], src[:, k, :], ACT.Square).then_inc(sem["square_ready"], 1)

                def split_head(q, dst):
                    act.wait_ge(sem["split_src"], q + 1)
                    act.activation(dst, split_tmp[:, q % RING, :], ACT.Copy).then_inc(sem["split_hi"], 1)

                def split_heads(name, dst):
                    for k in range(KT):
                        split_head(SPLITS[name] + k, dst[:, k, :])

                def up_chunk(which, j, loop=None):
                    n = START[f"up{which}"] + j
                    s, more = n % RING, 0 if loop is None else RING * loop
                    act.wait_ge(sem["chunk_done"], n + 1 + more)
                    act.activation(th[:, s, :], bank[2 * s][:, 0:TOK], ACT.Tanh, scale=0.5)\
                        .then_inc(sem["tanh_ready"], 1)
                    q = SPLITS[f"h{which}"] + j
                    act.wait_ge(sem["split_src"], q + 1 + more)
                    dst = h_hi[:, j, :] if loop is None else \
                        h_hi[:, bass.ds(loop * RING + j, 1), :].rearrange("p j t -> p (j t)")
                    act.activation(dst, split_tmp[:, q % RING, :], ACT.Copy).then_inc(sem["split_hi"], 1)

                def ffn(which):
                    n0 = START[f"up{which}"]
                    squares(f"ffn{which}_pre", None if which == 0 else "x_ready", x, XR[f"ffn{which}"] + 1)
                    split_heads(f"u_ffn{which}", u_hi)
                    for j in range(RING):
                        heads(n0 + j + 2)
                        up_chunk(which, j)
                    if which == 1:
                        act.wait_ge(sem["per_layer_turned"], 1)
                        for k in range(2):
                            act.activation(p_hi[:, k, :], bank[6 + k][:, 0:TOK], ACT.Copy).then_inc(sem["p_ready"], 1)
                    with act.Fori(1, 6) as i:
                        for j in range(RING):
                            heads(n0 + j + 2, loop=i)
                            up_chunk(which, j, loop=i)
                    for j in range(6 * RING, FT):
                        heads(n0 + j + 2)
                        up_chunk(which, j)
                    n1 = START[f"down{which}"]
                    for n in range(n1, n1 + 2 * KT):
                        heads(n + 2)
                        if (n - n1) % 2 == 1 and n - n1 > 1:
                            square_y(f"ffn{which}_post", (n - n1) // 2 - 1)
                    square_y(f"ffn{which}_post", KT - 1)

                def square_y(norm, k):
                    c = KT * NORM[norm] + k
                    act.wait_ge(sem["y_ready"], YR[norm] + k + 1)
                    act.wait_ge(sem["square_used"], c - 1)
                    act.activation(square[:, c % 2, :], y[:, k, :], ACT.Square).then_inc(sem["square_ready"], 1)

                step = Chain(act, sem["act_step"])

                heads(0)
                heads(1)
                act.wait_ge(sem["rows_turned"], 1)
                act.activation(bias_rev[:, ::-1], bank[2][0:HEADS, :], ACT.Copy, scale=-1.0).then_inc(sem["bias_rev_ready"], 1)
                act.wait_ge(sem["rows_loaded"], 16 * 11)
                step(act.activation(neg_a[:], neg_a[:], ACT.Exp))
                act.wait_ge(sem["bias_written"], 16)
                ffn(0)

                squares("mix_pre", "x_ready", x, XR["mix"] + 1)
                split_heads("u_mix", u_hi)
                act.wait_ge(sem["state_turned"], 1)
                for b in range(2):
                    act.activation(h_sample[:, 512 * b:512 * (b + 1)], bank[4 + b][:], ACT.Copy)\
                        .then_inc(sem["state_ready"], 1)
                heads(START["misc"] + 2)
                act.wait_ge(sem["dt_v"], 1)
                step(act.activation(dt_tmp[:, 1, :], dt_tmp[:, 1, :], ACT.Exp))
                act.activation(dt_tmp[:, 1, :], dt_tmp[:, 1, :], ACT.Ln, bias=1.0).then_inc(sem["dt_exp"], 1)

                def conv_pair(c):
                    for i in (2 * c, 2 * c + 1):
                        act.wait_ge(sem["evac"], EVAC["xbc"] + c + 1)
                        if i >= 2:
                            act.wait_ge(sem["conv_done"], i - 1)
                        act.activation(conv_acc[:, i % 2, :], xbc[:, i, 0:CONV_N], ACT.Identity,
                                       scale=conv_cols[:, i, 0:1], bias=conv_cols[:, i, 4:5])\
                            .then_inc(sem["conv_base"], 1)
                    for i in (2 * c, 2 * c + 1):
                        act.wait_ge(sem["conv_ready"], i + 1)
                        act.activation(conv_th[:, i % 2, :], conv_acc[:, i % 2, :], ACT.Tanh)\
                            .then_inc(sem["conv_tanh"], 1)

                for c in range(12):
                    heads(START["xbc"] + c + 2)
                    if c == 2:
                        act.wait_ge(sem["dt_done"], 1)
                        for t, (t0, t1, _) in enumerate(TILES):
                            act.activation(head_rows[32:32 + HEADS, t0:t1], head_rows[0:HEADS, t0:t1], ACT.Exp,
                                           bias=head_rows[0:HEADS, t1 - 1:t1], scale=-1.0)\
                                .then_inc(sem["decay_done"], 1)
                    if 2 <= c < 10:
                        if c % 2 == 0:
                            b = c // 2 - 1
                            act.wait_ge(sem["tail_turned"], b + 1)
                            act.activation(conv_tail[:, 512 * b:512 * (b + 1)], bank[4 + b][0:70, :], ACT.Copy)\
                                .then_inc(sem["tail_copied"], 1)
                        conv_pair(c - 2)
                for k in range(KT):
                    if k < 2:
                        act.wait_ge(sem["conv_done"], CT)
                    else:
                        act.wait_ge(sem["z_done"], k - 1)
                    act.wait_ge(sem["evac"], EVAC["z"] + k // 2 + 1)
                    act.activation(conv_th[:, k % 2, 0:TOK], z[:, k, :], ACT.Tanh).then_inc(sem["z_tanh"], 1)

                def gate(b, c, dst):
                    n = START[f"gate{b}"] + c if (b, c) not in ((0, 2), (0, 3)) else START["gate0b"] + c - 2
                    p = pair_of(n)
                    act.wait_ge(sem["chunk_done"], n + 1)
                    for half in range(2):
                        act.activation(dst[:, 2 * c + half, :], bank[2 * p + half][:, 0:TOK], ACT.Tanh, scale=0.5,
                                       bias=gain_cols[:, 2 * c + half, 9 + b:10 + b]).then_inc(sem["gate_tanh"], 1)

                heads(START["gate0"] + 2)
                gate(0, 0, y)
                for t, (_, _, n) in enumerate(TILES):
                    act.wait_ge(sem["b_turned"], t + 1)
                    act.activation(b_rows[0:n, t, :], bank[2 + t][0:n, :], ACT.Copy).then_inc(sem["b_ready"], 1)
                heads(START["gate0"] + 3)
                gate(0, 1, y)
                act.wait_ge(sem["delta_ready"], 1)
                for b in range(2):
                    act.activation(h_prompt[:, 512 * b:512 * (b + 1)], bank[3 + b][:], ACT.Copy)\
                        .then_inc(sem["h1_ready"], 1)

                def row_exponential(h):
                    act.wait_ge(sem["seg_ready"], h + 1)
                    if h >= 2:
                        act.wait_ge(sem["mt_ready"], h - 1)
                    act.activation(row_exp[:, h % 2, :], bank[5 + h % 2][:, 0:TOK], ACT.Exp)
                    act.activation(chunk_decay[:, h, :], bank[5 + h % 2][:, 255:TOK:64], ACT.Exp)\
                        .then_inc(sem["row_exp_ready"], 1)

                row_exponential(0)
                for h in range(HEADS):
                    act.wait_ge(sem["seg_ready"], h + 1)
                    act.activation(seg[:, h % 2, 0:SEQ], seg[:, h % 2, 0:SEQ], ACT.Exp)
                    act.activation(seg[0:DEC, h % 2, SEQ:TOK], seg[0:DEC, h % 2, SEQ:TOK], ACT.Exp)\
                        .then_inc(sem["seg_exp"], 1)
                    if h + 1 < HEADS:
                        row_exponential(h + 1)
                    if h % 2 == 0 and h < 12:
                        heads(START["qi"] + h // 2 + 2)
                heads(START["gate0b"] + 2)
                gate(0, 2, y)
                for b in range(4):
                    act.wait_ge(sem["h_turned"], b + 1)
                    if b == 2:
                        act.wait_ge(sem["h_stored"], 32)
                    act.activation(h_rows[:, 2 * (b % 2):2 * (b % 2) + 2, :],
                                   bank[3 + b][:].rearrange("p (c n) -> p c n", c=2), ACT.Copy)\
                        .then_inc(sem["h_rows_ready"], 1)
                heads(START["gate0b"] + 3)
                gate(0, 3, y)
                squares("ssm", "mixed", z)
                split_heads("ssm", br_hi)

                for n in range(START["branch0"], START["gate1"]):
                    heads(n + 2)
                act.wait_ge(sem["past_turned"], 1)
                act.activation(k_b_past_t[:].rearrange("p i t -> p (i t)"), bank[5][:, 0:384], ACT.Copy)\
                    .then_inc(sem["past_ready"], 1)
                for t, (_, _, n) in enumerate(TILES):
                    act.wait_ge(sem["k_turned"], t + 1)
                    act.activation(k_b_rows[0:n, t, :], bank[2 + t][0:n, 0:320], ACT.Copy).then_inc(sem["k_rows_ready"], 1)
                for h in range(4):
                    heads(START["gate1"] + h + 2)
                    gate(1, h, gates)
                    act.wait_ge(sem["idx_ready"], h + 1)
                    if h >= 2:
                        act.wait_ge(sem["idx_used"], h - 1)
                    act.activation(score_relu[:, h % 2, 0:384], bank[2 + h % 2][:, 0:384], ACT.Relu)
                    act.activation(score_relu[0:DEC, h % 2, 384:576], bank[4 + h % 2][0:DEC, 0:192], ACT.Relu)\
                        .then_inc(sem["idx_relu"], 1)

                def exponentials(c):
                    act.wait_ge(sem["shifted"], c + 1)
                    for j, (r, k0, k1) in enumerate(SPANS):
                        ins = act.activation(logit[0:r, c % 2, k0:k1], logit[0:r, c % 2, k0:k1], ACT.Exp, scale=-1.0,
                                             bias=shift[0:r, c % 2, j:j + 1], accum_out=denom[0:r, c % 2, j:j + 1])
                    ins.then_inc(sem["exped"], 1)

                def attention(first, n_heads, per_tile):
                    exponentials(first)
                    for h in range(n_heads):
                        c = first + h
                        if h + 1 < n_heads:
                            exponentials(c + 1)
                        act.wait_ge(sem["p_turned"], c + 1)
                        if c >= 2:
                            act.wait_ge(sem["attended"], c - 1)
                        act.activation(prob_t[:, c % 2, :], bank[5][:], ACT.Copy).then_inc(sem["p_copied"], 1)
                        if first == 8 and h % 4 == 1:
                            heads(START["gate2"] + h // 4 + 2)
                        if first == 8 and h % 4 == 2:
                            gate(2, h // 4, gates)
                        if h % per_tile == per_tile - 1:
                            tile = h // per_tile
                            act.wait_ge(sem["attended"], c + 1)
                            act.activation(br_hi[:, tile, :], bank[6 + tile % 2][:, 0:TOK], ACT.Copy)\
                                .then_inc(sem["attn_hi"], 1)

                attention(0, 8, 1)
                for n in range(START["branch1"], START["kc"]):
                    heads(n + 2)
                act.wait_ge(sem["past_turned"], 3)
                for b in range(2):
                    act.activation(k_c_past_t[:, 4 * b:4 * b + 4, :].rearrange("p i t -> p (i t)"), bank[6 + b][:],
                                   ACT.Copy).then_inc(sem["past_ready"], 1)
                for n in range(START["kc"], START["gate2"]):
                    heads(n + 2)
                for t, (_, _, rows_n) in enumerate(TILES):
                    for b in range(2):
                        act.wait_ge(sem["k_turned"], 3 + 2 * t + b + 1)
                        if b == 0:
                            if t == 0:
                                act.wait_ge(sem["past_ready"], 3)
                            else:
                                act.wait_ge(sem["k_stored"], 64 + 16 * t)
                        act.activation(k_c_rows[0:rows_n, 512 * b:512 * (b + 1)], bank[4 + (2 * t + b) % 4][0:rows_n, :],
                                       ACT.Copy).then_inc(sem["k_rows_ready"], 1)
                attention(8, 16, 2)
                for n in range(START["branch2"], START["out"]):
                    heads(n + 2)
                split_heads("mix", br_hi)
                for c in range(4):
                    n = START["out"] + c
                    heads(n + 2)
                    if c >= 1:
                        square_y("mix_post", 2 * c - 2)
                        square_y("mix_post", 2 * c - 1)
                square_y("mix_post", 6)
                square_y("mix_post", 7)
                act.wait_ge(sem["k_stored"], 112)
                act.wait_ge(sem["v_stored"], 64)
                ffn(1)
                squares("ple_pre", "x_ready", x, XR["ple"] + 1)
                split_heads("u_ple", u_hi)
                for c in range(4):
                    n = START["ple"] + 2 * c
                    heads(n + 2)
                    heads(n + 3)
                    act.wait_ge(sem["chunk_done"], n + 2)
                    s = pair_of(n + 1)
                    for half in range(2):
                        g = 24 + 2 * c + half
                        act.wait_ge(sem["merged"], g - 1)
                        act.activation(th[:, g % 2, :], bank[2 * s + half][:, 0:TOK], ACT.Tanh, scale=0.5)\
                            .then_inc(sem["gate_tanh"], 1)
                    if c >= 1:
                        square_y("ple_post", 2 * c - 2)
                        square_y("ple_post", 2 * c - 1)
                square_y("ple_post", 6)
                square_y("ple_post", 7)

            @block.tensor
            def _(pe):
                def claim(n, loop=None):
                    p = pair_of(n)
                    if loop is None:
                        pe.wait_ge(sem["w_lo_ready"], n + 1)
                        if frees(n) and freed_before(n):
                            pe.wait_ge(bank_free[p], freed_before(n))
                    else:
                        pe.wait_ge(sem["w_lo_ready"], n + 1 + RING * loop)
                        pe.wait_ge(bank_free[p], freed_before(n) + loop)

                def product(out, s, offset, stride, k_tiles, hi, lo, start=True, stop=True, ready=None):
                    for k in range(k_tiles):
                        if ready is not None:
                            ready(k)
                        at = offset + stride * k
                        wh, wl = w_hi[:, s, at:at + P], w_lo[:, s, at:at + P]
                        pe.matmul(out, wh, hi[:, k, :], start=start and k == 0, stop=False)
                        pe.matmul(out, wh, lo[:, k, :], start=False, stop=False)
                        last = pe.matmul(out, wl, hi[:, k, :], start=False, stop=stop and k == k_tiles - 1)
                    return last

                def wide_chunk(n, hi, lo, k_tiles=KT, ready=None, loop=None):
                    claim(n, loop)
                    s = n % RING
                    for half in range(2):
                        last = product(bank[2 * pair_of(n) + half][:, 0:TOK], s, P * half, 2 * P, k_tiles, hi, lo,
                                       ready=ready if half == 0 else None)
                    last.then_inc(sem["chunk_done"], 1)

                def token_chunk(n):
                    claim(n)
                    s = n % RING
                    for t, t0 in enumerate(STAT_TILES):
                        out = bank[2 * pair_of(n) + t // 2][:, 256 * (t % 2):256 * (t % 2) + 256]
                        for k in range(KT):
                            wh, wl = (w[:, s, 256 * k:256 * (k + 1)] for w in (w_hi, w_lo))
                            uh, ul = (u[:, k, t0:t0 + P] for u in (u_hi, u_lo))
                            pe.matmul(out, uh, wh, start=k == 0, stop=False)
                            pe.matmul(out, ul, wh, start=False, stop=False)
                            last = pe.matmul(out, uh, wl, start=False, stop=k == KT - 1)
                    last.then_inc(sem["chunk_done"], 1)

                def split_ready(name):
                    return lambda k: pe.wait_ge(sem["split_lo"], SPLITS[name] + k + 1)

                def square_sum(name, k):
                    i = NORM[name]
                    c, g = KT * i + k, k * NORMS[i][2] // KT
                    pe.wait_ge(sem["square_ready"], c + 1)
                    for t, t0 in enumerate(STAT_TILES):
                        ins = pe.matmul(stat_bank[:, 3 * g + t:3 * g + t + 1], square[:, c % 2, t0:t0 + P],
                                        ones[:, 0:1], start=k == 0 and t == 0, stop=k == KT - 1 and t == 2,
                                        skip_group_check=True)
                    ins.then_inc(sem["square_used"], 1)

                def norm(name, first=0):
                    i = NORM[name]
                    groups = NORMS[i][2]
                    for k in range(first, KT):
                        square_sum(name, k)
                    pe.wait_ge(sem["diag_ready"], i + 1)
                    for g, b in enumerate(ROW_BANKS[groups]):
                        for t, t0 in enumerate(STAT_TILES):
                            last = pe.matmul(bank[b][:, t0:t0 + P], ones[:], diagonal(3 * g + t), start=True,
                                             stop=True)
                    last.then_inc(sem["row_ready"], 1)

                def ffn(which):
                    norm(f"ffn{which}_pre")
                    n0 = START[f"up{which}"]
                    for j in range(RING):
                        wide_chunk(n0 + j, u_hi, u_lo, ready=split_ready(f"u_ffn{which}") if j == 0 else None)
                    if which == 1:
                        pe.wait_ge(sem["p_loaded"], 32)
                        for k in range(2):
                            for t, (t0, t1, n) in enumerate(TILES):
                                last = pe.transpose(bank[6 + k][:, t0:t1], p_rows[0:n, t, P * k:P * (k + 1)],
                                                    ident[0:n, 0:n])
                        last.then_inc(sem["per_layer_turned"], 1)
                    with pe.Fori(1, 6) as i:
                        for j in range(RING):
                            wide_chunk(n0 + j, u_hi, u_lo, loop=i)
                    for j in range(6 * RING, FT):
                        wide_chunk(n0 + j, u_hi, u_lo)
                    n1 = START[f"down{which}"]
                    for j in range(KT):
                        for half in range(2):
                            n = n1 + 2 * j + half
                            claim(n)
                            k0 = HALF_FT * half
                            ready = None
                            if j == 0:
                                def ready(k, k0=k0):
                                    pe.wait_ge(sem["split_lo"], SPLITS[f"h{which}"] + k0 + k + 1)
                            last = product(bank[2 * ((n1 + 2 * j) % RING)][:, 0:TOK], n % RING, 0, P, HALF_FT,
                                           h_hi[:, k0:k0 + HALF_FT, :], h_lo[:, k0:k0 + HALF_FT, :],
                                           start=half == 0, stop=half == 1, ready=ready)
                            last.then_inc(sem["chunk_done"], 1)
                        if j >= 1:
                            square_sum(f"ffn{which}_post", j - 1)
                    norm(f"ffn{which}_post", KT - 1)

                pe.wait_ge(sem["rows_loaded"], 16 * 11)
                for i in range(CT):
                    pe.transpose(bank[6][:, 8 * i:8 * i + 8], conv_rows[:, P * i:P * (i + 1)], ident[0:8, 0:8])
                for k in range(KT):
                    pe.transpose(bank[7][:, 12 * k:12 * k + 12], gain_rows[:, P * k:P * (k + 1)], ident[0:12, 0:12])
                for j in range(4):
                    last = pe.transpose(bank[2][0:HEADS, P * j:P * (j + 1)], bias_rows[:, j, :], ident[:])
                last.then_inc(sem["rows_turned"], 1)
                pe.wait_ge(sem["cols_ready"], 1)
                pe.wait_ge(sem["bias_rev_ready"], 1)
                ffn(0)

                norm("mix_pre")
                pe.wait_ge(sem["state_loaded"], 16)
                for i in range(KT):
                    last = pe.transpose(bank[4 + i // 4][:, P * (i % 4):P * (i % 4 + 1)], state_rows[:, i, :], ident[:])
                last.then_inc(sem["state_turned"], 1)
                wide_chunk(START["misc"], u_hi, u_lo, ready=split_ready("u_mix"))
                pe.wait_ge(sem["state_ready"], 2)
                for c in range(12):
                    wide_chunk(START["xbc"] + c, u_hi, u_lo)
                    if c % 2 == 0 and 2 <= c < 10:
                        b = c // 2 - 1
                        pe.wait_ge(sem["evac"], EVAC["xbc"] + 2 * b + 2)
                        for i in range(4):
                            last = pe.transpose(bank[4 + b][0:70, P * i:P * (i + 1)], xbc[:, 4 * b + i, 256:326],
                                                ident[:])
                        last.then_inc(sem["tail_turned"], 1)
                pe.wait_ge(sem["decay_done"], 3)
                pe.wait_ge(sem["dt_done"], 1)
                pe.wait_ge(sem["tail_copied"], 4)
                for t, (t0, t1, n) in enumerate(TILES):
                    last = pe.transpose(bank[7][0:n, P * t:P * (t + 1)], head_rows[:, t0:t1], ident[:])
                last.then_inc(sem["rows_cols_turned"], 1)
                wide_chunk(START["gate0"], u_hi, u_lo)
                pe.wait_ge(sem["conv_done"], CT)
                for t, (t0, t1, n) in enumerate(TILES):
                    for b in range(2):
                        if 2 * t + b < 2:
                            pe.wait_ge(sem["evac"], EVAC["z"] + 4)
                        if 2 * t + b == 5:
                            pe.wait_ge(sem["head_cols_ready"], 1)
                        for i in range(4):
                            last = pe.transpose(bank[2 + 2 * t + b][0:n, P * i:P * (i + 1)],
                                                xbc[:, 4 * b + i, t0:t1], ident[:])
                        last.then_inc(sem["xs_turned"], 1)
                for t, (t0, t1, n) in enumerate(TILES):
                    pe.wait_ge(sem["xdt_ready"], t + 1)
                    for g in range(GROUPS):
                        last = pe.transpose(bank[2 + t][0:n, P * g:P * (g + 1)], xbc[:, 8 + g, t0:t1], ident[:])
                    last.then_inc(sem["b_turned"], 1)
                wide_chunk(START["gate0"] + 1, u_hi, u_lo)
                pe.wait_ge(sem["xdt_ready"], 6)
                pe.wait_ge(sem["b_ready"], 1)
                for g in range(GROUPS):
                    for t, (t0, t1, n) in enumerate(TILES):
                        last = pe.matmul(bank[CB_BANK[g]][0:n, t0:t1], xbc[:, 8 + g, t0:t1], xbc[:, 12 + g, t0:t1],
                                         start=True, stop=True)
                    last.then_inc(sem["cb_ready"], 1)

                def state_delta(t):
                    n = TILES[t][2]
                    pe.wait_ge(sem["xdec_ready"], t + 1)
                    for g in range(GROUPS):
                        last = pe.matmul(bank[3 + g // 2][:, 256 * (g % 2):256 * (g % 2) + 256],
                                         b_rows[0:n, t, P * g:P * (g + 1)], xdec[0:n, 256 * g:256 * (g + 1)],
                                         start=True, stop=True)
                    last.then_inc(sem["delta_ready"], 1)

                pe.wait_ge(sem["b_ready"], 3)
                pe.wait_ge(sem["cb_masked"], 4)
                state_delta(0)

                def head_row(h):
                    if h >= 2:
                        pe.wait_ge(sem["row_exp_ready"], h - 1)
                        pe.wait_ge(sem["seg_ready"], h - 1)
                    pe.matmul(bank[5 + h % 2][:, 0:TOK], ident[0:HEADS, h:h + 1].broadcast_to([HEADS, P]),
                              head_rows[0:HEADS, :], start=True, stop=True).then_inc(sem["bc_ready"], 1)

                pe.wait_ge(sem["b_ready"], 3)
                head_row(0)
                pe.wait_ge(sem["h1_ready"], 2)
                for h in range(HEADS):
                    if h + 1 < HEADS:
                        head_row(h + 1)
                    pe.wait_ge(sem["mt_ready"], h + 1)
                    i, r0 = h // 2, 64 * (h % 2)
                    if i >= 2:
                        pe.wait_ge(sem["mixed"], i - 1)
                    out = bank[(7, 2)[i % 2]]
                    f = slice(64 * h, 64 * h + 64)
                    pe.matmul(out[r0:r0 + 64, 0:128], xdt[:, 0, f], seg[:, h % 2, 0:128], start=True, stop=True)
                    pe.matmul(out[r0:r0 + 64, 128:256], xdt[:, 1, f], seg[:, h % 2, 128:256], start=True, stop=False)
                    pe.matmul(out[r0:r0 + 64, 128:256], h_prompt[:, f], row_exp[:, h % 2, 128:256], start=False,
                              stop=True)
                    pe.matmul(out[r0:r0 + 64, 256:320], xdt[0:DEC, 2, f], seg[0:DEC, h % 2, 256:320], start=True,
                              stop=False)
                    pe.matmul(out[r0:r0 + 64, 256:320], h_sample[:, f], row_exp[:, h % 2, 256:320], start=False,
                              stop=True).then_inc(sem["head_done"], 1)
                    if h % 2 == 0 and h < 12:
                        wide_chunk(START["qi"] + h // 2, u_hi, u_lo)
                for t in (1, 2):
                    if t == 2:
                        pe.wait_ge(sem["h_final"], 1)
                    state_delta(t)
                    if t == 1:
                        wide_chunk(START["gate0b"], u_hi, u_lo)
                pe.wait_ge(sem["h_final"], 2)
                pe.wait_ge(sem["mixed"], KT)
                for b in range(4):
                    src = h_prompt if b < 2 else h_sample
                    for i in range(4):
                        at = 512 * (b % 2) + P * i
                        last = pe.transpose(bank[3 + b][:, P * i:P * (i + 1)], src[:, at:at + P], ident[:])
                    last.then_inc(sem["h_turned"], 1)
                wide_chunk(START["gate0b"] + 1, u_hi, u_lo)
                pe.wait_ge(sem["h_rows_ready"], 4)
                norm("ssm")

                def merge(b):
                    for c in range(4):
                        wide_chunk(START[f"branch{b}"] + c, br_hi, br_lo)

                pe.wait_ge(sem["split_lo"], SPLITS["ssm"] + KT)
                merge(0)
                token_chunk(START["vb"])
                pe.wait_ge(sem["merged"], 8)
                pe.wait_ge(sem["k_past_loaded"], 48)
                for i in range(3):
                    last = pe.transpose(bank[5][:, P * i:P * (i + 1)], k_b_past[:, P * i:P * (i + 1)], ident[:])
                last.then_inc(sem["past_turned"], 1)
                for t, (t0, t1, n) in enumerate(TILES):
                    for i in range(2):
                        pe.transpose(bank[2 + t][0:n, P * i:P * (i + 1)], k_b[:, i, t0:t1], ident[:])
                    pe.transpose(bank[2 + t][0:n, 256:320], ki[0:64, t0:t1], ident[0:64, 0:64])\
                        .then_inc(sem["k_turned"], 1)

                def scores(q, qp, k, k_past, wide, narrow):
                    pe.matmul(wide[:, 0:128], q[qp, 0:128], k[qp, 0:128], start=True, stop=True)
                    pe.matmul(wide[:, 128:384], q[qp, 128:256], k[qp, 0:256], start=True, stop=True)
                    pe.matmul(narrow[0:DEC, 0:128], q[qp, 256:320], k_past[qp, :], start=True, stop=True)
                    return pe.matmul(narrow[0:DEC, 128:192], q[qp, 256:320], k[qp, 256:320], start=True, stop=True)

                pe.wait_ge(sem["past_ready"], 1)
                for h in range(4):
                    wide_chunk(START["gate1"] + h, u_hi, u_lo)
                    if h == 0:
                        pe.wait_ge(sem["k_rows_ready"], 3)
                    if h >= 2:
                        pe.wait_ge(sem["idx_relu"], h - 1)
                    qp = slice(64 * (h % 2), 64 * (h % 2) + 64)
                    scores(q_i[:, h // 2, :], qp, ki[:], k_b_past_t[:, 2, :], bank[2 + h % 2], bank[4 + h % 2])\
                        .then_inc(sem["idx_ready"], 1)

                def attention(first, n_heads, per_tile, q, k, k_past, v, v_past, d, q_per_kv):
                    def score_head(h):
                        c = first + h
                        if c >= 1:
                            pe.wait_ge(sem["shifted"], c)
                        qp = slice(d * (h % per_tile), d * (h % per_tile) + d)
                        kt = h // q_per_kv // per_tile
                        scores(q[:, h // per_tile, :], qp, k[:, kt, :], k_past[:, kt, :], bank[2 + c % 2],
                               bank[4]).then_inc(sem["scored"], 1)

                    score_head(0)
                    for h in range(n_heads):
                        c = first + h
                        if h + 1 < n_heads:
                            score_head(h + 1)
                        pe.wait_ge(sem["normed"], c + 1)
                        if c >= 1:
                            pe.wait_ge(sem["p_copied"], c)
                        tb = bank[5]
                        for dst, r, k0 in ((0, 128, 0), (128, 128, 128), (256, 128, 256), (384, 64, 384), (448, 64, 448)):
                            last = pe.transpose(tb[:, dst:dst + r], logit[0:r, c % 2, k0:k0 + P], ident[0:r, 0:r])
                        last.then_inc(sem["p_turned"], 1)
                        if first == 8 and h % 4 == 0:
                            wide_chunk(START["gate2"] + h // 4, u_hi, u_lo)
                        tile = h // per_tile
                        all_tile = TILE0[first] + tile
                        if h % per_tile == 0 and tile >= 2:
                            pe.wait_ge(sem["attn_lo"], all_tile - 1)
                        pe.wait_ge(sem["p_copied"], c + 1)
                        r0 = d * (h % per_tile)
                        ob, pt = bank[6 + tile % 2][r0:r0 + d], prob_t[:, c % 2]
                        f = slice(d * (h // q_per_kv), d * (h // q_per_kv) + d)
                        pe.matmul(ob[:, 0:128], v[:, 0, f], pt[:, 0:128], start=True, stop=True)
                        pe.matmul(ob[:, 128:256], v[:, 0, f], pt[:, 128:256], start=True, stop=False)
                        pe.matmul(ob[:, 128:256], v[:, 1, f], pt[:, 256:384], start=False, stop=True)
                        pe.matmul(ob[:, 256:320], v_past[:, f], pt[:, 384:448], start=True, stop=False)
                        pe.matmul(ob[:, 256:320], v[64:128, 2, f], pt[64:128, 448:512], start=False, stop=True)\
                            .then_inc(sem["attended"], 1)

                pe.wait_ge(sem["k_rows_ready"], 3)
                pe.wait_ge(sem["idx_relu"], 4)
                pe.wait_ge(sem["v_past_loaded"], 16)
                attention(0, 8, 1, q_b, k_b, k_b_past_t, v_b, v_b_past, 128, 4)
                pe.wait_ge(sem["attn_lo"], 8)
                merge(1)
                pe.wait_ge(sem["k_past_loaded"], 64)
                for i in range(KT):
                    last = pe.transpose(bank[6 + i // 4][:, P * (i % 4):P * (i % 4 + 1)], k_c_rows[:, P * i:P * (i + 1)],
                                        ident[:])
                    if i % 4 == 3:
                        last.then_inc(sem["past_turned"], 1)
                for c in range(4):
                    wide_chunk(START["kc"] + c, u_hi, u_lo)
                for c in range(4):
                    token_chunk(START["vc"] + c)
                for c in range(4):
                    wide_chunk(START["qc"] + c, u_hi, u_lo)
                pe.wait_ge(sem["evac"], EVAC["qc"] + 4)
                pe.wait_ge(sem["past_ready"], 3)
                for t, (t0, t1, n) in enumerate(TILES):
                    for b in range(2):
                        if t == 2:
                            pe.wait_ge(sem["k_rows_ready"], 3 + b + 1)
                        for i in range(4):
                            last = pe.transpose(bank[4 + (2 * t + b) % 4][0:n, P * i:P * (i + 1)], k_c[:, 4 * b + i, t0:t1],
                                                ident[:])
                        last.then_inc(sem["k_turned"], 1)
                pe.wait_ge(sem["k_rows_ready"], 9)
                pe.wait_ge(sem["past_ready"], 3)
                pe.wait_ge(sem["v_past_loaded"], 32)
                attention(8, 16, 2, q_c, k_c, k_c_past_t, v_c, v_c_past, 64, 1)
                pe.wait_ge(sem["attn_lo"], 16)
                merge(2)
                for c in range(4):
                    wide_chunk(START["out"] + c, br_hi, br_lo, ready=split_ready("mix") if c == 0 else None)
                    if c >= 1:
                        square_sum("mix_post", 2 * c - 2)
                        square_sum("mix_post", 2 * c - 1)
                norm("mix_post", 6)
                ffn(1)
                norm("ple_pre")
                for c in range(4):
                    wide_chunk(START["ple"] + 2 * c, p_hi, p_lo, k_tiles=2)
                    wide_chunk(START["ple"] + 2 * c + 1, u_hi, u_lo, ready=split_ready("u_ple") if c == 0 else None)
                    if c >= 1:
                        square_sum("ple_post", 2 * c - 2)
                        square_sum("ple_post", 2 * c - 1)
                norm("ple_post", 6)

            @block.vector
            def _(dve):
                step = Chain(dve, sem["dve_step"])

                def norm_rows(name, scale=1.0):
                    i = NORM[name]
                    _, tiles, groups = NORMS[i]
                    w = 3 * groups
                    v, r, t = rs[:, 0, 0:w], rs[:, 1, 0:w], rs[:, 2, 0:w]
                    dve.wait_ge(sem["square_used"], KT * (i + 1))
                    step(dve.tensor_scalar(v, stat_bank[:, 0:w], groups / D, EPS, ALU.mult, ALU.add))
                    step(dve.tensor_scalar(r.bitcast(I32), v.bitcast(I32), -0.5, RSQRT_SEED, ALU.mult, ALU.add))
                    for _ in range(3):
                        step(dve.tensor_tensor(t, r, r, ALU.mult))
                        step(dve.scalar_tensor_tensor(out=t, in0=t, scalar=-0.5, in1=v, op0=ALU.mult, op1=ALU.mult))
                        step(dve.scalar_tensor_tensor(out=r, in0=t, scalar=1.5, in1=r, op0=ALU.add, op1=ALU.mult))
                    for c in range(w):
                        last = dve.tensor_scalar(diagonal(c), ident[:], r[:, c:c + 1], scale, ALU.mult, ALU.mult)
                    last.then_inc(sem["diag_ready"], 1)
                    dve.wait_ge(sem["row_ready"], i + 1)

                def split_rest(q, dst_hi, dst_lo):
                    dve.wait_ge(sem["split_hi"], q + 1)
                    dve.tensor_tensor(dst_lo, split_tmp[:, q % RING, :], f32(dst_hi), ALU.subtract)\
                        .then_inc(sem["split_lo"], 1)

                def split_source(q, write):
                    if q >= RING:
                        dve.wait_ge(sem["split_lo"], q - RING + 1)
                    write(split_tmp[:, q % RING, :]).then_inc(sem["split_src"], 1)

                def norm_split(name, split, src, gain, hi, lo):
                    groups = NORMS[NORM[name]][2]
                    banks = ROW_BANKS[groups]
                    q0 = SPLITS[split]
                    norm_rows(name)
                    for k in range(KT + 1):
                        if k < KT:
                            row = bank[banks[k * groups // KT]][:, 0:TOK]
                            split_source(q0 + k, lambda dst: dve.scalar_tensor_tensor(
                                out=dst, in0=src[:, k, :], scalar=gain_cols[:, k, gain:gain + 1], in1=row,
                                op0=ALU.mult, op1=ALU.mult))
                        if k >= 1:
                            split_rest(q0 + k - 1, hi[:, k - 1, :], lo[:, k - 1, :])

                def add_normed(name, gain, scale):
                    norm_rows(name, scale)
                    for k in range(KT + 1):
                        if k < KT:
                            dve.scalar_tensor_tensor(out=y[:, k, :], in0=y[:, k, :],
                                                     scalar=gain_cols[:, k, gain:gain + 1], in1=bank[7][:, 0:TOK],
                                                     op0=ALU.mult, op1=ALU.mult).then_inc(sem["dve_step"], 1)
                            step.count += 1
                        if k >= 1:
                            dve.wait_ge(sem["dve_step"], step.count - (1 if k < KT else 0))
                            dve.tensor_tensor(x[:, k - 1, :], x[:, k - 1, :], y[:, k - 1, :], ALU.add)\
                                .then_inc(sem["x_ready"], 1)

                def up_chunk(which, j, loop=None):
                    n = START[f"up{which}"] + j
                    s, more = n % RING, 0 if loop is None else RING * loop
                    q = SPLITS[f"h{which}"] + j
                    tmp = split_tmp[:, q % RING, :]
                    dve.wait_ge(sem["tanh_ready"], FT * which + j + 1 + more)
                    dve.scalar_tensor_tensor(out=tmp, in0=th[:, s, :], scalar=1.0, in1=bank[2 * s][:, 0:TOK],
                                             op0=ALU.add, op1=ALU.mult).then_inc(sem["silu_ready"], 1)
                    dve.wait_ge(sem["silu_ready"], FT * which + j + 1 + more)
                    dve.scalar_tensor_tensor(out=tmp, in0=tmp, scalar=0.5, in1=bank[2 * s + 1][:, 0:TOK],
                                             op0=ALU.mult, op1=ALU.mult).then_inc(sem["split_src"], 1)
                    dve.wait_ge(sem["split_hi"], q + 1 + more)
                    if loop is None:
                        hi, lo = h_hi[:, j, :], h_lo[:, j, :]
                    else:
                        hi, lo = (h[:, bass.ds(loop * RING + j, 1), :].rearrange("p j t -> p (j t)")
                                  for h in (h_hi, h_lo))
                    dve.tensor_tensor(lo, tmp, f32(hi), ALU.subtract).then_inc(sem["split_lo"], 1)
                    dve.wait_ge(sem["split_lo"], q + 1 + more)
                    dve.sem_inc(bank_free[s], 1)

                def ffn(which):
                    norm_split(f"ffn{which}_pre", f"u_ffn{which}", x, 4 * which, u_hi, u_lo)
                    for j in range(RING):
                        up_chunk(which, j)
                    if which == 1:
                        for k in range(2):
                            dve.wait_ge(sem["p_ready"], 2)
                            step(dve.tensor_tensor(p_lo[:, k, :], bank[6 + k][:, 0:TOK], f32(p_hi[:, k, :]),
                                                   ALU.subtract))
                    with dve.Fori(1, 6) as i:
                        for j in range(RING):
                            up_chunk(which, j, loop=i)
                    for j in range(6 * RING, FT):
                        up_chunk(which, j)
                    n1 = START[f"down{which}"]
                    for j in range(KT):
                        dve.wait_ge(sem["chunk_done"], n1 + 2 * j + 2)
                        s = (n1 + 2 * j) % RING
                        step(dve.tensor_copy(y[:, j, :], bank[2 * s][:, 0:TOK]))
                        dve.sem_inc(bank_free[s], 1)
                        dve.sem_inc(sem["y_ready"], 1)
                    add_normed(f"ffn{which}_post", 4 * which + 1, 0.5)

                def give_back(n):
                    dve.sem_inc(bank_free[pair_of(n)], 1)

                def evacuate(n, writes):
                    s = pair_of(n)
                    dve.wait_ge(sem["chunk_done"], n + 1)
                    for write in writes(bank[2 * s], bank[2 * s + 1]):
                        last = write
                    last.then_inc(sem["evac"], 1)
                    dve.wait_ge(sem["evac"], EVAC_OF[n] + 1)
                    give_back(n)

                dve.wait_ge(sem["rows_turned"], 1)
                cc = bank[6][:, 0:8 * CT].rearrange("p (i r) -> p i r", r=8)
                gc = bank[7][:, 0:12 * KT].rearrange("p (i r) -> p i r", r=12)
                dve.tensor_scalar(conv_cols[:, :, 0:5], cc[:, :, 0:5], 0.5, None, ALU.mult)
                dve.tensor_copy(conv_cols[:, :, 5:8], cc[:, :, 5:8])
                dve.tensor_copy(gain_cols[:, :, 0:9], gc[:, :, 0:9])
                step(dve.tensor_scalar(gain_cols[:, :, 9:12], gc[:, :, 9:12], 0.5, None, ALU.mult))
                dve.sem_inc(sem["cols_ready"], 1)
                ffn(0)

                norm_split("mix_pre", "u_mix", x, 2, u_hi, u_lo)
                dve.memset(xbc[:, :, 0:3], 0.0)
                step(dve.tensor_copy(xbc[:, :, SEQ + 3:SEQ + 6], conv_cols[:, :, 5:8]))
                evacuate(START["misc"], lambda b0, b1: (
                    dve.tensor_copy(ki[:], b0[:, 0:TOK]),
                    dve.tensor_scalar(dt_tmp[:, 0, :], b1[0:HEADS, 0:TOK], dt_bias[:], None, ALU.add),
                    dve.tensor_scalar(head_rows[96:100, :], b1[32:36, 0:TOK], 0.5, None, ALU.mult)))
                dve.scalar_tensor_tensor(out=dt_tmp[:, 1, :], in0=dt_tmp[:, 0, :], scalar=-1.0, in1=dt_tmp[:, 0, :],
                                         op0=ALU.mult, op1=ALU.min).then_inc(sem["dt_v"], 1)

                def copies(dst, k0, scale):
                    def writes(b0, b1):
                        for half, b in enumerate((b0, b1)):
                            if scale is None:
                                yield dve.tensor_copy(dst[:, k0 + half, :], b[:, 0:TOK])
                            else:
                                yield dve.tensor_scalar(dst[:, k0 + half, :], b[:, 0:TOK], scale, None, ALU.mult)
                    return writes

                def values(dst, c0):
                    def writes(b0, b1):
                        yield dve.tensor_copy(dst[:, 0:2, c0:c0 + 256], b0[:].rearrange("p (t c) -> p t c", c=256))
                        yield dve.tensor_copy(dst[:, 2, c0:c0 + 256], b1[:, 0:256])
                    return writes

                def dsa_writes(i):
                    if i == 0:
                        return copies(q_i, 0, 0.125)
                    if i == 1:
                        return copies(k_b, 0, None)
                    return copies(q_b, 2 * (i - 2), -float(128) ** -0.5)

                def cumulative_decay():
                    dve.wait_ge(sem["dt_exp"], 1)
                    dt_rows = dt_tmp[:, 0, :]
                    step(dve.scalar_tensor_tensor(out=dt_rows, in0=dt_rows, scalar=0.0, in1=dt_tmp[:, 1, :],
                                                  op0=ALU.max, op1=ALU.add))
                    dve.tensor_copy(head_rows[64:64 + HEADS, :], dt_rows)
                    dve.memset(dt_tmp[:, 1, :], 1.0)
                    step(dve.tensor_scalar(dt_tmp[:, 2, :], dt_rows, neg_a[:], -1.0, ALU.mult, ALU.mult))
                    for t0, t1, _ in TILES:
                        last = dve.tensor_tensor_scan(head_rows[0:HEADS, t0:t1], dt_tmp[:, 1, t0:t1],
                                                      dt_tmp[:, 2, t0:t1], 0.0, ALU.mult, ALU.add)
                    last.then_inc(sem["dt_done"], 1)

                def conv_pair(c):
                    dve.wait_ge(sem["conv_base"], 2 * c + 2)
                    for k in range(1, 4):
                        for i in (2 * c, 2 * c + 1):
                            acc = conv_acc[:, i % 2, :]
                            ins = dve.scalar_tensor_tensor(out=acc, in0=xbc[:, i, k:k + CONV_N],
                                                           scalar=conv_cols[:, i, k:k + 1], in1=acc, op0=ALU.mult,
                                                           op1=ALU.add)
                            if k < 3:
                                ins.then_inc(sem["dve_step"], 1)
                                step.count += 1
                                dve.wait_ge(sem["dve_step"], step.count - 1)
                            else:
                                if i % 2 == 0:
                                    dve.wait_ge(sem["dve_step"], step.count)
                                ins.then_inc(sem["conv_ready"], 1)
                    for i in (2 * c, 2 * c + 1):
                        dve.wait_ge(sem["conv_tanh"], i + 1)
                        dve.wait_ge(sem["conv_ready"], i + 1)
                        dve.wait_ge(sem["tail_turned"], i // 4 + 1)
                        for out0, t0, w in ((0, 0, SEQ), (SEQ, SEQ + 3, DEC)):
                            last = dve.scalar_tensor_tensor(out=xbc[:, i, out0:out0 + w],
                                                            in0=conv_th[:, i % 2, t0:t0 + w], scalar=1.0,
                                                            in1=conv_acc[:, i % 2, t0:t0 + w], op0=ALU.add,
                                                            op1=ALU.mult)
                        last.then_inc(sem["conv_done"], 1)

                for c in range(12):
                    if c < 8:
                        evacuate(START["xbc"] + c, lambda b0, b1: (
                            dve.tensor_copy(xbc[:, 2 * c + half, at:at + w], b[:, t0:t0 + w])
                            for half, b in enumerate((b0, b1)) for at, t0, w in ((3, 0, SEQ), (SEQ + 6, SEQ, DEC))))
                    else:
                        evacuate(START["xbc"] + c, lambda b0, b1: (
                            dve.tensor_scalar(z[:, 2 * (c - 8) + half, :], b[:, 0:TOK], 0.5, None, ALU.mult)
                            for half, b in enumerate((b0, b1))))
                    if c == 0:
                        cumulative_decay()
                    if 2 <= c < 10:
                        conv_pair(c - 2)
                for k in range(KT):
                    dve.wait_ge(sem["z_tanh"], k + 1)
                    dve.scalar_tensor_tensor(out=z[:, k, :], in0=conv_th[:, k % 2, 0:TOK], scalar=1.0, in1=z[:, k, :],
                                             op0=ALU.add, op1=ALU.mult).then_inc(sem["z_done"], 1)

                def gate_taken(n):
                    order = [m for m in range(N_CHUNKS) if CHUNKS[m][0] == "gate"]
                    dve.wait_ge(sem["gate_tanh"], 2 * order.index(n) + 2)
                    give_back(n)

                dve.wait_ge(sem["rows_cols_turned"], 1)
                dve.tensor_copy(head_cols[:, 0:2, :].rearrange("p t c -> p (t c)"), bank[7][:, 0:256])
                dve.tensor_copy(head_cols[0:DEC, 2, :], bank[7][0:DEC, 256:384]).then_inc(sem["head_cols_ready"], 1)
                dve.wait_ge(sem["head_cols_ready"], 1)
                dve.wait_ge(sem["tail_stored"], 32)
                for t, (_, _, n) in enumerate(TILES):
                    for b in range(2):
                        dve.wait_ge(sem["xs_turned"], 2 * t + b + 1)
                        dve.tensor_tensor(
                            xdt[0:n, t, 512 * b:512 * (b + 1)].rearrange("p (h d) -> p h d", d=64),
                            bank[2 + 2 * t + b][0:n, :].rearrange("p (h d) -> p h d", d=64),
                            head_cols[0:n, t, 64 + 8 * b:72 + 8 * b].unsqueeze(2).broadcast_to([n, 8, 64]), ALU.mult)\
                            .then_inc(sem["xdt_ready"], 1)
                gate_taken(START["gate0"])
                for g in range(GROUPS):
                    dve.wait_ge(sem["cb_ready"], GROUPS)
                    for t, (t0, t1, n) in enumerate(TILES):
                        last = dve.tensor_tensor(cb[0:n, g, t0:t1], bank[CB_BANK[g]][0:n, t0:t1], tri[0:n, 0:n], ALU.mult)
                    last.then_inc(sem["cb_masked"], 1)

                def decayed(t):
                    n = TILES[t][2]
                    if t >= 1:
                        dve.wait_ge(sem["delta_ready"], t)
                    dve.tensor_tensor(xdec[0:n, :].rearrange("p (h d) -> p h d", d=64),
                                      xdt[0:n, t, :].rearrange("p (h d) -> p h d", d=64),
                                      head_cols[0:n, t, 32:32 + HEADS].unsqueeze(2).broadcast_to([n, HEADS, 64]),
                                      ALU.mult).then_inc(sem["xdec_ready"], 1)

                dve.wait_ge(sem["xdt_ready"], 6)
                decayed(0)
                gate_taken(START["gate0"] + 1)

                def segments(h):
                    dve.wait_ge(sem["bc_ready"], h + 1)
                    if h >= 2:
                        dve.wait_ge(sem["head_done"], h - 1)
                    for t, (t0, t1, n) in enumerate(TILES):
                        last = dve.tensor_scalar(seg[0:n, h % 2, t0:t1], bank[5 + h % 2][0:n, t0:t1],
                                                 head_cols[0:n, t, h:h + 1], 0.0, ALU.subtract, ALU.min)
                    last.then_inc(sem["seg_ready"], 1)

                def mix_tile(i):
                    dve.wait_ge(sem["head_done"], 2 * i + 2)
                    mixed = split_tmp[:, 0, :]
                    step(dve.scalar_tensor_tensor(out=mixed, in0=xbc[:, i, 0:TOK], scalar=d_col[:, i:i + 1],
                                                  in1=bank[(7, 2)[i % 2]][:, 0:TOK], op0=ALU.mult, op1=ALU.add))
                    dve.tensor_tensor(z[:, i, :], z[:, i, :], mixed, ALU.mult).then_inc(sem["mixed"], 1)
                    dve.wait_ge(sem["mixed"], i + 1)

                dve.wait_ge(sem["conv_done"], CT)
                dve.wait_ge(sem["cb_masked"], 4)
                segments(0)
                for h in range(HEADS):
                    if h + 1 < HEADS:
                        segments(h + 1)
                    g = h // (HEADS // GROUPS)
                    dve.wait_ge(sem["seg_exp"], h + 1)
                    dve.tensor_tensor(seg[:, h % 2, 0:SEQ], seg[:, h % 2, 0:SEQ], cb[:, g, 0:SEQ], ALU.mult)
                    dve.tensor_tensor(seg[0:DEC, h % 2, SEQ:TOK], seg[0:DEC, h % 2, SEQ:TOK], cb[0:DEC, g, SEQ:TOK],
                                      ALU.mult)
                    dve.wait_ge(sem["row_exp_ready"], h + 1)
                    dve.tensor_tensor(row_exp[:, h % 2, 128:TOK], row_exp[:, h % 2, 128:TOK], xbc[:, 12 + g, 128:TOK],
                                      ALU.mult).then_inc(sem["mt_ready"], 1)
                    if h % 2 == 0 and h >= 2:
                        mix_tile(h // 2 - 1)
                    if h % 2 == 1 and h < 12:
                        evacuate(START["qi"] + h // 2, dsa_writes(h // 2))
                mix_tile(KT - 1)
                dve.wait_ge(sem["head_done"], HEADS)
                for t, state in ((1, h_prompt), (2, h_sample)):
                    decayed(t)
                    dve.wait_ge(sem["delta_ready"], t + 1)
                    if t == 2:
                        gate_taken(START["gate0b"])
                    for h in range(HEADS):
                        f = slice(64 * h, 64 * h + 64)
                        last = dve.scalar_tensor_tensor(out=state[:, f], in0=state[:, f],
                                                        scalar=chunk_decay[:, h, t - 1:t],
                                                        in1=bank[3 + h // 8][:, 64 * (h % 8):64 * (h % 8) + 64],
                                                        op0=ALU.mult, op1=ALU.add)
                    last.then_inc(sem["h_final"], 1)
                gate_taken(START["gate0b"] + 1)
                norm_split("ssm", "ssm", z, 8, br_hi, br_lo)

                def merge(b):
                    gated = y if b == 0 else gates
                    for c in range(4):
                        n = START[f"branch{b}"] + c
                        s = pair_of(n)
                        dve.wait_ge(sem["chunk_done"], n + 1)
                        for half in range(2):
                            k = 2 * c + half
                            ins = dve.scalar_tensor_tensor(out=gated[:, k, :], in0=gated[:, k, :], scalar=1.0,
                                                           in1=bank[2 * s + half][:, 0:TOK], op0=ALU.add,
                                                           op1=ALU.mult)
                            if b > 0:
                                step(ins)
                                ins = dve.tensor_tensor(y[:, k, :], y[:, k, :], gates[:, k, :], ALU.add)
                            ins.then_inc(sem["merged"], 1)
                        dve.wait_ge(sem["merged"], 8 * b + 2 * c + 2)
                        give_back(n)

                merge(0)
                evacuate(START["vb"], values(v_b, 0))

                for h in range(4):
                    gate_taken(START["gate1"] + h)
                    dve.wait_ge(sem["idx_relu"], h + 1)
                    for j, (r, k0, k1) in enumerate(SPANS):
                        weight = head_cols[0:r, j, 96 + h:97 + h]
                        if h == 0:
                            last = dve.tensor_scalar(score[0:r, k0:k1], score_relu[0:r, 0, k0:k1], weight, None,
                                                     ALU.mult)
                        else:
                            last = dve.scalar_tensor_tensor(out=score[0:r, k0:k1], in0=score_relu[0:r, h % 2, k0:k1],
                                                            scalar=weight, in1=score[0:r, k0:k1], op0=ALU.mult,
                                                            op1=ALU.add)
                    last.then_inc(sem["idx_used"], 1)
                    dve.wait_ge(sem["idx_used"], h + 1)
                dve.memset(score[0:64, 64:128], -BIG)
                step(dve.memset(score[0:64, 320:384], -BIG))
                for r, k0, k1, rounds in ((128, 0, 128, 8), (128, 128, 384, 8), (64, 384, 576, 6)):
                    for _ in range(rounds):
                        step(dve.max(top8[0:r, :], score[0:r, k0:k1]))
                        step(dve.match_replace(score[0:r, k0:k1], top8[0:r, :], score[0:r, k0:k1], GONE))
                for r, k0, k1 in ((128, 0, 384), (64, 384, 576)):
                    last = dve.tensor_scalar(dsa_mask[0:r, k0:k1], score[0:r, k0:k1], GONE / 2, BIG, ALU.is_gt,
                                             ALU.mult)
                last.then_inc(sem["mask_ready"], 1)
                dve.wait_ge(sem["mask_ready"], 1)

                def shifted(c, bias_of):
                    dve.wait_ge(sem["scored"], c + 1)
                    if c >= 2:
                        dve.wait_ge(sem["p_turned"], c - 1)
                    for j, (r, k0, k1) in enumerate(SPANS):
                        src = bank[2 + c % 2][:, k0:k1] if j < 2 else bank[4][0:r, 0:k1 - k0]
                        last = dve.tensor_tensor_reduce(out=logit[0:r, c % 2, k0:k1], in0=src, in1=bias_of(j, r, k0, k1),
                                                        scale=1.0, scalar=3e38, op0=ALU.add, op1=ALU.min,
                                                        accum_out=shift[0:r, c % 2, j:j + 1])
                    last.then_inc(sem["shifted"], 1)

                def attention(first, n_heads, per_tile, bias):
                    shifted(first, bias(0))
                    for h in range(n_heads):
                        c = first + h
                        if h + 1 < n_heads:
                            shifted(c + 1, bias(h + 1))
                        dve.wait_ge(sem["exped"], c + 1)
                        step(dve.reciprocal(denom[:, c % 2, :], denom[:, c % 2, :]))
                        for j, (r, k0, k1) in enumerate(SPANS):
                            last = dve.tensor_scalar(logit[0:r, c % 2, k0:k1], logit[0:r, c % 2, k0:k1],
                                                     denom[0:r, c % 2, j:j + 1], None, ALU.mult)
                        last.then_inc(sem["normed"], 1)
                        if first == 8 and h % 4 == 3:
                            gate_taken(START["gate2"] + h // 4)
                        if h % per_tile == 0 and h >= per_tile:
                            attn_rest(first, h // per_tile - 1)
                    attn_rest(first, n_heads // per_tile - 1)

                def attn_rest(first, tile):
                    dve.wait_ge(sem["attn_hi"], TILE0[first] + tile + 1)
                    dve.tensor_tensor(br_lo[:, tile, :], bank[6 + tile % 2][:, 0:TOK], f32(br_hi[:, tile, :]),
                                      ALU.subtract).then_inc(sem["attn_lo"], 1)

                attention(0, 8, 1, lambda h: lambda j, r, k0, k1: dsa_mask[0:r, k0:k1])
                merge(1)
                dve.wait_ge(sem["attended"], 8)
                dve.wait_ge(sem["k_stored"], 64)
                dve.wait_ge(sem["v_stored"], 32)
                for c in range(4):
                    evacuate(START["kc"] + c, copies(k_c, 2 * c, None))
                for c in range(4):
                    evacuate(START["vc"] + c, values(v_c, 256 * c))
                for c in range(4):
                    evacuate(START["qc"] + c, copies(q_c, 2 * c, -0.125))

                def band(h):
                    at = (128, 0, 0)
                    dve.wait_ge(sem[f"bias_loaded{h % 2}"], 16 * (h // 2 + 1))
                    step(dve.memset(band_bias[0:64, h % 2, 192:256], BIG))
                    return lambda j, r, k0, k1: band_bias[0:r, h % 2, at[j]:at[j] + k1 - k0]

                attention(8, 16, 2, band)
                merge(2)
                for k in range(KT + 1):
                    q = SPLITS["mix"] + k
                    if k < KT:
                        split_source(q, lambda dst: dve.tensor_scalar(dst, y[:, k, :], 0.5, None, ALU.mult))
                    if k >= 1:
                        if k == 1:
                            dve.wait_ge(sem["chunk_done"], START["out"])
                        split_rest(q - 1, br_hi[:, k - 1, :], br_lo[:, k - 1, :])
                for c in range(4):
                    n = START["out"] + c
                    dve.wait_ge(sem["chunk_done"], n + 1)
                    for half in range(2):
                        last = dve.tensor_copy(y[:, 2 * c + half, :], bank[2 * pair_of(n) + half][:, 0:TOK])
                        last.then_inc(sem["y_ready"], 1)
                    dve.wait_ge(sem["y_ready"], YR["mix_post"] + 2 * c + 2)
                    give_back(n)
                add_normed("mix_post", 3, 1.0)
                ffn(1)
                norm_split("ple_pre", "u_ple", x, 6, u_hi, u_lo)
                for c in range(4):
                    n = START["ple"] + 2 * c
                    evacuate(n, copies(y, 2 * c, 0.5))
                    for half in range(2):
                        k, g = 2 * c + half, 24 + 2 * c + half
                        dve.wait_ge(sem["gate_tanh"], g + 1)
                        step(dve.scalar_tensor_tensor(out=y[:, k, :], in0=th[:, g % 2, :], scalar=1.0, in1=y[:, k, :],
                                                      op0=ALU.add, op1=ALU.mult))
                        dve.sem_inc(sem["merged"], 1)
                        dve.sem_inc(sem["y_ready"], 1)
                    give_back(n + 1)
                add_normed("ple_post", 7, 1.0)

        SIZE = {"up": SLOT, "down": HALF_FT * P, "in": SLOT, "misc": SLOT, "gate": SLOT, "branch": SLOT, "out": SLOT,
                "ple": 512, "plegate": SLOT}
        XR = {"ffn0": 0, "mix": 0, "ffn1": 8, "ple": 16}
        YR = {"ffn0_post": 0, "mix_post": 8, "ffn1_post": 16, "ple_post": 24}
        EVAC_ORDER = [n for name, cnt in (("misc", 1), ("xbc", 8), ("z", 4), ("qi", 1), ("kb", 1), ("qb", 4), ("vb", 1),
                                          ("kc", 4), ("vc", 4), ("qc", 4)) for n in range(START[name], START[name] + cnt)]
        EVAC_ORDER += [START["ple"] + 2 * c for c in range(4)]
        EVAC_OF = {n: i for i, n in enumerate(EVAC_ORDER)}
        EVAC = {name: EVAC_OF[START[name]] for name in ("z", "xbc", "misc", "qi", "kb", "vb", "qb", "kc", "vc", "qc")}
        CB_BANK = (5, 6, 7, 2)
        SPANS = ((128, 0, 128), (128, 128, 384), (64, 384, 576))
        TILE0 = {0: 0, 8: 8}

        with nc.Fori(0, DEPTH) as layer:
            with nc.Block() as block:
                layer_body(layer, block)
            nc.all_engine_barrier(sems_to_clear=every)

        with nc.Block() as block:
            @block.tensor
            def _(pe):
                for t, (t0, t1, n) in enumerate(TILES):
                    for b in range(2):
                        for i in range(4):
                            last = pe.transpose(bank[2 * t + b][0:n, P * i:P * (i + 1)], x[:, 4 * b + i, t0:t1],
                                                ident[:])
                        last.then_inc(sem["y_turned"], 1)

            @block.vector
            def _(dve):
                for t, (_, _, n) in enumerate(TILES):
                    for b in range(2):
                        dve.wait_ge(sem["y_turned"], 2 * t + b + 1)
                        dve.tensor_copy(io_rows[0:n, t, 512 * b:512 * (b + 1)], bank[2 * t + b][0:n, :])\
                            .then_inc(sem["y_rows_ready"], 1)

            @block.sync
            def _(sp):
                for t, (_, _, n) in enumerate(TILES):
                    sp.wait_ge(sem["y_rows_ready"], 2 * t + 2)
                    dst = y_p[0, P * t:P * (t + 1)] if t < 2 else y_s[0]
                    sp.dma_start(dst, io_rows[0:n, t, :]).then_inc(sem["y_stored"], 16)
                sp.wait_ge(sem["y_stored"], 48)


INPUTS = ["x_prompt", "x_sample", "p_prompt", "p_sample", "cache_dsa_k", "cache_dsa_v", "cache_idx_k",
          "cache_band_k", "cache_band_v", "state_ssm", "state_conv", "norm_g", "ffn_w13", "ffn_w2", "w_in", "conv_w",
          "conv_b", "dt_bias", "a_log", "d_skip", "ssm_norm_g", "rel_bias", "w_gate", "b_gate", "w_branch", "w_out",
          "w_ple", "w_ple_gate"]
OUTPUTS = [
    ("y_prompt", (1, SEQ, D), (1, SEQ, D)), ("y_sample", (1, DEC, D), (1, DEC, D)),
    ("dsa_k_p", (DEPTH, 1, SEQ, 256), (DEPTH, 1, SEQ, 2, 128)), ("dsa_v_p", (DEPTH, 1, SEQ, 256), (DEPTH, 1, SEQ, 2, 128)),
    ("idx_k_p", (DEPTH, 1, SEQ, 64), (DEPTH, 1, SEQ, 64)),
    ("band_k_p", (DEPTH, 1, SEQ, D), (DEPTH, 1, SEQ, 16, 64)), ("band_v_p", (DEPTH, 1, SEQ, D), (DEPTH, 1, SEQ, 16, 64)),
    ("ssm_p", (DEPTH, 1, 16, 64, 128), (DEPTH, 1, 16, 64, 128)), ("conv_p", (DEPTH, 1, 3, CONV_CH), (DEPTH, 1, 3, CONV_CH)),
    ("dsa_k_s", (DEPTH, 1, DEC, 256), (DEPTH, 1, DEC, 2, 128)), ("dsa_v_s", (DEPTH, 1, DEC, 256), (DEPTH, 1, DEC, 2, 128)),
    ("idx_k_s", (DEPTH, 1, DEC, 64), (DEPTH, 1, DEC, 64)),
    ("band_k_s", (DEPTH, 1, DEC, D), (DEPTH, 1, DEC, 16, 64)), ("band_v_s", (DEPTH, 1, DEC, D), (DEPTH, 1, DEC, 16, 64)),
    ("ssm_s", (DEPTH, 1, 16, 64, 128), (DEPTH, 1, 16, 64, 128)), ("conv_s", (DEPTH, 1, 3, CONV_CH), (DEPTH, 1, 3, CONV_CH)),
]


def kernel(**inputs):
    import concourse.bacc as bacc
    from concourse.bass_utils import run_bass_kernel_spmd

    nc = bacc.Bacc("TRN2", target_bir_lowering=False, num_devices=1)
    arrays, aps = {}, {}
    for name in INPUTS:
        array = np.ascontiguousarray(inputs[name])
        arrays[f"in_{name}"] = array
        aps[name] = nc.dram_tensor(f"in_{name}", array.shape, mybir.dt.from_np(array.dtype), kind="ExternalInput").ap()
    outs = [nc.dram_tensor(f"out_{name}", shape, F32, kind="ExternalOutput").ap() for name, shape, _ in OUTPUTS]
    bias_line = nc.dram_tensor("bias_line", (HEADS, 512), F32).ap()
    bias_square = nc.dram_tensor("bias_square", (HEADS, P, 256), F32).ap()
    build(nc, aps, outs, bias_line, bias_square)
    r = run_bass_kernel_spmd(nc, [arrays], core_ids=[0])
    return tuple(r.results[0][f"out_{name}"].reshape(final) for name, _, final in OUTPUTS)
```

```python
from contextlib import ExitStack

import numpy as np
import concourse.bass as bass
from concourse import mybir

F32 = mybir.dt.float32
F32R = mybir.dt.float32r
I32 = mybir.dt.int32
ALU = mybir.AluOpType
ACT = mybir.ActivationFunctionType

P = 128
DEPTH, SEQ, DEC, PAST, D = 2, 256, 64, 128, 1024
TOK = SEQ + DEC
KT = D // P
D_FF = 2816
FT = D_FF // P
HALF_FT = FT // 2
PLE = 256
CONV_CH = 2048
CT = CONV_CH // P
HEADS = 16
D_STATE = 128
GROUPS = 4
IN_W = 8020
Z0, XBC0, DT0, QB0, KB0, VB0, QI0, KI0, WI0, QC0, KC0, VC0 = (
    0, 1024, 3072, 3088, 4112, 4368, 4624, 4880, 4944, 4948, 5972, 6996)
XP = SEQ + 3 + DEC + 3
CONV_N = XP - 3
RING = 3
SLOT = 2048
EPS = 1e-6
BIG = 1e30
GONE = -3e38
RSQRT_SEED = 1597463007.0
TILES = ((0, 128, 128), (128, 256, 128), (256, 320, 64))
STAT_TILES = (0, 128, 192)


def f32(ap):
    return ap.bitcast(F32)


def plan_chunks():
    chunks, start = [], {}

    def section(name, items):
        start[name] = len(chunks)
        chunks.extend(items)

    def ffn(which):
        section(f"up{which}", [("up", which, j) for j in range(FT)])
        section(f"down{which}", [("down", which, j, half) for j in range(KT) for half in range(2)])

    ffn(0)
    section("misc", [("misc",)])
    section("xbc", [("in", XBC0 + 256 * c) for c in range(8)])
    section("z", [("in", Z0 + 256 * c) for c in range(4)])
    section("gate0", [("gate", 0, c) for c in range(2)])
    section("qi", [("in", QI0)])
    section("kb", [("in", KB0)])
    section("qb", [("in", QB0 + 256 * c) for c in range(4)])
    section("gate0b", [("gate", 0, c) for c in (2, 3)])
    section("branch0", [("branch", 0, c) for c in range(4)])
    section("vb", [("in", VB0)])
    section("gate1", [("gate", 1, c) for c in range(4)])
    section("branch1", [("branch", 1, c) for c in range(4)])
    section("kc", [("in", KC0 + 256 * c) for c in range(4)])
    section("vc", [("in", VC0 + 256 * c) for c in range(4)])
    section("qc", [("in", QC0 + 256 * c) for c in range(4)])
    section("gate2", [("gate", 2, c) for c in range(4)])
    section("branch2", [("branch", 2, c) for c in range(4)])
    section("out", [("out", c) for c in range(4)])
    ffn(1)
    section("ple", [("ple", c) for c in range(4)])
    section("plegate", [("plegate", c) for c in range(4)])
    return chunks, start


CHUNKS, START = plan_chunks()
N_CHUNKS = len(CHUNKS)


def loads_of(n):
    return {"up": 2, "misc": 5}.get(CHUNKS[n][0], 1)


def loaded_count(n):
    return 16 * sum(loads_of(m) for m in range(n % RING, n + 1, RING))


def pair_of(n):
    if CHUNKS[n][0] in ("up", "down"):
        return n % RING
    if START["gate0"] <= n < START["branch0"] or START["gate2"] <= n < START["branch2"]:
        return 0
    if START["branch0"] <= n < START["branch1"]:
        return 3 * (n % 2)
    return n % 2


def frees(n):
    return not (CHUNKS[n][0] == "down" and CHUNKS[n][3] == 1)


def freed_before(n):
    return sum(frees(m) for m in range(n) if pair_of(m) == pair_of(n))


def build(nc, a, outs, bias_line, bias_square):
    (y_p, y_s, dsa_k_p, dsa_v_p, idx_k_p, band_k_p, band_v_p, ssm_p, conv_p,
     dsa_k_s, dsa_v_s, idx_k_s, band_k_s, band_v_s, ssm_s, conv_s) = outs
    with ExitStack() as ctx:
        def sb(name, shape, dt=F32, stack=ctx):
            return stack.enter_context(nc.sbuf_tensor(name, shape, dt))

        bank = [ctx.enter_context(nc.psum_tensor(f"bank{i}", [P, 512], F32)) for i in range(8)]
        stat_bank, row_bank = bank[6], bank[7]

        stage = sb("stage", [P, RING, SLOT])
        w_hi = sb("w_hi", [P, RING, SLOT], F32R)
        w_lo = sb("w_lo", [P, RING, SLOT], F32R)
        x = sb("x", [P, KT, TOK])
        y = sb("y", [P, KT, TOK])
        u_hi = sb("u_hi", [P, KT, TOK], F32R)
        u_lo = sb("u_lo", [P, KT, TOK], F32R)
        ident = sb("ident", [P, P])
        ones = sb("ones", [P, 1])
        tri = sb("tri", [P, P])
        conv_cols = sb("conv_cols", [P, CT, 8])
        gain_cols = sb("gain_cols", [P, KT, 12])
        head_rows = sb("head_rows", [P, TOK])
        head_cols = sb("head_cols", [P, 3, P])
        d_col = sb("d_col", [P, KT])
        dt_bias = sb("dt_bias", [HEADS, 1])
        neg_a = sb("neg_a", [HEADS, 1])
        square_total = sb("square_total", [P, 2, TOK])
        rms_row = sb("rms_row", [P, TOK])
        split_tmp = sb("split_tmp", [P, RING, TOK])
        square = split_tmp[:, 0:2, :]
        rs = sb("rs", [P, 5, 12])
        shift = sb("shift", [P, 2, 3])
        denom = sb("denom", [P, 2, 3])
        chunk_decay = sb("chunk_decay", [P, HEADS, 2])

        with ExitStack() as region:
            h_hi = sb("h_hi", [P, FT, TOK], F32R, region)
            h_lo = sb("h_lo", [P, FT, TOK], F32R, region)
            th = sb("th", [P, RING, TOK], F32, region)
            p_rows = sb("p_rows", [P, 3, PLE], F32, region)
            p_hi = sb("p_hi", [P, 2, TOK], F32R, region)
            p_lo = sb("p_lo", [P, 2, TOK], F32R, region)
            conv_rows = sb("conv_rows", [8, CONV_CH], F32, region)
            gain_rows = sb("gain_rows", [12, D], F32, region)
            bias_rows = sb("bias_rows", [P, 4, HEADS], F32, region)
            bias_rev = sb("bias_rev", [HEADS, 512], F32, region)
        with ExitStack() as region:
            embedded = sb("embedded", [P, KT, TOK], F32, region)
        with ExitStack() as region:
            io_rows = sb("io_rows", [P, 3, D], F32, region)
        with ExitStack() as region:
            ki = sb("ki", [P, TOK], F32, region)
            with ExitStack() as over:
                br_hi = sb("br_hi", [P, KT, TOK], F32R, over)
                br_lo = sb("br_lo", [P, KT, TOK], F32R, over)
                band_bias = sb("band_bias", [P, 2, 256], F32, over)
            with ExitStack() as mamba:
                conv_tail = sb("conv_tail", [70, CONV_CH], F32, mamba)
            xdt = sb("xdt", [P, 3, D], F32, region)
            b_rows = sb("b_rows", [P, 3, GROUPS * D_STATE], F32, region)
            xdec = sb("xdec", [P, D], F32, region)
            with ExitStack() as mamba:
                z = sb("z", [P, KT, TOK], F32, mamba)
                xbc = sb("xbc", [P, CT, XP], F32, mamba)
                h_sample = sb("h_sample", [P, D], F32, mamba)
                with ExitStack() as early:
                    state_rows = sb("state_rows", [P, KT, P], F32, early)
                with ExitStack() as early:
                    conv_acc = sb("conv_acc", [P, 2, CONV_N], F32, early)
                    conv_th = sb("conv_th", [P, 2, CONV_N], F32, early)
                    dt_tmp = sb("dt_tmp", [HEADS, 3, TOK], F32, early)
                h_prompt = sb("h_prompt", [P, D], F32, mamba)
                row_exp = sb("row_exp", [P, 2, TOK], F32, mamba)
                seg = sb("seg", [P, 2, TOK], F32, mamba)
                cb = xbc[:, CT - 2 * GROUPS:CT - GROUPS, :]
                h_rows = cb[:, :, 0:2 * P]
                q_b = sb("q_b", [P, KT, TOK], F32, mamba)
                k_b = sb("k_b", [P, 2, TOK], F32, mamba)
                q_i = sb("q_i", [P, 2, TOK], F32, mamba)
            attn = region.enter_context(ExitStack())
            logit = sb("logit", [P, 2, 576], F32, attn)
            prob_t = sb("prob_t", [P, 2, 512], F32, attn)
            gates = sb("gates", [P, KT, TOK], F32, attn)
            k_c_rows = prob_t[:].rearrange("p c k -> p (c k)")
            with ExitStack() as dsa:
                v_b = sb("v_b", [P, 3, 256], F32, dsa)
                v_b_past = sb("v_b_past", [P, 256], F32, dsa)
                k_b_past = sb("k_b_past", [P, 384], F32, dsa)
                k_b_past_t = sb("k_b_past_t", [P, 3, PAST], F32, dsa)
                k_b_rows = sb("k_b_rows", [P, 3, 320], F32, dsa)
                score = sb("score", [P, 576], F32, dsa)
                score_relu = sb("score_relu", [P, 2, 576], F32, dsa)
                top8 = sb("top8", [P, 3, 8], F32, dsa)
                dsa_mask = sb("dsa_mask", [P, 576], F32, dsa)
            with ExitStack() as band:
                q_c = sb("q_c", [P, KT, TOK], F32, band)
                k_c = sb("k_c", [P, KT, TOK], F32, band)
                v_c = sb("v_c", [P, 3, D], F32, band)
                v_c_past = sb("v_c_past", [P, D], F32, band)
                k_c_past_t = sb("k_c_past_t", [P, KT, PAST], F32, band)

        names = [
            "loaded0", "loaded1", "loaded2", "w_hi_ready", "w_lo_ready", "chunk_done", "bank_free0", "bank_free1",
            "bank_free2", "bank_free3", "rows_loaded", "gains_loaded", "gains_turned", "p_loaded",
            "per_layer_turned", "rows_turned", "cols_ready", "p_ready", "bias_rev_ready", "bias_written",
            "bias_squared", "square_ready", "square_summed", "square_used", "rms_ready", "row_ready",
            "rms_row_ready", "y_normed", "u_hi_ready", "u_lo_ready", "gate_scaled", "b_scaled", "split_src",
            "split_hi", "split_lo", "tanh_ready", "silu_ready", "x_ready", "y_ready", "dve_step", "act_step",
            "pool_step", "evac", "z_tanh", "z_done", "tail_turned", "tail_copied", "tail_stored", "conv_base",
            "conv_ready", "conv_tanh", "conv_done", "dt_v", "dt_exp", "dt_done", "decay_done", "rows_cols_turned",
            "head_cols_ready", "state_loaded", "state_turned", "state_ready", "xs_turned", "xdt_ready", "b_turned",
            "b_ready", "cb_ready", "cb_masked", "xdec_ready", "delta_ready", "h1_ready", "bc_ready",
            "row_exp_ready", "seg_ready", "seg_exp", "mt_ready", "head_done", "mixed", "h_final", "h_turned",
            "h_rows_ready", "h_stored", "k_past_loaded", "v_past_loaded", "past_turned", "past_ready", "k_turned",
            "k_rows_ready", "k_stored", "v_stored", "idx_ready", "idx_relu", "idx_used", "mask_ready", "scored",
            "shifted", "exped", "normed", "p_turned", "p_copied", "attended", "attn_hi", "attn_lo", "bias_loaded0",
            "bias_loaded1", "gate_tanh", "merged", "x_loaded", "x_turned", "y_turned", "y_rows_ready", "y_stored",
            "setup"]
        sem = {name: ctx.enter_context(nc.semaphore(name)) for name in names}
        every = range(min(s.num for s in sem.values()), max(s.num for s in sem.values()) + 1)
        assert len(every) == len(names)
        loaded = [sem[f"loaded{s}"] for s in range(RING)]
        bank_free = [sem[f"bank_free{pair}"] for pair in range(4)]

        class Chain:

            def __init__(self, engine, semaphore):
                self.engine, self.semaphore, self.count = engine, semaphore, 0

            def __call__(self, instruction):
                self.count += 1
                instruction.then_inc(self.semaphore, 1)
                self.engine.wait_ge(self.semaphore, self.count)

        with nc.Block() as block:
            @block.sync
            def _(sp):
                sp.dma_start(io_rows[:, 0:2, :], a["x_prompt"][0].rearrange("(t p) d -> p t d", p=P))\
                    .then_inc(sem["x_loaded"], 16)
                sp.dma_start(io_rows[0:DEC, 2, :], a["x_sample"][0]).then_inc(sem["x_loaded"], 16)

            @block.gpsimd
            def _(pool):
                pool.memset(ident[:], 0.0).then_inc(sem["pool_step"], 1)
                pool.memset(ones[:], 1.0).then_inc(sem["pool_step"], 1)
                pool.memset(tri[:], 1.0).then_inc(sem["pool_step"], 1)
                pool.memset(head_rows[:], 0.0).then_inc(sem["pool_step"], 1)
                pool.memset(shift[:], 0.0).then_inc(sem["pool_step"], 1)
                pool.memset(denom[:], 1.0).then_inc(sem["pool_step"], 1)
                pool.wait_ge(sem["pool_step"], 3)
                pool.affine_select(out=ident[:], in_=ident[:], compare_op=ALU.not_equal, fill=1.0, base=0,
                                   pattern=[[-1, P]], channel_multiplier=1).then_inc(sem["setup"], 1)
                pool.affine_select(out=tri[:], in_=tri[:], compare_op=ALU.is_ge, fill=0.0, base=0,
                                   pattern=[[1, P]], channel_multiplier=-1).then_inc(sem["setup"], 1)

            @block.tensor
            def _(pe):
                pe.wait_ge(sem["setup"], 1)
                pe.wait_ge(sem["x_loaded"], 32)
                for k in range(KT):
                    for t, (t0, t1, n) in enumerate(TILES):
                        last = pe.transpose(bank[k][:, t0:t1], io_rows[0:n, t, P * k:P * (k + 1)], ident[0:n, 0:n])
                    last.then_inc(sem["x_turned"], 1)

            @block.vector
            def _(dve):
                for k in range(KT):
                    dve.wait_ge(sem["x_turned"], k + 1)
                    dve.tensor_copy(x[:, k, :], bank[k][:, 0:TOK]).then_inc(sem["dve_step"], 1)

        nc.all_engine_barrier(sems_to_clear=every)

        NORMS = [("ffn0_pre", 1), ("ffn0_post", 1), ("mix_pre", 1), ("ssm", 4), ("mix_post", 1), ("ffn1_pre", 1),
                 ("ffn1_post", 1), ("ple_pre", 1), ("ple_post", 1)]
        NORM = {name: i for i, (name, _) in enumerate(NORMS)}
        ROW_BANKS = {1: [7], 4: [2, 3, 4, 5]}
        GROUPS_BEFORE = [sum(g for _, g in NORMS[:i]) for i in range(len(NORMS) + 1)]
        SUMS_BEFORE = [sum(KT - g for _, g in NORMS[:i]) for i in range(len(NORMS) + 1)]

        def square_place(name, k):
            i = NORM[name]
            groups = NORMS[i][1]
            g, first = k * groups // KT, k % (KT // groups) == 0
            return GROUPS_BEFORE[i] + g, first, SUMS_BEFORE[i] + k - g - 1

        U = {"ffn0": 0, "mix": KT, "merged": 2 * KT, "ffn1": 3 * KT, "ple": 4 * KT}
        SPLITS = {}
        count = 0
        for name, n in (("h0", FT), ("ssm", KT), ("h1", FT)):
            SPLITS[name] = count
            count += n

        def layer_body(layer, block):
            @block.sync
            def _(sp):
                def load_chunk(n, up_tile=None, loop=None):
                    kind, s = CHUNKS[n], n % RING
                    if loop is not None:
                        j = up_tile
                        src = a["ffn_w13"][layer, kind[1]].rearrange("(k p) (h j c) -> p k h j c", p=P, h=2, c=P)
                        parts = [(stage[:, s, 0:SLOT].rearrange("p (k h c) -> p k h c", h=2, c=P)[:, :, h, :],
                                  src[:, :, h, bass.ds(j, 1), :].rearrange("p k j c -> p k (j c)"))
                                 for h in range(2)]
                        sp.wait_ge(sem["w_lo_ready"], n - RING + 1 + RING * loop)
                        for dst, src_part in parts:
                            sp.dma_start(dst, src_part).then_inc(loaded[s], 16)
                        return
                    if n >= RING:
                        sp.wait_ge(sem["w_lo_ready"], n - RING + 1)
                    cols = stage[:, s, 0:SLOT].rearrange("p (k c) -> p k c", c=256)
                    if kind[0] == "up":
                        src = a["ffn_w13"][layer, kind[1]].rearrange("(k p) (h j c) -> p k h j c", p=P, h=2, c=P)
                        dst = stage[:, s, 0:SLOT].rearrange("p (k h c) -> p k h c", h=2, c=P)
                        for h in range(2):
                            sp.dma_start(dst[:, :, h, :], src[:, :, h, kind[2], :]).then_inc(loaded[s], 16)
                    elif kind[0] == "down":
                        src = a["ffn_w2"][layer, kind[1]].rearrange("(k p) (j c) -> p k j c", p=P, c=P)
                        sp.dma_start(stage[:, s, 0:HALF_FT * P].rearrange("p (k c) -> p k c", c=P),
                                     src[:, HALF_FT * kind[3]:HALF_FT * (kind[3] + 1), kind[2], :])\
                            .then_inc(loaded[s], 16)
                    elif kind[0] == "misc":
                        src = a["w_in"][layer].rearrange("(k p) c -> p k c", p=P)
                        for dst, c, w in ((0, KI0, 64), (64, KI0, 64), (128, DT0, 32), (160, WI0, 32), (192, DT0, 64)):
                            sp.dma_start(cols[:, :, dst:dst + w], src[:, :, c:c + w]).then_inc(loaded[s], 16)
                    elif kind[0] == "ple":
                        src = a["w_ple"][layer].rearrange("(k p) (j c) -> p k j c", p=P, c=256)
                        sp.dma_start(cols[:, 0:2, :], src[:, :, kind[1], :]).then_inc(loaded[s], 16)
                    else:
                        if kind[0] == "in":
                            src, c = a["w_in"][layer], kind[1]
                        elif kind[0] == "gate":
                            src, c = a["w_gate"][layer], kind[1] * D + 256 * kind[2]
                        elif kind[0] == "branch":
                            src, c = a["w_branch"][layer, kind[1]], 256 * kind[2]
                        elif kind[0] == "out":
                            src, c = a["w_out"][layer], 256 * kind[1]
                        else:
                            src, c = a["w_ple_gate"][layer], 256 * kind[1]
                        sp.dma_start(cols, src.rearrange("(k p) c -> p k c", p=P)[:, :, c:c + 256])\
                            .then_inc(loaded[s], 16)

                def load_ffn(which):
                    n0 = START[f"up{which}"]
                    for n in range(n0 + 2 * (1 - which), n0 + RING):
                        load_chunk(n)
                    if which == 1:
                        sp.wait_ge(sem["chunk_done"], START["up1"])
                        sp.wait_ge(sem["v_stored"], 64)
                        sp.wait_ge(sem["k_stored"], 112)
                        sp.dma_start(p_rows[:, 0:2, :], a["p_prompt"][layer, 0].rearrange("(t p) c -> p t c", p=P))\
                            .then_inc(sem["p_loaded"], 16)
                        sp.dma_start(p_rows[0:DEC, 2, :], a["p_sample"][layer, 0]).then_inc(sem["p_loaded"], 16)
                    if which == 0:
                        sp.wait_ge(sem["bias_rev_ready"], 1)
                        sp.dma_start(bias_line, bias_rev[:]).then_inc(sem["bias_written"], 16)
                    with sp.Fori(1, 6) as i:
                        for s in range(RING):
                            load_chunk(n0 + s, up_tile=i * RING + s, loop=i)
                    for n in range(n0 + 6 * RING, START[f"down{which}"] + 2 * KT):
                        load_chunk(n)

                sp.dma_start(gain_rows[0:8, :], a["norm_g"][layer]).then_inc(sem["gains_loaded"], 16)
                load_chunk(0)
                load_chunk(1)
                rows = sem["rows_loaded"]
                sp.dma_start(conv_rows[0:4, :], a["conv_w"][layer]).then_inc(rows, 16)
                sp.dma_start(conv_rows[4:5, :], a["conv_b"][layer].unsqueeze(0)).then_inc(rows, 16)
                sp.dma_start(conv_rows[5:8, :], a["state_conv"][layer, 0]).then_inc(rows, 16)
                sp.dma_start(gain_rows[8:9, :], a["ssm_norm_g"][layer].unsqueeze(0)).then_inc(rows, 16)
                sp.dma_start(gain_rows[9:12, :], a["b_gate"][layer].rearrange("(r c) -> r c", c=D)).then_inc(rows, 16)
                sp.dma_start(bias_rows[:], a["rel_bias"][layer, 0:512].rearrange("(j p) h -> p j h", p=P))\
                    .then_inc(rows, 16)
                sp.dma_start(dt_bias[:], a["dt_bias"][layer].unsqueeze(1)).then_inc(rows, 16)
                sp.dma_start(neg_a[:], a["a_log"][layer].unsqueeze(1)).then_inc(rows, 16)
                skip = a["d_skip"][layer].rearrange("(i h) -> h i", h=2)
                for half in range(2):
                    sp.dma_start(d_col[64 * half:64 * (half + 1), :], skip[half:half + 1, :].broadcast_to([64, KT]),
                                 allow_slow_non_contiguous=True)\
                        .then_inc(rows, 16)
                load_ffn(0)
                sp.wait_ge(sem["bias_written"], 16)
                sp.dma_start(bias_square, bass.AP(bias_line.tensor, 127, [[512, HEADS], [-1, P], [1, 256]]))\
                    .then_inc(sem["bias_squared"], 16)
                for n in range(START["misc"], START["misc"] + 2):
                    load_chunk(n)
                sp.wait_ge(sem["chunk_done"], START["misc"])
                sp.dma_start(state_rows[:], a["state_ssm"][layer, 0].rearrange("(i h) d n -> (h d) i n", h=2))\
                    .then_inc(sem["state_loaded"], 16)
                for n in range(START["misc"] + 2, START["gate0"] + 2):
                    load_chunk(n)
                sp.wait_ge(sem["tail_copied"], 4)
                sp.dma_start(conv_p[layer, 0], conv_tail[0:3, :]).then_inc(sem["tail_stored"], 16)
                sp.dma_start(conv_s[layer, 0], conv_tail[67:70, :]).then_inc(sem["tail_stored"], 16)
                for n in range(START["gate0"] + 2, START["branch0"] + 2):
                    load_chunk(n)
                for b, dst in enumerate((ssm_p, ssm_s)):
                    sp.wait_ge(sem["h_rows_ready"], 2 * b + 2)
                    for i in range(2):
                        sp.dma_start(dst[layer, 0].rearrange("(c i h) d n -> i (h d) c n", c=GROUPS, h=2)[i],
                                     h_rows[:, :, P * i:P * (i + 1)]).then_inc(sem["h_stored"], 16)
                sp.wait_ge(sem["h_stored"], 64)
                ck = a["cache_dsa_k"][layer, 0].rearrange("t g d -> t (g d)")
                cv = a["cache_dsa_v"][layer, 0].rearrange("t g d -> t (g d)")
                sp.dma_start(k_b_past[:, 0:256], ck).then_inc(sem["k_past_loaded"], 16)
                for c in range(2):
                    sp.dma_start(k_b_past[:, 256 + 64 * c:320 + 64 * c], a["cache_idx_k"][layer, 0])\
                        .then_inc(sem["k_past_loaded"], 16)
                sp.dma_start(v_b_past[:], cv).then_inc(sem["v_past_loaded"], 16)
                for n in range(START["branch0"] + 2, START["gate1"] + 2):
                    load_chunk(n)

                def store_tokens(src, prompt, sample, signal, rows_at=0):
                    sp.dma_start(prompt[layer, 0].rearrange("(t p) c -> p t c", p=P), src[:, 0:2]).then_inc(signal, 16)
                    sp.dma_start(sample[layer, 0], src[rows_at:rows_at + DEC, 2]).then_inc(signal, 16)

                sp.wait_ge(sem["k_rows_ready"], 3)
                store_tokens(k_b_rows[:, :, 0:256], dsa_k_p, dsa_k_s, sem["k_stored"])
                store_tokens(k_b_rows[:, :, 256:320], idx_k_p, idx_k_s, sem["k_stored"])
                sp.wait_ge(sem["evac"], EVAC["vb"] + 1)
                store_tokens(v_b[:], dsa_v_p, dsa_v_s, sem["v_stored"], 64)
                for n in range(START["gate1"] + 2, START["branch1"] + 2):
                    load_chunk(n)
                sp.wait_ge(sem["k_stored"], 64)
                sp.wait_ge(sem["v_stored"], 32)
                sp.wait_ge(sem["attended"], KT)
                sp.wait_ge(sem["bias_squared"], 16)
                sp.dma_start(k_c_rows, a["cache_band_k"][layer, 0].rearrange("t h d -> t (h d)"))\
                    .then_inc(sem["k_past_loaded"], 16)
                sp.dma_start(v_c_past[:], a["cache_band_v"][layer, 0].rearrange("t h d -> t (h d)"))\
                    .then_inc(sem["v_past_loaded"], 16)
                for n in range(START["branch1"] + 2, START["gate2"] + 2):
                    load_chunk(n)
                    t = n - (START["qc"] + 3)
                    if 0 <= t < 3:
                        sp.wait_ge(sem["k_rows_ready"], 3 + 2 * (t + 1))
                        dst = band_k_p[layer, 0, P * t:P * (t + 1)] if t < 2 else band_k_s[layer, 0]
                        sp.dma_start(dst, k_c_rows[0:TILES[t][2], :]).then_inc(sem["k_stored"], 16)
                for h in range(HEADS):
                    if h >= 2:
                        sp.wait_ge(sem["shifted"], 8 + h - 1)
                    sp.dma_start(band_bias[:, h % 2, :], bias_square[h]).then_inc(sem[f"bias_loaded{h % 2}"], 16)
                    if h % 4 == 3:
                        load_chunk(START["gate2"] + 2 + h // 4)
                store_tokens(v_c[:], band_v_p, band_v_s, sem["v_stored"], 64)
                for n in range(START["gate2"] + 6, START["up1"]):
                    load_chunk(n)
                load_ffn(1)
                for n in range(START["ple"], N_CHUNKS):
                    load_chunk(n)
                sp.wait_ge(sem["tail_stored"], 32)
                sp.wait_ge(sem["k_stored"], 112)

            @block.gpsimd
            def _(pool):
                def rest(n, loop=None):
                    s = n % RING
                    size = SIZE[CHUNKS[n][0]]
                    pool.wait_ge(sem["w_hi_ready"], n + 1 if loop is None else n + 1 + RING * loop)
                    pool.tensor_tensor(w_lo[:, s, 0:size], stage[:, s, 0:size], f32(w_hi[:, s, 0:size]), ALU.subtract)\
                        .then_inc(sem["w_lo_ready"], 1)

                def rest_ffn(which):
                    n0 = START[f"up{which}"]
                    if which == 0:
                        pool.wait_ge(sem["w_lo_ready"], 1)
                    for n in range(n0 + 1 + which, n0 + RING):
                        rest(n)
                    with pool.Fori(1, 6) as i:
                        for s in range(RING):
                            rest(n0 + s, loop=i)
                    for n in range(n0 + 6 * RING, START[f"down{which}"] + 2 * KT):
                        rest(n)

                def add_to_x(number):
                    for k in range(KT if number < 3 else POOL_TILES):
                        pool.wait_ge(sem["y_normed"], KT * number + k + 1)
                        pool.tensor_tensor(x[:, k, :], x[:, k, :], y[:, k, :], ALU.add).then_inc(sem["x_ready"], 1)

                rest_ffn(0)
                rest(START["misc"])
                rest(START["misc"] + 1)
                add_to_x(0)
                for n in range(START["misc"] + 2, START["up1"] + 2):
                    rest(n)
                add_to_x(1)
                rest_ffn(1)
                for n in range(START["ple"], START["plegate"] + 1):
                    rest(n)
                add_to_x(2)
                for n in range(START["plegate"] + 1, N_CHUNKS):
                    rest(n)
                add_to_x(3)

            @block.scalar
            def _(act):
                step = Chain(act, sem["act_step"])

                def heads(n, loop=None):
                    if n >= N_CHUNKS:
                        return
                    s = n % RING
                    size = SIZE[CHUNKS[n][0]]
                    if loop is None:
                        act.wait_ge(loaded[s], loaded_count(n))
                        if n >= RING:
                            act.wait_ge(sem["chunk_done"], n - RING + 1)
                    else:
                        act.wait_ge(loaded[s], loaded_count(n) + 32 * loop)
                        act.wait_ge(sem["chunk_done"], n - RING + 1 + RING * loop)
                    act.activation(w_hi[:, s, 0:size], stage[:, s, 0:size], ACT.Copy).then_inc(sem["w_hi_ready"], 1)

                def square_of(norm, k, src):
                    group, first, number = square_place(norm, k)
                    if first:
                        if group >= 2:
                            act.wait_ge(sem["square_used"], group - 1)
                        dst = square_total[:, group % 2, :]
                    else:
                        if number >= 2:
                            act.wait_ge(sem["square_summed"], number - 1)
                        dst = square[:, number % 2, :]
                    act.activation(dst, src[:, k, :], ACT.Square).then_inc(sem["square_ready"], 1)

                def x_heads(section, gain):
                    for k in range(KT):
                        if section != "ffn0":
                            act.wait_ge(sem["x_ready"], XR[section] + k + 1)
                        act.activation(u_hi[:, k, :], x[:, k, :], ACT.Copy, scale=gain_cols[:, k, gain:gain + 1])\
                            .then_inc(sem["u_hi_ready"], 1)
                        if section == "ffn0" and k in (1, KT - 1):
                            heads(k // (KT - 1))
                    for k in range(KT):
                        square_of({"mix": "mix_pre", "ple": "ple_pre"}.get(section, section + "_pre"), k, x)

                def split_head(q, dst):
                    act.wait_ge(sem["split_src"], q + 1)
                    act.activation(dst, split_tmp[:, q % RING, :], ACT.Copy).then_inc(sem["split_hi"], 1)

                def split_heads(name, dst):
                    for k in range(KT):
                        split_head(SPLITS[name] + k, dst[:, k, :])

                def up_chunk(which, j, loop=None):
                    n = START[f"up{which}"] + j
                    s, more = n % RING, 0 if loop is None else RING * loop
                    act.wait_ge(sem["gate_scaled"], FT * which + j + 1 + more)
                    act.activation(th[:, s, :], split_tmp[:, (SPLITS[f"h{which}"] + j) % RING, :], ACT.Tanh, scale=0.5)\
                        .then_inc(sem["tanh_ready"], 1)
                    q = SPLITS[f"h{which}"] + j
                    act.wait_ge(sem["split_src"], q + 1 + more)
                    dst = h_hi[:, j, :] if loop is None else \
                        h_hi[:, bass.ds(loop * RING + j, 1), :].rearrange("p j t -> p (j t)")
                    act.activation(dst, split_tmp[:, q % RING, :], ACT.Copy).then_inc(sem["split_hi"], 1)

                def ffn(which):
                    n0 = START[f"up{which}"]
                    x_heads(f"ffn{which}", 4 * which)
                    if which == 0:
                        act.wait_ge(sem["rows_turned"], 1)
                        act.activation(bias_rev[:, ::-1], bank[4][0:HEADS, :], ACT.Copy, scale=-1.0)\
                            .then_inc(sem["bias_rev_ready"], 1)
                        step(act.activation(neg_a[:], neg_a[:], ACT.Exp))
                    for j in range(RING):
                        heads(n0 + j + 2)
                        up_chunk(which, j)
                    if which == 1:
                        act.wait_ge(sem["per_layer_turned"], 1)
                        for k in range(2):
                            act.activation(p_hi[:, k, :], bank[6 + k][:, 0:TOK], ACT.Copy).then_inc(sem["p_ready"], 1)
                    with act.Fori(1, 6) as i:
                        for j in range(RING):
                            heads(n0 + j + 2, loop=i)
                            up_chunk(which, j, loop=i)
                    for j in range(6 * RING, FT):
                        heads(n0 + j + 2)
                        up_chunk(which, j)
                    n1 = START[f"down{which}"]
                    for n in range(n1, n1 + 2 * KT):
                        heads(n + 2)
                        if (n - n1) % 2 == 1 and n - n1 > 1:
                            square_y(f"ffn{which}_post", (n - n1) // 2 - 1)
                    square_y(f"ffn{which}_post", KT - 1)

                def square_y(norm, k):
                    act.wait_ge(sem["y_ready"], YR[norm] + k + 1)
                    square_of(norm, k, y)

                act.wait_ge(sem["cols_ready"], 1)
                ffn(0)

                x_heads("mix", 2)
                act.wait_ge(sem["state_turned"], 1)
                for b in range(2):
                    act.activation(h_sample[:, 512 * b:512 * (b + 1)], bank[4 + b][:], ACT.Copy)\
                        .then_inc(sem["state_ready"], 1)
                heads(START["misc"] + 2)
                act.wait_ge(sem["dt_v"], 1)
                step(act.activation(dt_tmp[:, 1, :], dt_tmp[:, 1, :], ACT.Exp))
                act.activation(dt_tmp[:, 1, :], dt_tmp[:, 1, :], ACT.Ln, bias=1.0).then_inc(sem["dt_exp"], 1)

                def conv_pair(c):
                    for i in (2 * c, 2 * c + 1):
                        act.wait_ge(sem["evac"], EVAC["xbc"] + c + 1)
                        if i >= 2:
                            act.wait_ge(sem["conv_done"], i - 1)
                        act.activation(conv_acc[:, i % 2, :], xbc[:, i, 0:CONV_N], ACT.Identity,
                                       scale=conv_cols[:, i, 0:1], bias=conv_cols[:, i, 4:5])\
                            .then_inc(sem["conv_base"], 1)
                    for i in (2 * c, 2 * c + 1):
                        act.wait_ge(sem["conv_ready"], i + 1)
                        act.activation(conv_th[:, i % 2, :], conv_acc[:, i % 2, :], ACT.Tanh)\
                            .then_inc(sem["conv_tanh"], 1)

                for c in range(12):
                    heads(START["xbc"] + c + 2)
                    if c == 2:
                        act.wait_ge(sem["dt_done"], 1)
                        for t, (t0, t1, _) in enumerate(TILES):
                            act.activation(head_rows[32:32 + HEADS, t0:t1], head_rows[0:HEADS, t0:t1], ACT.Exp,
                                           bias=head_rows[0:HEADS, t1 - 1:t1], scale=-1.0)\
                                .then_inc(sem["decay_done"], 1)
                    if 2 <= c < 10:
                        if c % 2 == 0:
                            b = c // 2 - 1
                            act.wait_ge(sem["tail_turned"], b + 1)
                            act.activation(conv_tail[:, 512 * b:512 * (b + 1)], bank[4 + b][0:70, :], ACT.Copy)\
                                .then_inc(sem["tail_copied"], 1)
                        conv_pair(c - 2)
                for k in range(KT):
                    if k < 2:
                        act.wait_ge(sem["conv_done"], CT)
                    else:
                        act.wait_ge(sem["z_done"], k - 1)
                    act.wait_ge(sem["evac"], EVAC["z"] + k // 2 + 1)
                    act.activation(conv_th[:, k % 2, 0:TOK], z[:, k, :], ACT.Tanh).then_inc(sem["z_tanh"], 1)

                def gate(b, c, dst):
                    n = START[f"gate{b}"] + c if (b, c) not in ((0, 2), (0, 3)) else START["gate0b"] + c - 2
                    act.wait_ge(sem["evac"], EVAC_OF[n] + 1)
                    for half in range(2):
                        act.activation(dst[:, 2 * c + half, :], dst[:, 2 * c + half, :], ACT.Tanh, scale=0.5,
                                       bias=gain_cols[:, 2 * c + half, 9 + b:10 + b]).then_inc(sem["gate_tanh"], 1)

                heads(START["gate0"] + 2)
                gate(0, 0, y)
                for t, (_, _, n) in enumerate(TILES):
                    act.wait_ge(sem["b_turned"], t + 1)
                    act.activation(b_rows[0:n, t, :], bank[2 + t][0:n, :], ACT.Copy).then_inc(sem["b_ready"], 1)
                heads(START["gate0"] + 3)
                gate(0, 1, y)
                act.wait_ge(sem["delta_ready"], 1)
                for b in range(2):
                    act.activation(h_prompt[:, 512 * b:512 * (b + 1)], bank[3 + b][:], ACT.Copy)\
                        .then_inc(sem["h1_ready"], 1)

                def row_exponential(h):
                    act.wait_ge(sem["seg_ready"], h + 1)
                    if h >= 2:
                        act.wait_ge(sem["mt_ready"], h - 1)
                    act.activation(row_exp[:, h % 2, :], bank[5 + h % 2][:, 0:TOK], ACT.Exp)
                    act.activation(chunk_decay[:, h, :], bank[5 + h % 2][:, 255:TOK:64], ACT.Exp)\
                        .then_inc(sem["row_exp_ready"], 1)

                row_exponential(0)
                for h in range(HEADS):
                    act.wait_ge(sem["seg_ready"], h + 1)
                    act.activation(seg[:, h % 2, 0:SEQ], seg[:, h % 2, 0:SEQ], ACT.Exp)
                    act.activation(seg[0:DEC, h % 2, SEQ:TOK], seg[0:DEC, h % 2, SEQ:TOK], ACT.Exp)\
                        .then_inc(sem["seg_exp"], 1)
                    if h + 1 < HEADS:
                        row_exponential(h + 1)
                    if h % 2 == 0 and h < 12:
                        heads(START["qi"] + h // 2 + 2)
                    if h % 2 == 1 and h >= 5 and h < 13:
                        k = (h - 5) // 2
                        act.wait_ge(sem["mixed"], k + 1)
                        square_of("ssm", k, z)
                heads(START["gate0b"] + 2)
                for k in range(4, KT):
                    act.wait_ge(sem["mixed"], k + 1)
                    square_of("ssm", k, z)

                def state_rows_out(b):
                    act.wait_ge(sem["h_turned"], b + 1)
                    if b == 2:
                        act.wait_ge(sem["h_stored"], 32)
                    act.activation(h_rows[:, 2 * (b % 2):2 * (b % 2) + 2, :],
                                   bank[H_BANK[b]][:].rearrange("p (c n) -> p c n", c=2), ACT.Copy)\
                        .then_inc(sem["h_rows_ready"], 1)

                gate(0, 2, y)
                heads(START["gate0b"] + 3)
                for b in range(4):
                    state_rows_out(b)
                split_heads("ssm", br_hi)
                gate(0, 3, y)

                def index_relu(h):
                    act.wait_ge(sem["idx_ready"], h + 1)
                    if h >= 2:
                        act.wait_ge(sem["idx_used"], h - 1)
                    act.activation(score_relu[:, h % 2, 0:384], bank[2 + h % 2][:, 0:384], ACT.Relu)
                    act.activation(score_relu[0:DEC, h % 2, 384:576], bank[4 + h % 2][0:DEC, 0:192], ACT.Relu)\
                        .then_inc(sem["idx_relu"], 1)

                heads(START["branch0"] + 2)
                act.wait_ge(sem["past_turned"], 1)
                act.activation(k_b_past_t[:].rearrange("p i t -> p (i t)"), bank[5][:, 0:384], ACT.Copy)\
                    .then_inc(sem["past_ready"], 1)
                for c in (1, 2):
                    heads(START["branch0"] + c + 2)
                    index_relu(2 * c - 2)
                    index_relu(2 * c - 1)
                heads(START["branch0"] + 5)
                heads(START["vb"] + 2)
                for t, (_, _, n) in enumerate(TILES):
                    act.wait_ge(sem["k_turned"], t + 1)
                    act.activation(k_b_rows[0:n, t, :], bank[2 + t][0:n, 0:320], ACT.Copy).then_inc(sem["k_rows_ready"], 1)
                for h in range(4):
                    heads(START["gate1"] + h + 2)
                    gate(1, h, gates)

                def exponentials(c):
                    act.wait_ge(sem["shifted"], c + 1)
                    for j, (r, k0, k1) in enumerate(SPANS):
                        ins = act.activation(logit[0:r, c % 2, k0:k1], logit[0:r, c % 2, k0:k1], ACT.Exp, scale=-1.0,
                                             bias=shift[0:r, c % 2, j:j + 1], accum_out=denom[0:r, c % 2, j:j + 1])
                    ins.then_inc(sem["exped"], 1)

                def attention(first, n_heads, per_tile):
                    exponentials(first)
                    for h in range(n_heads):
                        c = first + h
                        if h + 1 < n_heads:
                            exponentials(c + 1)
                        act.wait_ge(sem["p_turned"], c + 1)
                        if c >= 2:
                            act.wait_ge(sem["attended"], c - 1)
                        act.activation(prob_t[:, c % 2, :], bank[5][:], ACT.Copy).then_inc(sem["p_copied"], 1)
                        if first == 8 and h % 4 == 2:
                            heads(START["gate2"] + h // 4 + 2)
                        if first == 8 and h % 4 == 3:
                            gate(2, h // 4, gates)
                        if h % per_tile == per_tile - 1:
                            tile = h // per_tile
                            act.wait_ge(sem["attended"], c + 1)
                            act.activation(br_hi[:, tile, :], bank[6 + tile % 2][:, 0:TOK], ACT.Copy)\
                                .then_inc(sem["attn_hi"], 1)

                attention(0, 8, 1)
                for n in range(START["branch1"], START["kc"]):
                    heads(n + 2)
                act.wait_ge(sem["past_turned"], 3)
                for b in range(2):
                    act.activation(k_c_past_t[:, 4 * b:4 * b + 4, :].rearrange("p i t -> p (i t)"), bank[6 + b][:],
                                   ACT.Copy).then_inc(sem["past_ready"], 1)
                for n in range(START["kc"], START["gate2"]):
                    heads(n + 2)
                    unit = n - START["vc"] - 1
                    if 0 <= unit < 6:
                        t, b = unit // 2, unit % 2
                        rows_n = TILES[t][2]
                        act.wait_ge(sem["k_turned"], 3 + unit + 1)
                        if b == 0:
                            if t == 0:
                                act.wait_ge(sem["past_ready"], 3)
                            else:
                                act.wait_ge(sem["k_stored"], 64 + 16 * t)
                        act.activation(k_c_rows[0:rows_n, 512 * b:512 * (b + 1)], bank[4 + unit % 4][0:rows_n, :],
                                       ACT.Copy).then_inc(sem["k_rows_ready"], 1)
                act.wait_ge(sem["k_stored"], 112)
                attention(8, 16, 2)
                for c in range(4):
                    heads(START["branch2"] + c + 2)
                    act.wait_ge(sem["merged"], 16 + 2 * c + 2)
                    for k in (2 * c, 2 * c + 1):
                        act.activation(u_hi[:, k, :], y[:, k, :], ACT.Copy, scale=0.5).then_inc(sem["u_hi_ready"], 1)
                for c in range(4):
                    n = START["out"] + c
                    heads(n + 2)
                    if c >= 1:
                        square_y("mix_post", 2 * c - 2)
                        square_y("mix_post", 2 * c - 1)
                square_y("mix_post", 6)
                square_y("mix_post", 7)
                act.wait_ge(sem["k_stored"], 112)
                act.wait_ge(sem["v_stored"], 64)
                ffn(1)
                for n in range(START["ple"] + 2, START["plegate"] + 2):
                    heads(n)
                x_heads("ple", 6)
                for c in range(4):
                    heads(START["plegate"] + c + 2)
                    for half in range(2):
                        g = 24 + 2 * c + half
                        act.wait_ge(sem["gate_scaled"], 2 * FT + 2 * c + half + 1)
                        act.activation(th[:, g % 2, :], th[:, g % 2, :], ACT.Tanh, scale=0.5)\
                            .then_inc(sem["gate_tanh"], 1)
                    if c >= 1:
                        square_y("ple_post", 2 * c - 2)
                        square_y("ple_post", 2 * c - 1)
                square_y("ple_post", 6)
                square_y("ple_post", 7)

            @block.tensor
            def _(pe):
                def claim(n, loop=None):
                    p = pair_of(n)
                    if loop is None:
                        pe.wait_ge(sem["w_lo_ready"], n + 1)
                        if frees(n) and freed_before(n):
                            pe.wait_ge(bank_free[p], freed_before(n))
                    else:
                        pe.wait_ge(sem["w_lo_ready"], n + 1 + RING * loop)
                        pe.wait_ge(bank_free[p], freed_before(n) + loop)

                def product(out, s, offset, stride, k_tiles, hi, lo, start=True, stop=True, ready=None):
                    for k in range(k_tiles):
                        if ready is not None:
                            ready(k)
                        at = offset + stride * k
                        wh, wl = w_hi[:, s, at:at + P], w_lo[:, s, at:at + P]
                        pe.matmul(out, wh, hi[:, k, :], start=start and k == 0, stop=False)
                        pe.matmul(out, wh, lo[:, k, :], start=False, stop=False)
                        last = pe.matmul(out, wl, hi[:, k, :], start=False, stop=stop and k == k_tiles - 1)
                    return last

                def wide_chunk(n, hi, lo, k_tiles=KT, ready=None, loop=None):
                    claim(n, loop)
                    s = n % RING
                    for half in range(2):
                        last = product(bank[2 * pair_of(n) + half][:, 0:TOK], s, P * half, 2 * P, k_tiles, hi, lo,
                                       ready=ready if half == 0 else None)
                    last.then_inc(sem["chunk_done"], 1)

                def token_chunk(n):
                    claim(n)
                    s = n % RING
                    for t, t0 in enumerate(STAT_TILES):
                        out = bank[2 * pair_of(n) + t // 2][:, 256 * (t % 2):256 * (t % 2) + 256]
                        for k in range(KT):
                            wh, wl = (w[:, s, 256 * k:256 * (k + 1)] for w in (w_hi, w_lo))
                            uh, ul = (u[:, k, t0:t0 + P] for u in (u_hi, u_lo))
                            pe.matmul(out, uh, wh, start=k == 0, stop=False)
                            pe.matmul(out, ul, wh, start=False, stop=False)
                            last = pe.matmul(out, uh, wl, start=False, stop=k == KT - 1)
                    last.then_inc(sem["chunk_done"], 1)

                def split_ready(name):
                    return lambda k: pe.wait_ge(sem["split_lo"], SPLITS[name] + k + 1)

                def u_ready(section):
                    return lambda k: pe.wait_ge(sem["u_lo_ready"], U[section] + k + 1)

                def token_sums(name, only=None):
                    i = NORM[name]
                    for g in only or range(NORMS[i][1]):
                        pe.wait_ge(sem["square_summed"], square_place(name, KT // NORMS[i][1] * (g + 1) - 1)[2] + 1)
                        for t, t0 in enumerate(STAT_TILES):
                            ins = pe.matmul(stat_bank[:, 3 * g + t:3 * g + t + 1],
                                            square_total[:, (GROUPS_BEFORE[i] + g) % 2, t0:t0 + P], ones[:],
                                            start=True, stop=True)
                        ins.then_inc(sem["square_used"], 1)

                def rms_rows(name):
                    i = NORM[name]
                    groups = NORMS[i][1]
                    pe.wait_ge(sem["rms_ready"], i + 1)
                    for g, b in enumerate(ROW_BANKS[groups]):
                        for t, t0 in enumerate(STAT_TILES):
                            c = 3 * g + t
                            column = rms_columns(groups)[:, c:c + 1].broadcast_to([P, P])
                            last = pe.matmul(bank[b][:, t0:t0 + P], column, ident[:], start=True, stop=True)
                    last.then_inc(sem["row_ready"], 1)

                def small_inputs():
                    pe.wait_ge(sem["rows_loaded"], 16 * 10)
                    for i in range(CT):
                        pe.transpose(bank[6][:, 8 * i:8 * i + 8], conv_rows[:, P * i:P * (i + 1)], ident[0:8, 0:8])
                    for k in range(KT):
                        pe.transpose(bank[7][:, 12 * k:12 * k + 12], gain_rows[:, P * k:P * (k + 1)],
                                     ident[0:12, 0:12])
                    for j in range(4):
                        last = pe.transpose(bank[4][0:HEADS, P * j:P * (j + 1)], bias_rows[:, j, :], ident[:])
                    last.then_inc(sem["rows_turned"], 1)
                    pe.wait_ge(sem["cols_ready"], 2)

                def ffn(which):
                    n0 = START[f"up{which}"]
                    for j in range(RING):
                        wide_chunk(n0 + j, u_hi, u_lo, ready=u_ready(f"ffn{which}") if j == 0 else None)
                        if j == 0 and which == 0:
                            small_inputs()
                        if j == 0:
                            token_sums(f"ffn{which}_pre")
                        if j == 1:
                            rms_rows(f"ffn{which}_pre")
                            if which == 0:
                                pe.wait_ge(sem["bias_rev_ready"], 1)
                    if which == 1:
                        pe.wait_ge(sem["p_loaded"], 32)
                        pe.wait_ge(sem["rms_row_ready"], 3)
                        for k in range(2):
                            for t, (t0, t1, n) in enumerate(TILES):
                                last = pe.transpose(bank[6 + k][:, t0:t1], p_rows[0:n, t, P * k:P * (k + 1)],
                                                    ident[0:n, 0:n])
                        last.then_inc(sem["per_layer_turned"], 1)
                    with pe.Fori(1, 6) as i:
                        for j in range(RING):
                            wide_chunk(n0 + j, u_hi, u_lo, loop=i)
                    for j in range(6 * RING, FT):
                        wide_chunk(n0 + j, u_hi, u_lo)
                    n1 = START[f"down{which}"]
                    for j in range(KT):
                        for half in range(2):
                            n = n1 + 2 * j + half
                            claim(n)
                            k0 = HALF_FT * half
                            ready = None
                            if j == 0:
                                def ready(k, k0=k0):
                                    pe.wait_ge(sem["split_lo"], SPLITS[f"h{which}"] + k0 + k + 1)
                            last = product(bank[2 * ((n1 + 2 * j) % RING)][:, 0:TOK], n % RING, 0, P, HALF_FT,
                                           h_hi[:, k0:k0 + HALF_FT, :], h_lo[:, k0:k0 + HALF_FT, :],
                                           start=half == 0, stop=half == 1, ready=ready)
                            last.then_inc(sem["chunk_done"], 1)
                    if which == 0:
                        token_sums("ffn0_post")
                        rms_rows("ffn0_post")
                    else:
                        for c in range(4):
                            wide_chunk(START["ple"] + c, p_hi, p_lo, k_tiles=2)
                            if c == 0:
                                token_sums("ffn1_post")
                            if c == 2:
                                rms_rows("ffn1_post")

                pe.wait_ge(sem["gains_loaded"], 16)
                for k in range(KT):
                    last = pe.transpose(bank[7][:, 12 * k:12 * k + 8], gain_rows[0:8, P * k:P * (k + 1)],
                                        ident[0:8, 0:8])
                last.then_inc(sem["gains_turned"], 1)
                ffn(0)

                pe.wait_ge(sem["state_loaded"], 16)
                for i in range(KT):
                    last = pe.transpose(bank[4 + i // 4][:, P * (i % 4):P * (i % 4 + 1)], state_rows[:, i, :], ident[:])
                last.then_inc(sem["state_turned"], 1)
                wide_chunk(START["misc"], u_hi, u_lo, ready=u_ready("mix"))
                token_sums("mix_pre")
                for c in range(12):
                    wide_chunk(START["xbc"] + c, u_hi, u_lo)
                    if c == 0:
                        rms_rows("mix_pre")
                        pe.wait_ge(sem["state_ready"], 2)
                    if c % 2 == 0 and 2 <= c < 10:
                        b = c // 2 - 1
                        pe.wait_ge(sem["evac"], EVAC["xbc"] + 2 * b + 2)
                        for i in range(4):
                            last = pe.transpose(bank[4 + b][0:70, P * i:P * (i + 1)], xbc[:, 4 * b + i, 256:326],
                                                ident[:])
                        last.then_inc(sem["tail_turned"], 1)
                pe.wait_ge(sem["decay_done"], 3)
                pe.wait_ge(sem["dt_done"], 1)
                pe.wait_ge(sem["tail_copied"], 4)
                for t, (t0, t1, n) in enumerate(TILES):
                    last = pe.transpose(bank[7][0:n, P * t:P * (t + 1)], head_rows[:, t0:t1], ident[:])
                last.then_inc(sem["rows_cols_turned"], 1)
                wide_chunk(START["gate0"], u_hi, u_lo)
                pe.wait_ge(sem["conv_done"], CT)
                for t, (t0, t1, n) in enumerate(TILES):
                    for b in range(2):
                        if 2 * t + b < 2:
                            pe.wait_ge(sem["evac"], EVAC["z"] + 4)
                        if 2 * t + b == 5:
                            pe.wait_ge(sem["head_cols_ready"], 1)
                        for i in range(4):
                            last = pe.transpose(bank[2 + 2 * t + b][0:n, P * i:P * (i + 1)],
                                                xbc[:, 4 * b + i, t0:t1], ident[:])
                        last.then_inc(sem["xs_turned"], 1)
                for t, (t0, t1, n) in enumerate(TILES):
                    pe.wait_ge(sem["xdt_ready"], t + 1)
                    for g in range(GROUPS):
                        last = pe.transpose(bank[2 + t][0:n, P * g:P * (g + 1)], xbc[:, 8 + g, t0:t1], ident[:])
                    last.then_inc(sem["b_turned"], 1)
                wide_chunk(START["gate0"] + 1, u_hi, u_lo)
                pe.wait_ge(sem["xdt_ready"], 6)
                pe.wait_ge(sem["b_ready"], 1)
                for g in range(GROUPS):
                    for t, (t0, t1, n) in enumerate(TILES):
                        last = pe.matmul(bank[CB_BANK[g]][0:n, t0:t1], xbc[:, 8 + g, t0:t1], xbc[:, 12 + g, t0:t1],
                                         start=True, stop=True)
                    last.then_inc(sem["cb_ready"], 1)

                def state_delta(t):
                    n = TILES[t][2]
                    pe.wait_ge(sem["xdec_ready"], t + 1)
                    for g in range(GROUPS):
                        last = pe.matmul(bank[3 + g // 2][:, 256 * (g % 2):256 * (g % 2) + 256],
                                         b_rows[0:n, t, P * g:P * (g + 1)], xdec[0:n, 256 * g:256 * (g + 1)],
                                         start=True, stop=True)
                    last.then_inc(sem["delta_ready"], 1)

                pe.wait_ge(sem["b_ready"], 3)
                pe.wait_ge(sem["cb_masked"], 4)
                state_delta(0)

                def head_row(h):
                    if h >= 2:
                        pe.wait_ge(sem["row_exp_ready"], h - 1)
                        pe.wait_ge(sem["seg_ready"], h - 1)
                    pe.matmul(bank[5 + h % 2][:, 0:TOK], ident[0:HEADS, h:h + 1].broadcast_to([HEADS, P]),
                              head_rows[0:HEADS, :], start=True, stop=True).then_inc(sem["bc_ready"], 1)

                pe.wait_ge(sem["b_ready"], 3)
                head_row(0)
                head_row(1)
                pe.wait_ge(sem["h1_ready"], 2)
                for h in range(HEADS):
                    pe.wait_ge(sem["mt_ready"], h + 1)
                    i, r0 = h // 2, 64 * (h % 2)
                    if i >= 2:
                        pe.wait_ge(sem["mixed"], i - 1)
                    out = bank[(7, 2)[i % 2]]
                    f = slice(64 * h, 64 * h + 64)
                    pe.matmul(out[r0:r0 + 64, 0:128], xdt[:, 0, f], seg[:, h % 2, 0:128], start=True, stop=True)
                    pe.matmul(out[r0:r0 + 64, 128:256], xdt[:, 1, f], seg[:, h % 2, 128:256], start=True, stop=False)
                    pe.matmul(out[r0:r0 + 64, 128:256], h_prompt[:, f], row_exp[:, h % 2, 128:256], start=False,
                              stop=True)
                    pe.matmul(out[r0:r0 + 64, 256:320], xdt[0:DEC, 2, f], seg[0:DEC, h % 2, 256:320], start=True,
                              stop=False)
                    pe.matmul(out[r0:r0 + 64, 256:320], h_sample[:, f], row_exp[:, h % 2, 256:320], start=False,
                              stop=True).then_inc(sem["head_done"], 1)
                    if h + 2 < HEADS:
                        head_row(h + 2)
                    if h % 2 == 0 and h < 12:
                        wide_chunk(START["qi"] + h // 2, u_hi, u_lo)
                    if h == 12:
                        state_delta(1)
                def turn_state(b):
                    src = h_prompt if b < 2 else h_sample
                    for i in range(4):
                        at = 512 * (b % 2) + P * i
                        last = pe.transpose(bank[H_BANK[b]][:, P * i:P * (i + 1)], src[:, at:at + P], ident[:])
                    last.then_inc(sem["h_turned"], 1)

                token_sums("ssm", (0, 1))
                wide_chunk(START["gate0b"], u_hi, u_lo)
                pe.wait_ge(sem["h_final"], 1)
                state_delta(2)
                token_sums("ssm", (2, 3))
                pe.wait_ge(sem["mixed"], KT)
                turn_state(0)
                turn_state(1)
                wide_chunk(START["gate0b"] + 1, u_hi, u_lo)
                pe.wait_ge(sem["h_final"], 2)
                pe.wait_ge(sem["h_rows_ready"], 2)
                rms_rows("ssm")
                turn_state(2)
                turn_state(3)

                def scores(q, qp, k, k_past, wide, narrow):
                    pe.matmul(wide[:, 0:128], q[qp, 0:128], k[qp, 0:128], start=True, stop=True)
                    pe.matmul(wide[:, 128:384], q[qp, 128:256], k[qp, 0:256], start=True, stop=True)
                    pe.matmul(narrow[0:DEC, 0:128], q[qp, 256:320], k_past[qp, :], start=True, stop=True)
                    return pe.matmul(narrow[0:DEC, 128:192], q[qp, 256:320], k[qp, 256:320], start=True, stop=True)

                def merge(b):
                    for c in range(4):
                        wide_chunk(START[f"branch{b}"] + c, br_hi, br_lo)

                pe.wait_ge(sem["h_rows_ready"], 4)
                for c in range(4):
                    wide_chunk(START["branch0"] + c, br_hi, br_lo, ready=split_ready("ssm") if c == 0 else None)
                    if c == 0:
                        pe.wait_ge(sem["k_past_loaded"], 48)
                        for i in range(3):
                            last = pe.transpose(bank[5][:, P * i:P * (i + 1)], k_b_past[:, P * i:P * (i + 1)], ident[:])
                        last.then_inc(sem["past_turned"], 1)
                    if c in (1, 2):
                        pe.wait_ge(sem["past_ready"], 1)
                        for h in (2 * c - 2, 2 * c - 1):
                            if h >= 2:
                                pe.wait_ge(sem["idx_relu"], h - 1)
                            qp = slice(64 * (h % 2), 64 * (h % 2) + 64)
                            scores(q_i[:, h // 2, :], qp, ki[:], k_b_past_t[:, 2, :], bank[2 + h % 2], bank[4 + h % 2])\
                                .then_inc(sem["idx_ready"], 1)
                token_chunk(START["vb"])
                pe.wait_ge(sem["idx_relu"], 4)
                for t, (t0, t1, n) in enumerate(TILES):
                    for i in range(2):
                        pe.transpose(bank[2 + t][0:n, P * i:P * (i + 1)], k_b[:, i, t0:t1], ident[:])
                    pe.transpose(bank[2 + t][0:n, 256:320], ki[0:64, t0:t1], ident[0:64, 0:64])\
                        .then_inc(sem["k_turned"], 1)
                for h in range(4):
                    wide_chunk(START["gate1"] + h, u_hi, u_lo)

                def attention(first, n_heads, per_tile, q, k, k_past, v, v_past, d, q_per_kv):
                    def score_head(h):
                        c = first + h
                        if c >= 1:
                            pe.wait_ge(sem["shifted"], c)
                        qp = slice(d * (h % per_tile), d * (h % per_tile) + d)
                        kt = h // q_per_kv // per_tile
                        scores(q[:, h // per_tile, :], qp, k[:, kt, :], k_past[:, kt, :], bank[2 + c % 2],
                               bank[4]).then_inc(sem["scored"], 1)

                    score_head(0)
                    score_head(1)
                    for h in range(n_heads):
                        c = first + h
                        pe.wait_ge(sem["normed"], c + 1)
                        if c >= 1:
                            pe.wait_ge(sem["p_copied"], c)
                        tb = bank[5]
                        for dst, r, k0 in ((0, 128, 0), (128, 128, 128), (256, 128, 256), (384, 64, 384), (448, 64, 448)):
                            last = pe.transpose(tb[:, dst:dst + r], logit[0:r, c % 2, k0:k0 + P], ident[0:r, 0:r])
                        last.then_inc(sem["p_turned"], 1)
                        if h + 2 < n_heads:
                            score_head(h + 2)
                        if first == 8 and h % 4 == 1:
                            wide_chunk(START["gate2"] + h // 4, u_hi, u_lo)
                        tile = h // per_tile
                        all_tile = TILE0[first] + tile
                        if h % per_tile == 0 and tile >= 2:
                            pe.wait_ge(sem["attn_lo"], all_tile - 1)
                        pe.wait_ge(sem["p_copied"], c + 1)
                        r0 = d * (h % per_tile)
                        ob, pt = bank[6 + tile % 2][r0:r0 + d], prob_t[:, c % 2]
                        f = slice(d * (h // q_per_kv), d * (h // q_per_kv) + d)
                        pe.matmul(ob[:, 0:128], v[:, 0, f], pt[:, 0:128], start=True, stop=True)
                        pe.matmul(ob[:, 128:256], v[:, 0, f], pt[:, 128:256], start=True, stop=False)
                        pe.matmul(ob[:, 128:256], v[:, 1, f], pt[:, 256:384], start=False, stop=True)
                        pe.matmul(ob[:, 256:320], v_past[:, f], pt[:, 384:448], start=True, stop=False)
                        pe.matmul(ob[:, 256:320], v[64:128, 2, f], pt[64:128, 448:512], start=False, stop=True)\
                            .then_inc(sem["attended"], 1)

                pe.wait_ge(sem["k_rows_ready"], 3)
                pe.wait_ge(sem["evac"], EVAC["gate1"] + 4)
                pe.wait_ge(sem["v_past_loaded"], 16)
                attention(0, 8, 1, q_b, k_b, k_b_past_t, v_b, v_b_past, 128, 4)
                pe.wait_ge(sem["attn_lo"], 8)
                merge(1)
                pe.wait_ge(sem["k_past_loaded"], 64)
                for i in range(KT):
                    last = pe.transpose(bank[6 + i // 4][:, P * (i % 4):P * (i % 4 + 1)], k_c_rows[:, P * i:P * (i + 1)],
                                        ident[:])
                    if i % 4 == 3:
                        last.then_inc(sem["past_turned"], 1)
                for c in range(4):
                    wide_chunk(START["kc"] + c, u_hi, u_lo)
                for n in range(START["vc"], START["gate2"]):
                    if n < START["qc"]:
                        token_chunk(n)
                    else:
                        wide_chunk(n, u_hi, u_lo)
                    unit = n - START["vc"] - 1
                    if 0 <= unit < 6:
                        t, b = unit // 2, unit % 2
                        t0, t1, rows_n = TILES[t]
                        pe.wait_ge(sem["evac"], EVAC["kc"] + 4)
                        pe.wait_ge(sem["past_ready"], 3)
                        if unit >= 4:
                            pe.wait_ge(sem["k_rows_ready"], 3 + unit - 3)
                        for i in range(4):
                            last = pe.transpose(bank[4 + unit % 4][0:rows_n, P * i:P * (i + 1)],
                                                k_c[:, 4 * b + i, t0:t1], ident[:])
                        last.then_inc(sem["k_turned"], 1)
                pe.wait_ge(sem["evac"], EVAC["qc"] + 4)
                pe.wait_ge(sem["k_rows_ready"], 9)
                pe.wait_ge(sem["past_ready"], 3)
                pe.wait_ge(sem["v_past_loaded"], 32)
                attention(8, 16, 2, q_c, k_c, k_c_past_t, v_c, v_c_past, 64, 1)
                pe.wait_ge(sem["attn_lo"], 16)
                merge(2)
                for c in range(4):
                    wide_chunk(START["out"] + c, u_hi, u_lo, ready=u_ready("merged") if c == 0 else None)
                token_sums("mix_post")
                rms_rows("mix_post")
                ffn(1)
                for c in range(4):
                    wide_chunk(START["plegate"] + c, u_hi, u_lo, ready=u_ready("ple") if c == 0 else None)
                    if c == 0:
                        token_sums("ple_pre")
                    if c == 1:
                        rms_rows("ple_pre")
                token_sums("ple_post")
                rms_rows("ple_post")

            @block.vector
            def _(dve):
                step = Chain(dve, sem["dve_step"])

                def sum_square(name, k):
                    group, first, number = square_place(name, k)
                    if first:
                        return
                    dve.wait_ge(sem["square_ready"], KT * NORM[name] + k + 1)
                    if number >= 1:
                        dve.wait_ge(sem["square_summed"], number)
                    total = square_total[:, group % 2, :]
                    dve.tensor_tensor(total, total, square[:, number % 2, :], ALU.add)\
                        .then_inc(sem["square_summed"], 1)

                def norm_columns(name):
                    i = NORM[name]
                    groups = NORMS[i][1]
                    w = 3 * groups
                    v, t, r = rs[:, 0, 0:w], rs[:, 1, 0:w], rms_columns(groups)
                    dve.wait_ge(sem["square_used"], GROUPS_BEFORE[i + 1])
                    step(dve.tensor_scalar(v, stat_bank[:, 0:w], groups / D, EPS, ALU.mult, ALU.add))
                    step(dve.tensor_scalar(r.bitcast(I32), v.bitcast(I32), -0.5, RSQRT_SEED, ALU.mult, ALU.add))
                    for newton in range(3):
                        step(dve.tensor_tensor(t, r, r, ALU.mult))
                        step(dve.scalar_tensor_tensor(out=t, in0=t, scalar=-0.5, in1=v, op0=ALU.mult, op1=ALU.mult))
                        ins = dve.scalar_tensor_tensor(out=r, in0=t, scalar=1.5, in1=r, op0=ALU.add, op1=ALU.mult)
                        if newton < 2:
                            step(ins)
                    ins.then_inc(sem["rms_ready"], 1)

                def norm_rows(name):
                    norm_columns(name)
                    dve.wait_ge(sem["row_ready"], NORM[name] + 1)

                def rms_row_of(name, meanwhile=None):
                    for k in range(KT):
                        sum_square(name, k)
                    if meanwhile is not None:
                        meanwhile()
                    norm_rows(name)
                    dve.tensor_copy(rms_row[:], bank[7][:, 0:TOK]).then_inc(sem["rms_row_ready"], 1)
                    dve.wait_ge(sem["rms_row_ready"], 1 + ["ffn0_pre", "mix_pre", "ffn1_pre", "ple_pre"].index(name))

                def x_rest(section, gain, k):
                    dve.wait_ge(sem["u_hi_ready"], U[section] + k + 1)
                    dve.scalar_tensor_tensor(out=u_lo[:, k, :], in0=x[:, k, :], scalar=gain_cols[:, k, gain:gain + 1],
                                             in1=f32(u_hi[:, k, :]), op0=ALU.mult, op1=ALU.subtract)\
                        .then_inc(sem["u_lo_ready"], 1)

                def split_rest(q, dst_hi, dst_lo):
                    dve.wait_ge(sem["split_hi"], q + 1)
                    dve.tensor_tensor(dst_lo, split_tmp[:, q % RING, :], f32(dst_hi), ALU.subtract)\
                        .then_inc(sem["split_lo"], 1)

                def split_source(q, write):
                    if q >= RING:
                        dve.wait_ge(sem["split_lo"], q - RING + 1)
                    write(split_tmp[:, q % RING, :]).then_inc(sem["split_src"], 1)

                def norm_split(name, split, src, gain, hi, lo):
                    groups = NORMS[NORM[name]][1]
                    banks = ROW_BANKS[groups]
                    q0 = SPLITS[split]
                    dve.wait_ge(sem["row_ready"], NORM[name] + 1)
                    for k in range(KT + 1):
                        if k < KT:
                            row = bank[banks[k * groups // KT]][:, 0:TOK]
                            split_source(q0 + k, lambda dst: dve.scalar_tensor_tensor(
                                out=dst, in0=src[:, k, :], scalar=gain_cols[:, k, gain:gain + 1], in1=row,
                                op0=ALU.mult, op1=ALU.mult))
                        if k >= 1:
                            split_rest(q0 + k - 1, hi[:, k - 1, :], lo[:, k - 1, :])

                def add_normed(name, gain, section=None, next_gain=None, beside=None):
                    norm_columns(name)
                    if beside is not None:
                        beside()
                    dve.wait_ge(sem["row_ready"], NORM[name] + 1)
                    for k in range(KT + 3):
                        if k < KT:
                            dve.scalar_tensor_tensor(out=y[:, k, :], in0=y[:, k, :],
                                                     scalar=gain_cols[:, k, gain:gain + 1], in1=bank[7][:, 0:TOK],
                                                     op0=ALU.mult, op1=ALU.mult).then_inc(sem["y_normed"], 1)
                        if k >= 3 and section is not None:
                            x_rest(section, next_gain, k - 3)
                    if section is None:
                        dve.wait_ge(sem["y_normed"], 4 * KT)
                        for k in range(POOL_TILES, KT):
                            dve.tensor_tensor(x[:, k, :], x[:, k, :], y[:, k, :], ALU.add).then_inc(sem["x_ready"], 1)

                def up_chunk(which, j, loop=None):
                    n = START[f"up{which}"] + j
                    s, more = n % RING, 0 if loop is None else RING * loop
                    q = SPLITS[f"h{which}"] + j
                    tmp = split_tmp[:, q % RING, :]
                    dve.wait_ge(sem["chunk_done"], n + 1 + more)
                    dve.tensor_tensor(tmp, bank[2 * s][:, 0:TOK], rms_row[:], ALU.mult).then_inc(sem["gate_scaled"], 1)
                    b = bank[2 * s + 1][:, 0:TOK]
                    dve.scalar_tensor_tensor(out=b, in0=b, scalar=0.5, in1=rms_row[:], op0=ALU.mult, op1=ALU.mult)\
                        .then_inc(sem["b_scaled"], 1)
                    dve.wait_ge(sem["tanh_ready"], FT * which + j + 1 + more)
                    dve.wait_ge(sem["gate_scaled"], FT * which + j + 1 + more)
                    dve.scalar_tensor_tensor(out=tmp, in0=th[:, s, :], scalar=1.0, in1=tmp,
                                             op0=ALU.add, op1=ALU.mult).then_inc(sem["silu_ready"], 1)
                    dve.wait_ge(sem["b_scaled"], FT * which + j + 1 + more)
                    dve.wait_ge(sem["silu_ready"], FT * which + j + 1 + more)
                    dve.tensor_tensor(tmp, tmp, b, ALU.mult).then_inc(sem["split_src"], 1)
                    dve.wait_ge(sem["split_hi"], q + 1 + more)
                    if loop is None:
                        hi, lo = h_hi[:, j, :], h_lo[:, j, :]
                    else:
                        hi, lo = (h[:, bass.ds(loop * RING + j, 1), :].rearrange("p j t -> p (j t)")
                                  for h in (h_hi, h_lo))
                    dve.tensor_tensor(lo, tmp, f32(hi), ALU.subtract).then_inc(sem["split_lo"], 1)
                    dve.wait_ge(sem["split_lo"], q + 1 + more)
                    dve.sem_inc(bank_free[s], 1)

                def ffn(which):
                    if which == 0:
                        for k in range(KT):
                            x_rest("ffn0", 0, k)
                            if k == 1:
                                dve.wait_ge(sem["w_hi_ready"], 1)
                                dve.tensor_tensor(w_lo[:, 0, :], stage[:, 0, :], f32(w_hi[:, 0, :]), ALU.subtract)\
                                    .then_inc(sem["w_lo_ready"], 1)
                    rms_row_of(f"ffn{which}_pre", small_inputs if which == 0 else None)
                    for j in range(RING):
                        up_chunk(which, j)
                    if which == 1:
                        for k in range(2):
                            dve.wait_ge(sem["p_ready"], 2)
                            step(dve.tensor_tensor(p_lo[:, k, :], bank[6 + k][:, 0:TOK], f32(p_hi[:, k, :]),
                                                   ALU.subtract))
                    with dve.Fori(1, 6) as i:
                        for j in range(RING):
                            up_chunk(which, j, loop=i)
                    for j in range(6 * RING, FT):
                        up_chunk(which, j)
                    n1 = START[f"down{which}"]
                    for j in range(KT):
                        dve.wait_ge(sem["chunk_done"], n1 + 2 * j + 2)
                        s = (n1 + 2 * j) % RING
                        step(dve.tensor_copy(y[:, j, :], bank[2 * s][:, 0:TOK]))
                        dve.sem_inc(bank_free[s], 1)
                        dve.sem_inc(sem["y_ready"], 1)
                        if j >= 1:
                            sum_square(f"ffn{which}_post", j - 1)
                    sum_square(f"ffn{which}_post", KT - 1)
                    if which == 0:
                        add_normed("ffn0_post", 1, "mix", 2)
                    else:
                        embed(0)
                        add_normed("ffn1_post", 5, "ple", 6, beside=lambda: (embed(1), embed(2)))
                        embed(3)

                def give_back(n):
                    dve.sem_inc(bank_free[pair_of(n)], 1)

                def evacuate(n, writes):
                    s = pair_of(n)
                    dve.wait_ge(sem["chunk_done"], n + 1)
                    for write in writes(bank[2 * s], bank[2 * s + 1]):
                        last = write
                    last.then_inc(sem["evac"], 1)
                    dve.wait_ge(sem["evac"], EVAC_OF[n] + 1)
                    give_back(n)

                cc = bank[6][:, 0:8 * CT].rearrange("p (i r) -> p i r", r=8)
                gc = bank[7][:, 0:12 * KT].rearrange("p (i r) -> p i r", r=12)

                def small_inputs():
                    dve.wait_ge(sem["rows_turned"], 1)
                    dve.tensor_scalar(conv_cols[:, :, 0:5], cc[:, :, 0:5], 0.5, None, ALU.mult)
                    dve.tensor_copy(conv_cols[:, :, 5:8], cc[:, :, 5:8])
                    dve.tensor_copy(gain_cols[:, :, 8:9], gc[:, :, 8:9])
                    step(dve.tensor_scalar(gain_cols[:, :, 9:12], gc[:, :, 9:12], 0.5, None, ALU.mult))
                    dve.sem_inc(sem["cols_ready"], 1)

                def embed(c):
                    evacuate(START["ple"] + c, lambda b0, b1: (
                        dve.tensor_scalar(embedded[:, 2 * c + half, :], b[:, 0:TOK], 0.5, None, ALU.mult)
                        for half, b in enumerate((b0, b1))))

                dve.wait_ge(sem["gains_turned"], 1)
                step(dve.tensor_copy(gain_cols[:, :, 0:8], gc[:, :, 0:8]))
                step(dve.tensor_scalar(gain_cols[:, :, 1:6:4], gc[:, :, 1:6:4], 0.5, None, ALU.mult))
                dve.sem_inc(sem["cols_ready"], 1)
                ffn(0)

                rms_row_of("mix_pre")
                dve.memset(xbc[:, :, 0:3], 0.0)
                step(dve.tensor_copy(xbc[:, :, SEQ + 3:SEQ + 6], conv_cols[:, :, 5:8]))
                evacuate(START["misc"], lambda b0, b1: (
                    dve.tensor_tensor(ki[:], b0[:, 0:TOK], rms_row[:], ALU.mult),
                    dve.scalar_tensor_tensor(out=head_rows[96:100, :], in0=b1[32:36, 0:TOK], scalar=0.5,
                                             in1=rms_row[32:36, :], op0=ALU.mult, op1=ALU.mult),
                    dve.tensor_tensor(dt_tmp[:, 0, :], b1[0:HEADS, 0:TOK], rms_row[0:HEADS, :], ALU.mult)))
                step(dve.tensor_scalar(dt_tmp[:, 0, :], dt_tmp[:, 0, :], dt_bias[:], None, ALU.add))
                dve.scalar_tensor_tensor(out=dt_tmp[:, 1, :], in0=dt_tmp[:, 0, :], scalar=-1.0, in1=dt_tmp[:, 0, :],
                                         op0=ALU.mult, op1=ALU.min).then_inc(sem["dt_v"], 1)

                def copies(dst, k0, scale):
                    def writes(b0, b1):
                        for half, b in enumerate((b0, b1)):
                            yield dve.scalar_tensor_tensor(out=dst[:, k0 + half, :], in0=b[:, 0:TOK], scalar=scale,
                                                           in1=rms_row[:], op0=ALU.mult, op1=ALU.mult)
                    return writes

                def values(dst, c0):
                    def writes(b0, b1):
                        for t in range(3):
                            src = (b0, b1)[t // 2][:, 256 * (t % 2):256 * (t % 2) + 256]
                            yield dve.tensor_scalar(dst[:, t, c0:c0 + 256], src,
                                                    rms_columns(1)[:, t:t + 1], None, ALU.mult)
                    return writes

                def dsa_writes(i):
                    if i == 0:
                        return copies(q_i, 0, 0.125)
                    if i == 1:
                        return copies(k_b, 0, 1.0)
                    return copies(q_b, 2 * (i - 2), -float(128) ** -0.5)

                def cumulative_decay():
                    dve.wait_ge(sem["dt_exp"], 1)
                    dt_rows = dt_tmp[:, 0, :]
                    step(dve.scalar_tensor_tensor(out=dt_rows, in0=dt_rows, scalar=0.0, in1=dt_tmp[:, 1, :],
                                                  op0=ALU.max, op1=ALU.add))
                    dve.tensor_copy(head_rows[64:64 + HEADS, :], dt_rows)
                    dve.memset(dt_tmp[:, 1, :], 1.0)
                    step(dve.tensor_scalar(dt_tmp[:, 2, :], dt_rows, neg_a[:], -1.0, ALU.mult, ALU.mult))
                    for t0, t1, _ in TILES:
                        last = dve.tensor_tensor_scan(head_rows[0:HEADS, t0:t1], dt_tmp[:, 1, t0:t1],
                                                      dt_tmp[:, 2, t0:t1], 0.0, ALU.mult, ALU.add)
                    last.then_inc(sem["dt_done"], 1)

                def conv_pair(c):
                    dve.wait_ge(sem["conv_base"], 2 * c + 2)
                    for k in range(1, 4):
                        for i in (2 * c, 2 * c + 1):
                            acc = conv_acc[:, i % 2, :]
                            ins = dve.scalar_tensor_tensor(out=acc, in0=xbc[:, i, k:k + CONV_N],
                                                           scalar=conv_cols[:, i, k:k + 1], in1=acc, op0=ALU.mult,
                                                           op1=ALU.add)
                            if k < 3:
                                ins.then_inc(sem["dve_step"], 1)
                                step.count += 1
                                dve.wait_ge(sem["dve_step"], step.count - 1)
                            else:
                                if i % 2 == 0:
                                    dve.wait_ge(sem["dve_step"], step.count)
                                ins.then_inc(sem["conv_ready"], 1)
                    for i in (2 * c, 2 * c + 1):
                        dve.wait_ge(sem["conv_tanh"], i + 1)
                        dve.wait_ge(sem["conv_ready"], i + 1)
                        dve.wait_ge(sem["tail_turned"], i // 4 + 1)
                        for out0, t0, w in ((0, 0, SEQ), (SEQ, SEQ + 3, DEC)):
                            last = dve.scalar_tensor_tensor(out=xbc[:, i, out0:out0 + w],
                                                            in0=conv_th[:, i % 2, t0:t0 + w], scalar=1.0,
                                                            in1=conv_acc[:, i % 2, t0:t0 + w], op0=ALU.add,
                                                            op1=ALU.mult)
                        last.then_inc(sem["conv_done"], 1)

                for c in range(12):
                    if c < 8:
                        evacuate(START["xbc"] + c, lambda b0, b1: (
                            dve.tensor_tensor(xbc[:, 2 * c + half, at:at + w], b[:, t0:t0 + w],
                                              rms_row[:, t0:t0 + w], ALU.mult)
                            for half, b in enumerate((b0, b1)) for at, t0, w in ((3, 0, SEQ), (SEQ + 6, SEQ, DEC))))
                    else:
                        evacuate(START["xbc"] + c, copies(z, 2 * (c - 8), 0.5))
                    if c == 0:
                        cumulative_decay()
                    if 2 <= c < 10:
                        conv_pair(c - 2)
                for k in range(KT):
                    dve.wait_ge(sem["z_tanh"], k + 1)
                    dve.scalar_tensor_tensor(out=z[:, k, :], in0=conv_th[:, k % 2, 0:TOK], scalar=1.0, in1=z[:, k, :],
                                             op0=ALU.add, op1=ALU.mult).then_inc(sem["z_done"], 1)

                def gate_of(b, c, dst):
                    n = START[f"gate{b}"] + c if (b, c) not in ((0, 2), (0, 3)) else START["gate0b"] + c - 2
                    evacuate(n, copies(dst, 2 * c, 1.0))

                dve.wait_ge(sem["rows_cols_turned"], 1)
                dve.tensor_copy(head_cols[:, 0:2, :].rearrange("p t c -> p (t c)"), bank[7][:, 0:256])
                dve.tensor_copy(head_cols[0:DEC, 2, :], bank[7][0:DEC, 256:384]).then_inc(sem["head_cols_ready"], 1)
                dve.wait_ge(sem["head_cols_ready"], 1)
                gate_of(0, 0, y)
                dve.wait_ge(sem["tail_stored"], 32)
                for t, (_, _, n) in enumerate(TILES):
                    for b in range(2):
                        dve.wait_ge(sem["xs_turned"], 2 * t + b + 1)
                        dve.tensor_tensor(
                            xdt[0:n, t, 512 * b:512 * (b + 1)].rearrange("p (h d) -> p h d", d=64),
                            bank[2 + 2 * t + b][0:n, :].rearrange("p (h d) -> p h d", d=64),
                            head_cols[0:n, t, 64 + 8 * b:72 + 8 * b].unsqueeze(2).broadcast_to([n, 8, 64]), ALU.mult)\
                            .then_inc(sem["xdt_ready"], 1)
                for g in range(GROUPS):
                    dve.wait_ge(sem["cb_ready"], GROUPS)
                    for t, (t0, t1, n) in enumerate(TILES):
                        last = dve.tensor_tensor(cb[0:n, g, t0:t1], bank[CB_BANK[g]][0:n, t0:t1], tri[0:n, 0:n], ALU.mult)
                    last.then_inc(sem["cb_masked"], 1)

                def decayed(t):
                    n = TILES[t][2]
                    if t >= 1:
                        dve.wait_ge(sem["delta_ready"], t)
                    dve.tensor_tensor(xdec[0:n, :].rearrange("p (h d) -> p h d", d=64),
                                      xdt[0:n, t, :].rearrange("p (h d) -> p h d", d=64),
                                      head_cols[0:n, t, 32:32 + HEADS].unsqueeze(2).broadcast_to([n, HEADS, 64]),
                                      ALU.mult).then_inc(sem["xdec_ready"], 1)

                dve.wait_ge(sem["xdt_ready"], 6)
                decayed(0)
                gate_of(0, 1, y)

                def segments(h):
                    dve.wait_ge(sem["bc_ready"], h + 1)
                    if h >= 2:
                        dve.wait_ge(sem["head_done"], h - 1)
                    for t, (t0, t1, n) in enumerate(TILES):
                        last = dve.tensor_scalar(seg[0:n, h % 2, t0:t1], bank[5 + h % 2][0:n, t0:t1],
                                                 head_cols[0:n, t, h:h + 1], 0.0, ALU.subtract, ALU.min)
                    last.then_inc(sem["seg_ready"], 1)

                def mix_tile(i):
                    dve.wait_ge(sem["head_done"], 2 * i + 2)
                    mixed = split_tmp[:, 2, :]
                    step(dve.scalar_tensor_tensor(out=mixed, in0=xbc[:, i, 0:TOK], scalar=d_col[:, i:i + 1],
                                                  in1=bank[(7, 2)[i % 2]][:, 0:TOK], op0=ALU.mult, op1=ALU.add))
                    dve.tensor_tensor(z[:, i, :], z[:, i, :], mixed, ALU.mult).then_inc(sem["mixed"], 1)
                    dve.wait_ge(sem["mixed"], i + 1)

                dve.wait_ge(sem["conv_done"], CT)
                dve.wait_ge(sem["cb_masked"], 4)
                def weigh(h):
                    g = h // (HEADS // GROUPS)
                    dve.wait_ge(sem["seg_exp"], h + 1)
                    dve.tensor_tensor(seg[:, h % 2, 0:SEQ], seg[:, h % 2, 0:SEQ], cb[:, g, 0:SEQ], ALU.mult)
                    dve.tensor_tensor(seg[0:DEC, h % 2, SEQ:TOK], seg[0:DEC, h % 2, SEQ:TOK], cb[0:DEC, g, SEQ:TOK],
                                      ALU.mult)
                    dve.wait_ge(sem["row_exp_ready"], h + 1)
                    dve.tensor_tensor(row_exp[:, h % 2, 128:TOK], row_exp[:, h % 2, 128:TOK], xbc[:, 12 + g, 128:TOK],
                                      ALU.mult).then_inc(sem["mt_ready"], 1)

                segments(0)
                segments(1)
                weigh(0)
                for h in range(HEADS):
                    if h + 1 < HEADS:
                        weigh(h + 1)
                    if h + 2 < HEADS:
                        segments(h + 2)
                    if h == 10:
                        decayed(1)
                    if h % 2 == 0 and h >= 2:
                        mix_tile(h // 2 - 1)
                    if h % 2 == 1 and h >= 7 and h < 15:
                        sum_square("ssm", (h - 7) // 2)
                    if h % 2 == 1 and h < 12:
                        evacuate(START["qi"] + h // 2, dsa_writes(h // 2))
                mix_tile(KT - 1)
                dve.wait_ge(sem["head_done"], HEADS)
                def final_state(t, state):
                    dve.wait_ge(sem["delta_ready"], t + 1)
                    for h in range(HEADS):
                        f = slice(64 * h, 64 * h + 64)
                        last = dve.scalar_tensor_tensor(out=state[:, f], in0=state[:, f],
                                                        scalar=chunk_decay[:, h, t - 1:t],
                                                        in1=bank[3 + h // 8][:, 64 * (h % 8):64 * (h % 8) + 64],
                                                        op0=ALU.mult, op1=ALU.add)
                    last.then_inc(sem["h_final"], 1)

                final_state(1, h_prompt)
                decayed(2)
                for k in range(4, KT):
                    sum_square("ssm", k)
                gate_of(0, 2, y)
                norm_columns("ssm")
                final_state(2, h_sample)
                gate_of(0, 3, y)
                norm_split("ssm", "ssm", z, 8, br_hi, br_lo)

                def merge_chunk(b, c):
                    gated = y if b == 0 else gates
                    n = START[f"branch{b}"] + c
                    dve.wait_ge(sem["chunk_done"], n + 1)
                    dve.wait_ge(sem["gate_tanh"], 8 * b + 2 * c + 2)
                    for half in range(2):
                        k = 2 * c + half
                        ins = dve.scalar_tensor_tensor(out=gated[:, k, :], in0=gated[:, k, :], scalar=1.0,
                                                       in1=bank[2 * pair_of(n) + half][:, 0:TOK], op0=ALU.add,
                                                       op1=ALU.mult)
                        if b > 0:
                            step(ins)
                            ins = dve.tensor_tensor(y[:, k, :], y[:, k, :], gates[:, k, :], ALU.add)
                        ins.then_inc(sem["merged"], 1)
                    dve.wait_ge(sem["merged"], 8 * b + 2 * c + 2)
                    give_back(n)

                def index_sum(h):
                    dve.wait_ge(sem["idx_relu"], h + 1)
                    for j, (r, k0, k1) in enumerate(SPANS):
                        weight = head_cols[0:r, j, 96 + h:97 + h]
                        if h == 0:
                            last = dve.tensor_scalar(score[0:r, k0:k1], score_relu[0:r, 0, k0:k1], weight, None,
                                                     ALU.mult)
                        else:
                            last = dve.scalar_tensor_tensor(out=score[0:r, k0:k1], in0=score_relu[0:r, h % 2, k0:k1],
                                                            scalar=weight, in1=score[0:r, k0:k1], op0=ALU.mult,
                                                            op1=ALU.add)
                    last.then_inc(sem["idx_used"], 1)
                    dve.wait_ge(sem["idx_used"], h + 1)

                for c in range(4):
                    merge_chunk(0, c)
                    if c >= 2:
                        index_sum(2 * c - 4)
                        index_sum(2 * c - 3)
                dve.memset(score[0:64, 64:128], -BIG)
                step(dve.memset(score[0:64, 320:384], -BIG))
                written = [step.count] * len(SPANS)

                def top_round(number):
                    spans = [(j, *SPANS[j]) for j in range(3) if number < (8, 8, 6)[j]]
                    for replace in (False, True):
                        for j, r, k0, k1 in spans:
                            dve.wait_ge(sem["dve_step"], written[j])
                            span, top = score[0:r, k0:k1], top8[0:r, j, :]
                            ins = dve.match_replace(span, top, span, GONE) if replace else dve.max(top, span)
                            ins.then_inc(sem["dve_step"], 1)
                            step.count += 1
                            written[j] = step.count

                for number in range(8):
                    top_round(number)
                    if number == 1:
                        evacuate(START["vb"], values(v_b, 0))
                    if number in (3, 5, 7):
                        gate_of(1, number // 2 - 1, gates)
                dve.wait_ge(sem["dve_step"], step.count)
                for r, k0, k1 in ((128, 0, 384), (64, 384, 576)):
                    last = dve.tensor_scalar(dsa_mask[0:r, k0:k1], score[0:r, k0:k1], GONE / 2, BIG, ALU.is_gt,
                                             ALU.mult)
                last.then_inc(sem["mask_ready"], 1)
                dve.wait_ge(sem["mask_ready"], 1)
                gate_of(1, 3, gates)

                def shifted(c, bias_of):
                    dve.wait_ge(sem["scored"], c + 1)
                    if c >= 2:
                        dve.wait_ge(sem["p_turned"], c - 1)
                    for j, (r, k0, k1) in enumerate(SPANS):
                        src = bank[2 + c % 2][:, k0:k1] if j < 2 else bank[4][0:r, 0:k1 - k0]
                        last = dve.tensor_tensor_reduce(out=logit[0:r, c % 2, k0:k1], in0=src, in1=bias_of(j, r, k0, k1),
                                                        scale=1.0, scalar=3e38, op0=ALU.add, op1=ALU.min,
                                                        accum_out=shift[0:r, c % 2, j:j + 1])
                    last.then_inc(sem["shifted"], 1)

                def attention(first, n_heads, per_tile, bias):
                    def normed(c):
                        dve.wait_ge(sem["exped"], c + 1)
                        step(dve.reciprocal(denom[:, c % 2, :], denom[:, c % 2, :]))
                        for j, (r, k0, k1) in enumerate(SPANS):
                            last = dve.tensor_scalar(logit[0:r, c % 2, k0:k1], logit[0:r, c % 2, k0:k1],
                                                     denom[0:r, c % 2, j:j + 1], None, ALU.mult)
                        last.then_inc(sem["normed"], 1)

                    shifted(first, bias(0))
                    shifted(first + 1, bias(1))
                    normed(first)
                    for h in range(n_heads):
                        c = first + h
                        if h + 1 < n_heads:
                            normed(c + 1)
                        if first == 8 and h % 4 == 2:
                            gate_of(2, h // 4, gates)
                        if h + 2 < n_heads:
                            shifted(c + 2, bias(h + 2))
                        if h % per_tile == 0 and h >= per_tile:
                            attn_rest(first, h // per_tile - 1)
                    attn_rest(first, n_heads // per_tile - 1)

                def attn_rest(first, tile):
                    dve.wait_ge(sem["attn_hi"], TILE0[first] + tile + 1)
                    dve.tensor_tensor(br_lo[:, tile, :], bank[6 + tile % 2][:, 0:TOK], f32(br_hi[:, tile, :]),
                                      ALU.subtract).then_inc(sem["attn_lo"], 1)

                attention(0, 8, 1, lambda h: lambda j, r, k0, k1: dsa_mask[0:r, k0:k1])
                for c in range(4):
                    merge_chunk(1, c)
                dve.wait_ge(sem["attended"], 8)
                dve.wait_ge(sem["k_stored"], 64)
                dve.wait_ge(sem["v_stored"], 32)
                for c in range(4):
                    evacuate(START["kc"] + c, copies(k_c, 2 * c, 1.0))
                for c in range(4):
                    evacuate(START["vc"] + c, values(v_c, 256 * c))
                for c in range(4):
                    evacuate(START["qc"] + c, copies(q_c, 2 * c, -0.125))

                def band(h):
                    at = (128, 0, 0)
                    dve.wait_ge(sem[f"bias_loaded{h % 2}"], 16 * (h // 2 + 1))
                    step(dve.memset(band_bias[0:64, h % 2, 192:256], BIG))
                    return lambda j, r, k0, k1: band_bias[0:r, h % 2, at[j]:at[j] + k1 - k0]

                attention(8, 16, 2, band)
                for c in range(5):
                    if c < 4:
                        merge_chunk(2, c)
                    if c >= 1:
                        for k in (2 * c - 2, 2 * c - 1):
                            dve.wait_ge(sem["u_hi_ready"], U["merged"] + k + 1)
                            dve.scalar_tensor_tensor(out=u_lo[:, k, :], in0=y[:, k, :], scalar=0.5,
                                                     in1=f32(u_hi[:, k, :]), op0=ALU.mult, op1=ALU.subtract)\
                                .then_inc(sem["u_lo_ready"], 1)
                for c in range(4):
                    n = START["out"] + c
                    dve.wait_ge(sem["chunk_done"], n + 1)
                    for half in range(2):
                        last = dve.tensor_copy(y[:, 2 * c + half, :], bank[2 * pair_of(n) + half][:, 0:TOK])
                        last.then_inc(sem["y_ready"], 1)
                    dve.wait_ge(sem["y_ready"], YR["mix_post"] + 2 * c + 2)
                    give_back(n)
                    if c >= 1:
                        sum_square("mix_post", 2 * c - 2)
                        sum_square("mix_post", 2 * c - 1)
                sum_square("mix_post", 6)
                sum_square("mix_post", 7)
                add_normed("mix_post", 3, "ffn1", 4)
                ffn(1)
                rms_row_of("ple_pre")
                for c in range(4):
                    n = START["plegate"] + c
                    dve.wait_ge(sem["chunk_done"], n + 1)
                    for half in range(2):
                        dve.tensor_tensor(th[:, half, :], bank[2 * pair_of(n) + half][:, 0:TOK], rms_row[:],
                                          ALU.mult).then_inc(sem["gate_scaled"], 1)
                    dve.wait_ge(sem["gate_scaled"], 2 * FT + 2 * c + 2)
                    give_back(n)
                    for half in range(2):
                        k, g = 2 * c + half, 24 + 2 * c + half
                        dve.wait_ge(sem["gate_tanh"], g + 1)
                        step(dve.scalar_tensor_tensor(out=y[:, k, :], in0=th[:, g % 2, :], scalar=1.0,
                                                      in1=embedded[:, k, :], op0=ALU.add, op1=ALU.mult))
                        dve.sem_inc(sem["merged"], 1)
                        dve.sem_inc(sem["y_ready"], 1)
                    if c >= 1:
                        sum_square("ple_post", 2 * c - 2)
                        sum_square("ple_post", 2 * c - 1)
                sum_square("ple_post", 6)
                sum_square("ple_post", 7)
                add_normed("ple_post", 7)

        SIZE = {"up": SLOT, "down": HALF_FT * P, "in": SLOT, "misc": SLOT, "gate": SLOT, "branch": SLOT, "out": SLOT,
                "ple": 512, "plegate": SLOT}
        XR = {"ffn0": 0, "mix": 0, "ffn1": 8, "ple": 16}
        YR = {"ffn0_post": 0, "mix_post": 8, "ffn1_post": 16, "ple_post": 24}
        EVAC_ORDER = [n for name, cnt in (
            ("misc", 1), ("xbc", 8), ("z", 4), ("gate0", 2), ("qi", 1), ("kb", 1), ("qb", 4),
            ("gate0b", 2), ("vb", 1), ("gate1", 4), ("kc", 4), ("vc", 4), ("qc", 4),
            ("gate2", 4)) for n in range(START[name], START[name] + cnt)]
        EVAC_ORDER += [START["ple"] + c for c in range(4)]
        EVAC_OF = {n: i for i, n in enumerate(EVAC_ORDER)}
        EVAC = {name: EVAC_OF[START[name]] for name in START if START[name] in EVAC_OF}
        CB_BANK = (5, 6, 7, 2)
        H_BANK = (7, 5, 7, 6)
        POOL_TILES = 5

        def rms_columns(groups):
            return rs[:, 3, 0:3] if groups == 1 else rs[:, 4, 0:12]

        SPANS = ((128, 0, 128), (128, 128, 384), (64, 384, 576))
        TILE0 = {0: 0, 8: 8}

        with nc.Fori(0, DEPTH) as layer:
            with nc.Block() as block:
                layer_body(layer, block)
            nc.all_engine_barrier(sems_to_clear=every)

        with nc.Block() as block:
            @block.tensor
            def _(pe):
                for t, (t0, t1, n) in enumerate(TILES):
                    for b in range(2):
                        for i in range(4):
                            last = pe.transpose(bank[2 * t + b][0:n, P * i:P * (i + 1)], x[:, 4 * b + i, t0:t1],
                                                ident[:])
                        last.then_inc(sem["y_turned"], 1)

            @block.vector
            def _(dve):
                for t, (_, _, n) in enumerate(TILES):
                    for b in range(2):
                        dve.wait_ge(sem["y_turned"], 2 * t + b + 1)
                        dve.tensor_copy(io_rows[0:n, t, 512 * b:512 * (b + 1)], bank[2 * t + b][0:n, :])\
                            .then_inc(sem["y_rows_ready"], 1)

            @block.sync
            def _(sp):
                for t, (_, _, n) in enumerate(TILES):
                    sp.wait_ge(sem["y_rows_ready"], 2 * t + 2)
                    dst = y_p[0, P * t:P * (t + 1)] if t < 2 else y_s[0]
                    sp.dma_start(dst, io_rows[0:n, t, :]).then_inc(sem["y_stored"], 16)
                sp.wait_ge(sem["y_stored"], 48)


INPUTS = ["x_prompt", "x_sample", "p_prompt", "p_sample", "cache_dsa_k", "cache_dsa_v", "cache_idx_k",
          "cache_band_k", "cache_band_v", "state_ssm", "state_conv", "norm_g", "ffn_w13", "ffn_w2", "w_in", "conv_w",
          "conv_b", "dt_bias", "a_log", "d_skip", "ssm_norm_g", "rel_bias", "w_gate", "b_gate", "w_branch", "w_out",
          "w_ple", "w_ple_gate"]
OUTPUTS = [
    ("y_prompt", (1, SEQ, D), (1, SEQ, D)), ("y_sample", (1, DEC, D), (1, DEC, D)),
    ("dsa_k_p", (DEPTH, 1, SEQ, 256), (DEPTH, 1, SEQ, 2, 128)), ("dsa_v_p", (DEPTH, 1, SEQ, 256), (DEPTH, 1, SEQ, 2, 128)),
    ("idx_k_p", (DEPTH, 1, SEQ, 64), (DEPTH, 1, SEQ, 64)),
    ("band_k_p", (DEPTH, 1, SEQ, D), (DEPTH, 1, SEQ, 16, 64)), ("band_v_p", (DEPTH, 1, SEQ, D), (DEPTH, 1, SEQ, 16, 64)),
    ("ssm_p", (DEPTH, 1, 16, 64, 128), (DEPTH, 1, 16, 64, 128)), ("conv_p", (DEPTH, 1, 3, CONV_CH), (DEPTH, 1, 3, CONV_CH)),
    ("dsa_k_s", (DEPTH, 1, DEC, 256), (DEPTH, 1, DEC, 2, 128)), ("dsa_v_s", (DEPTH, 1, DEC, 256), (DEPTH, 1, DEC, 2, 128)),
    ("idx_k_s", (DEPTH, 1, DEC, 64), (DEPTH, 1, DEC, 64)),
    ("band_k_s", (DEPTH, 1, DEC, D), (DEPTH, 1, DEC, 16, 64)), ("band_v_s", (DEPTH, 1, DEC, D), (DEPTH, 1, DEC, 16, 64)),
    ("ssm_s", (DEPTH, 1, 16, 64, 128), (DEPTH, 1, 16, 64, 128)), ("conv_s", (DEPTH, 1, 3, CONV_CH), (DEPTH, 1, 3, CONV_CH)),
]


def kernel(**inputs):
    import concourse.bacc as bacc
    from concourse.bass_utils import run_bass_kernel_spmd

    nc = bacc.Bacc("TRN2", target_bir_lowering=False, num_devices=1)
    arrays, aps = {}, {}
    for name in INPUTS:
        array = np.ascontiguousarray(inputs[name])
        arrays[f"in_{name}"] = array
        aps[name] = nc.dram_tensor(f"in_{name}", array.shape, mybir.dt.from_np(array.dtype), kind="ExternalInput").ap()
    outs = [nc.dram_tensor(f"out_{name}", shape, F32, kind="ExternalOutput").ap() for name, shape, _ in OUTPUTS]
    bias_line = nc.dram_tensor("bias_line", (HEADS, 512), F32).ap()
    bias_square = nc.dram_tensor("bias_square", (HEADS, P, 256), F32).ap()
    build(nc, aps, outs, bias_line, bias_square)
    r = run_bass_kernel_spmd(nc, [arrays], core_ids=[0])
    return tuple(r.results[0][f"out_{name}"].reshape(final) for name, _, final in OUTPUTS)
```
